# Optimizing a Trainium2 kernel written in Bass

```python
import math
import jax
import jax.numpy as jnp
from jax import lax
import numpy as np

D_MODEL = 1024
BATCH = 1
SEQ = 512
DEPTH = 1

ATT_HEADS = 8
ATT_HEAD_DIM = 64
ATT_QK_WIDTH = ATT_HEADS * 2 * ATT_HEAD_DIM
ATT_V_WIDTH = ATT_HEADS * 2 * ATT_HEAD_DIM
ROPE_THETA = 10000.0
Q_BLOCK = 128
SSD_EXPAND = 2
SSD_INNER = SSD_EXPAND * D_MODEL
SSD_HEAD_DIM = 64
SSD_HEADS = SSD_INNER // SSD_HEAD_DIM
SSD_GROUPS = 8
SSD_HEADS_PER_GROUP = SSD_HEADS // SSD_GROUPS
SSD_STATE = 128
SSD_CONV = 4
SSD_CONV_CH = SSD_INNER + 2 * SSD_GROUPS * SSD_STATE
SSD_CHUNK = 128
IN_SPLITS = (ATT_QK_WIDTH, ATT_QK_WIDTH, ATT_V_WIDTH, SSD_INNER, SSD_CONV_CH, SSD_HEADS, D_MODEL, D_MODEL)
IN_COLS = sum(IN_SPLITS)
MOE_GROUPS = 8
MOE_EXPERTS_PER_GROUP = 8
MOE_EXPERTS = MOE_GROUPS * MOE_EXPERTS_PER_GROUP
MOE_TOP_K = 2
MOE_HIDDEN = 512
MOE_BLOCK = 128
NORM_EPS = 1e-6
SUBLN_EPS = 1e-5
SSD_NORM_EPS = 1e-5


def rms_norm(x, w, eps):
    xf = x.astype(jnp.float32)
    y = xf * lax.rsqrt(jnp.mean(xf * xf, axis=-1, keepdims=True) + eps)
    return (y * w.astype(jnp.float32)).astype(x.dtype)

def rotary_tables(positions):
    inv_freq = 1.0 / (ROPE_THETA ** (jnp.arange(0, ATT_HEAD_DIM, 2, dtype=jnp.float32) / ATT_HEAD_DIM))
    ang = positions.astype(jnp.float32)[..., None] * inv_freq
    return jnp.cos(ang), jnp.sin(ang)

def apply_rotary(t, cos, sin):
    c = cos[:, :, None, None, :]
    sn = sin[:, :, None, None, :]
    tf = t.astype(jnp.float32)
    t1, t2 = jnp.split(tf, 2, axis=-1)
    return jnp.concatenate([t1 * c - t2 * sn, t2 * c + t1 * sn], axis=-1).astype(t.dtype)

def diff_attention(q, k, v, lam):
    s = q.shape[1]
    scale = ATT_HEAD_DIM ** -0.5
    outs = []
    for blk in range(s // Q_BLOCK):
        q_lo = blk * Q_BLOCK
        q_hi = q_lo + Q_BLOCK
        scores = jnp.einsum('bqhcd,bkhcd->bhcqk', q[:, q_lo:q_hi], k[:, :q_hi],
                            preferred_element_type=jnp.float32) * scale
        causal = (q_lo + jnp.arange(Q_BLOCK))[:, None] >= jnp.arange(q_hi)[None, :]
        probs = jax.nn.softmax(jnp.where(causal, scores, -jnp.inf), axis=-1)
        weights = probs[:, :, 0] - lam * probs[:, :, 1]
        outs.append(jnp.einsum('bhqk,bkhe->bqhe', weights.astype(v.dtype), v[:, :q_hi]))
    return jnp.concatenate(outs, axis=1)

def causal_depthwise_conv(u, w, bias):
    out = lax.conv_general_dilated(u, w[:, None, :], window_strides=(1,), padding=[(SSD_CONV - 1, 0)],
                                   dimension_numbers=('NWC', 'WIO', 'NWC'),
                                   feature_group_count=u.shape[-1])
    return out + bias

def ssd_chunked_scan(xdt, a, bm, cm):
    b, s, g, r, p = xdt.shape
    n = bm.shape[-1]
    nc = s // SSD_CHUNK

    def to_chunks(t):
        return jnp.moveaxis(t.reshape(b, nc, SSD_CHUNK, *t.shape[2:]), 1, 0)

    causal = jnp.tril(jnp.ones((SSD_CHUNK, SSD_CHUNK), dtype=bool))

    def step(state, inp):
        xc, ac, bc, cc = inp
        cum = jnp.cumsum(ac, axis=1)
        cum_t = jnp.moveaxis(cum, 1, -1)
        seg = cum_t[..., :, None] - cum_t[..., None, :]
        decay = jnp.exp(jnp.where(causal, seg, -jnp.inf))
        cb = jnp.einsum('bign,bjgn->bgij', cc, bc)
        y_diag = jnp.einsum('bgij,bgrij,bjgrp->bigrp', cb, decay, xc)
        y_off = jnp.einsum('bign,bgrpn->bigrp', cc, state) * jnp.exp(cum)[..., None]
        total = cum[:, -1]
        w_tail = jnp.exp(total[:, None] - cum)
        new_state = state * jnp.exp(total)[..., None, None] + jnp.einsum('bjgn,bjgr,bjgrp->bgrpn', bc, w_tail, xc)
        return new_state, y_diag + y_off

    init = jnp.zeros((b, g, r, p, n), jnp.float32)
    _, ys = lax.scan(step, init, (to_chunks(xdt), to_chunks(a), to_chunks(bm), to_chunks(cm)))
    return jnp.moveaxis(ys, 0, 1).reshape(b, s, g, r, p)

def ssd_branch(z, xbc, dt_raw, conv_w, conv_b, dt_bias, a_log, d_skip, norm_w):
    b, s, _ = z.shape
    xbc = jax.nn.silu(causal_depthwise_conv(xbc, conv_w, conv_b))
    xs, bm, cm = jnp.split(xbc, [SSD_INNER, SSD_INNER + SSD_GROUPS * SSD_STATE], axis=-1)
    xs = xs.reshape(b, s, SSD_GROUPS, SSD_HEADS_PER_GROUP, SSD_HEAD_DIM).astype(jnp.float32)
    bm = bm.reshape(b, s, SSD_GROUPS, SSD_STATE).astype(jnp.float32)
    cm = cm.reshape(b, s, SSD_GROUPS, SSD_STATE).astype(jnp.float32)
    dt = jax.nn.softplus(dt_raw.astype(jnp.float32) + dt_bias.astype(jnp.float32))
    dt = dt.reshape(b, s, SSD_GROUPS, SSD_HEADS_PER_GROUP)
    a = -jnp.exp(a_log.astype(jnp.float32)).reshape(SSD_GROUPS, SSD_HEADS_PER_GROUP)
    dsk = d_skip.astype(jnp.float32).reshape(SSD_GROUPS, SSD_HEADS_PER_GROUP)
    y = ssd_chunked_scan(xs * dt[..., None], dt * a, bm, cm) + dsk[..., None] * xs
    y = y.reshape(b, s, SSD_INNER) * jax.nn.silu(z.astype(jnp.float32))
    yg = y.reshape(b, s, SSD_GROUPS, SSD_INNER // SSD_GROUPS)
    yg = yg * lax.rsqrt(jnp.mean(yg * yg, axis=-1, keepdims=True) + SSD_NORM_EPS)
    return (yg.reshape(b, s, SSD_INNER) * norm_w.astype(jnp.float32)).astype(z.dtype)

def hierarchical_moe(h, w_gr, b_gr, w_er, b_er, w_gate, w_up, w_down):
    b, s, d = h.shape
    t = h.reshape(-1, d)
    n_tok = t.shape[0]
    g_logits = jnp.matmul(t, w_gr).astype(jnp.float32) + b_gr.astype(jnp.float32)
    g_prob = jax.nn.softmax(g_logits, axis=-1)
    g_sel = jnp.argmax(g_logits, axis=-1)
    g_gate = jnp.take_along_axis(g_prob, g_sel[:, None], axis=-1)[:, 0]
    e_logits = (jnp.matmul(t, w_er).astype(jnp.float32) + b_er.astype(jnp.float32))
    e_logits = e_logits.reshape(n_tok, MOE_GROUPS, MOE_EXPERTS_PER_GROUP)
    e_sel_logits = jnp.take_along_axis(e_logits, g_sel[:, None, None], axis=1)[:, 0]
    top_v, top_i = lax.top_k(e_sel_logits, MOE_TOP_K)
    weights = g_gate[:, None] * jax.nn.softmax(top_v, axis=-1)
    eid = g_sel[:, None].astype(jnp.int32) * MOE_EXPERTS_PER_GROUP + top_i.astype(jnp.int32)
    n_assign = n_tok * MOE_TOP_K
    flat_e = eid.reshape(-1)
    flat_tok = jnp.repeat(jnp.arange(n_tok, dtype=jnp.int32), MOE_TOP_K)
    flat_w = weights.reshape(-1)
    order = jnp.argsort(flat_e)
    se, st, sw = flat_e[order], flat_tok[order], flat_w[order]
    counts = jnp.bincount(flat_e, length=MOE_EXPERTS)
    starts = jnp.cumsum(counts) - counts
    padded = ((counts + MOE_BLOCK - 1) // MOE_BLOCK) * MOE_BLOCK
    pad_end = jnp.cumsum(padded)
    pad_start = pad_end - padded
    dest = pad_start[se] + (jnp.arange(n_assign, dtype=jnp.int32) - starts[se])
    n_buf = n_assign + MOE_EXPERTS * MOE_BLOCK
    n_blocks = n_buf // MOE_BLOCK
    buf_tok = jnp.zeros((n_buf,), jnp.int32).at[dest].set(st)
    buf_w = jnp.zeros((n_buf,), jnp.float32).at[dest].set(sw)
    blk_expert = jnp.minimum(jnp.searchsorted(pad_end, jnp.arange(n_blocks) * MOE_BLOCK, side='right'),
                             MOE_EXPERTS - 1)
    xb = t[buf_tok].reshape(n_blocks, MOE_BLOCK, d)

    def expert_block(args):
        xblk, e = args
        hid = jax.nn.silu(xblk @ w_gate[e]) * (xblk @ w_up[e])
        return hid @ w_down[e]

    yb = lax.map(expert_block, (xb, blk_expert)).reshape(n_buf, d)
    out = jnp.zeros((n_tok, d), jnp.float32).at[buf_tok].add(yb.astype(jnp.float32) * buf_w[:, None])
    return out.astype(h.dtype).reshape(b, s, d)

def first_inputs(seed: int = 0) -> dict:
    key = jax.random.key(seed)
    ks = jax.random.split(key, 28)
    f32 = jnp.float32

    def normal(k, shape, scale):
        return jax.random.normal(k, shape, f32) * scale

    x = normal(ks[0], (BATCH, SEQ, D_MODEL), 1.0)
    positions = (jnp.arange(SEQ, dtype=jnp.int32)[None, :]
                 + jax.random.randint(ks[1], (BATCH, 1), 0, SEQ, dtype=jnp.int32))
    norm_mix_w = 1.0 + normal(ks[2], (DEPTH, D_MODEL), 0.02)
    w_in = normal(ks[3], (DEPTH, D_MODEL, IN_COLS), D_MODEL ** -0.5)
    conv_w = normal(ks[4], (DEPTH, SSD_CONV, SSD_CONV_CH), SSD_CONV ** -0.5)
    conv_b = normal(ks[5], (DEPTH, SSD_CONV_CH), 0.02)
    dt0 = jnp.exp(jax.random.uniform(ks[6], (DEPTH, SSD_HEADS), f32, math.log(1e-3), math.log(1e-1)))
    dt_bias = dt0 + jnp.log(-jnp.expm1(-dt0))
    a_log = jnp.log(jax.random.uniform(ks[7], (DEPTH, SSD_HEADS), f32, 1.0, 16.0))
    d_skip = 1.0 + normal(ks[8], (DEPTH, SSD_HEADS), 0.1)
    ssd_norm_w = 1.0 + normal(ks[9], (DEPTH, SSD_INNER), 0.02)
    lambda_q1 = normal(ks[10], (DEPTH, ATT_HEAD_DIM), 0.1)
    lambda_k1 = normal(ks[11], (DEPTH, ATT_HEAD_DIM), 0.1)
    lambda_q2 = normal(ks[12], (DEPTH, ATT_HEAD_DIM), 0.1)
    lambda_k2 = normal(ks[13], (DEPTH, ATT_HEAD_DIM), 0.1)
    subln_w = 1.0 + normal(ks[14], (DEPTH, 2 * ATT_HEAD_DIM), 0.02)
    w_branch_attn = normal(ks[15], (DEPTH, ATT_V_WIDTH, D_MODEL), ATT_V_WIDTH ** -0.5)
    w_branch_ssd = normal(ks[16], (DEPTH, SSD_INNER, D_MODEL), SSD_INNER ** -0.5)
    w_out = normal(ks[17], (DEPTH, D_MODEL, D_MODEL), D_MODEL ** -0.5)
    norm_ffn_w = 1.0 + normal(ks[18], (DEPTH, D_MODEL), 0.02)
    w_group_router = normal(ks[19], (DEPTH, D_MODEL, MOE_GROUPS), D_MODEL ** -0.5)
    b_group_router = normal(ks[20], (DEPTH, MOE_GROUPS), 0.01)
    w_expert_router = normal(ks[21], (DEPTH, D_MODEL, MOE_EXPERTS), D_MODEL ** -0.5)
    b_expert_router = normal(ks[22], (DEPTH, MOE_EXPERTS), 0.01)
    w_expert_gate = normal(ks[23], (DEPTH, MOE_EXPERTS, D_MODEL, MOE_HIDDEN), D_MODEL ** -0.5)
    w_expert_up = normal(ks[24], (DEPTH, MOE_EXPERTS, D_MODEL, MOE_HIDDEN), D_MODEL ** -0.5)
    w_expert_down = normal(ks[25], (DEPTH, MOE_EXPERTS, MOE_HIDDEN, D_MODEL), MOE_HIDDEN ** -0.5)
    final_norm_w = 1.0 + normal(ks[26], (D_MODEL,), 0.02)
    return {'x': x, 'positions': positions, 'norm_mix_w': norm_mix_w, 'w_in': w_in,
            'conv_w': conv_w, 'conv_b': conv_b, 'dt_bias': dt_bias, 'a_log': a_log, 'd_skip': d_skip,
            'ssd_norm_w': ssd_norm_w, 'lambda_q1': lambda_q1, 'lambda_k1': lambda_k1,
            'lambda_q2': lambda_q2, 'lambda_k2': lambda_k2, 'subln_w': subln_w,
            'w_branch_attn': w_branch_attn, 'w_branch_ssd': w_branch_ssd, 'w_out': w_out,
            'norm_ffn_w': norm_ffn_w, 'w_group_router': w_group_router, 'b_group_router': b_group_router,
            'w_expert_router': w_expert_router, 'b_expert_router': b_expert_router,
            'w_expert_gate': w_expert_gate, 'w_expert_up': w_expert_up, 'w_expert_down': w_expert_down,
            'final_norm_w': final_norm_w}

def first_block(x, positions, norm_mix_w, w_in, conv_w, conv_b, dt_bias, a_log, d_skip, ssd_norm_w,
              lambda_q1, lambda_k1, lambda_q2, lambda_k2, subln_w, w_branch_attn, w_branch_ssd, w_out,
              norm_ffn_w, w_group_router, b_group_router, w_expert_router, b_expert_router,
              w_expert_gate, w_expert_up, w_expert_down, final_norm_w):
    b, s, _ = x.shape
    cos, sin = rotary_tables(positions)
    split_at = [int(o) for o in np.cumsum(IN_SPLITS)[:-1]]
    for l in range(DEPTH):
        lam_init = 0.8 - 0.6 * math.exp(-0.3 * l)
        h = rms_norm(x, norm_mix_w[l], NORM_EPS)
        proj = h @ w_in[l]
        q, k, v, z, xbc, dt_raw, gate_a, gate_s = jnp.split(proj, split_at, axis=-1)
        q = apply_rotary(q.reshape(b, s, ATT_HEADS, 2, ATT_HEAD_DIM), cos, sin)
        k = apply_rotary(k.reshape(b, s, ATT_HEADS, 2, ATT_HEAD_DIM), cos, sin)
        v = v.reshape(b, s, ATT_HEADS, 2 * ATT_HEAD_DIM)
        lam = (jnp.exp(jnp.sum(lambda_q1[l].astype(jnp.float32) * lambda_k1[l].astype(jnp.float32)))
               - jnp.exp(jnp.sum(lambda_q2[l].astype(jnp.float32) * lambda_k2[l].astype(jnp.float32)))
               + lam_init)
        att = diff_attention(q, k, v, lam)
        att = (rms_norm(att, subln_w[l], SUBLN_EPS) * (1.0 - lam_init)).reshape(b, s, ATT_V_WIDTH)
        ssd = ssd_branch(z, xbc, dt_raw, conv_w[l], conv_b[l], dt_bias[l], a_log[l], d_skip[l], ssd_norm_w[l])
        merged = (jax.nn.sigmoid(gate_a) * (att @ w_branch_attn[l])
                  + jax.nn.sigmoid(gate_s) * (ssd @ w_branch_ssd[l]))
        x = x + merged @ w_out[l]
        h2 = rms_norm(x, norm_ffn_w[l], NORM_EPS)
        x = x + hierarchical_moe(h2, w_group_router[l], b_group_router[l], w_expert_router[l],
                                 b_expert_router[l], w_expert_gate[l], w_expert_up[l], w_expert_down[l])
    return rms_norm(x, final_norm_w, NORM_EPS)


DEPTH_2 = 2

ROPE_BASE = 10000.0

RW_HEADS = 4
RW_HEAD_DIM = 64
RW_DIM = RW_HEADS * RW_HEAD_DIM
RW_DECAY_RANK = 32
RW_A_RANK = 32
RW_V_RANK = 32
RW_GATE_RANK = 64
RW_GN_EPS = 64e-5
RW_IN = 3 * RW_DIM + RW_DECAY_RANK + RW_A_RANK + RW_GATE_RANK

RET_HEADS = 4
RET_HEAD_DIM = 64
RET_DIM = RET_HEADS * RET_HEAD_DIM
RET_CHUNK = 128
RET_IN = 4 * RET_DIM

MLA_HEADS = 8
MLA_NOPE = 64
MLA_ROPE = 32
MLA_V = 64
MLA_Q_RANK = 384
MLA_KV_RANK = 256
MLA_DIM = MLA_HEADS * MLA_V
MLA_IN = MLA_Q_RANK + MLA_KV_RANK + MLA_ROPE
ATTN_BLOCK = 128

IN_DIM = RW_IN + RET_IN + MLA_IN
MIX_DIM = RW_DIM + RET_DIM + MLA_DIM
D_FF = -(-(8 * D_MODEL) // (3 * 256)) * 256


def rms_norm_2(x, g):
    xf = x.astype(jnp.float32)
    y = xf * lax.rsqrt(jnp.mean(xf * xf, axis=-1, keepdims=True) + NORM_EPS)
    return (y * g.astype(jnp.float32)).astype(x.dtype)

def rope(x, positions):
    d = x.shape[-1]
    inv = ROPE_BASE ** (-jnp.arange(0, d, 2, dtype=jnp.float32) / d)
    ang = positions.astype(jnp.float32)[..., None] * inv
    ang = ang.reshape(ang.shape[:2] + (1,) * (x.ndim - 3) + ang.shape[-1:])
    cos, sin = jnp.cos(ang), jnp.sin(ang)
    xf = x.astype(jnp.float32)
    x1, x2 = xf[..., : d // 2], xf[..., d // 2:]
    return jnp.concatenate([x1 * cos - x2 * sin, x2 * cos + x1 * sin], axis=-1).astype(x.dtype)

def token_shift(p):
    return jnp.pad(p, ((0, 0), (1, 0), (0, 0)))[:, :-1]

def rwkv7_mixer(p, mu, w0, w2, a0, a2, g2, k_k, k_a, r_k, gn_w, gn_b, v_first, v_res):
    B, S, _ = p.shape
    p = p.astype(jnp.float32)
    ps = p + (token_shift(p) - p) * mu
    o1, o2, o3 = RW_DIM, 2 * RW_DIM, 3 * RW_DIM
    o4, o5 = o3 + RW_DECAY_RANK, o3 + RW_DECAY_RANK + RW_A_RANK
    r, k, v = ps[..., :o1], ps[..., o1:o2], ps[..., o2:o3]
    wd, ad, gd = ps[..., o3:o4], ps[..., o4:o5], ps[..., o5:]
    w = -jax.nn.softplus(-(w0 + jnp.tanh(wd) @ w2)) - 0.5
    decay = jnp.exp(-jnp.exp(w))
    a = jax.nn.sigmoid(a0 + ad @ a2)
    g = jax.nn.sigmoid(gd) @ g2
    if v_res is None:
        v_first = v
    else:
        v0, v1, v2 = v_res
        v = v + (v_first - v) * jax.nn.sigmoid(v0 + (v @ v1) @ v2)
    heads = lambda t: t.reshape(B, S, RW_HEADS, RW_HEAD_DIM)
    kk = heads(k * k_k)
    kk = kk * lax.rsqrt(jnp.maximum(jnp.sum(kk * kk, axis=-1, keepdims=True), 1e-24))
    k = k * (1.0 + (a - 1.0) * k_a)
    r_h, k_h, v_h, w_h, a_h = heads(r), heads(k), heads(v), heads(decay), heads(a)

    def step(state, inp):
        rt, kt, vt, wt, kkt, at = inp
        sa = jnp.einsum('bhvk,bhk->bhv', state, -kkt)
        state = (state * wt[:, :, None, :] + sa[..., None] * (kkt * at)[:, :, None, :]
                 + vt[..., None] * kt[:, :, None, :])
        return state, jnp.einsum('bhvk,bhk->bhv', state, rt)

    xs = tuple(jnp.moveaxis(t, 1, 0) for t in (r_h, k_h, v_h, w_h, kk, a_h))
    s0 = jnp.zeros((B, RW_HEADS, RW_HEAD_DIM, RW_HEAD_DIM), jnp.float32)
    _, y = lax.scan(step, s0, xs)
    y = jnp.moveaxis(y, 0, 1)
    mean = jnp.mean(y, axis=-1, keepdims=True)
    var = jnp.mean(jnp.square(y - mean), axis=-1, keepdims=True)
    y = ((y - mean) * lax.rsqrt(var + RW_GN_EPS)).reshape(B, S, RW_DIM) * gn_w + gn_b
    bonus = jnp.sum(r_h * k_h * r_k, axis=-1, keepdims=True) * v_h
    y = (y + bonus.reshape(B, S, RW_DIM)) * g
    return y, v_first

def retention_mixer(p, positions):
    B, S, _ = p.shape
    p = p.astype(jnp.float32)
    q, k, v, g = jnp.split(p, 4, axis=-1)
    heads = lambda t: t.reshape(B, S, RET_HEADS, RET_HEAD_DIM)
    q = rope(heads(q), positions)
    k = rope(heads(k), positions) * (RET_HEAD_DIM ** -0.5)
    v = heads(v)
    log_gamma = jnp.log(1.0 - 2.0 ** (-5.0 - jnp.arange(RET_HEADS, dtype=jnp.float32)))
    n_chunks = S // RET_CHUNK
    chunk = lambda t: t.reshape(B, n_chunks, RET_CHUNK, RET_HEADS, RET_HEAD_DIM).transpose(0, 3, 1, 2, 4)
    qc, kc, vc = chunk(q), chunk(k), chunk(v)
    idx = jnp.arange(RET_CHUNK, dtype=jnp.float32)
    diff = idx[:, None] - idx[None, :]
    dmask = jnp.where(diff >= 0, jnp.exp(log_gamma[:, None, None] * jnp.maximum(diff, 0.0)), 0.0)
    inner = jnp.einsum('bhnqd,bhnkd->bhnqk', qc, kc) * dmask[:, None]
    inner = jnp.einsum('bhnqk,bhnkd->bhnqd', inner, vc)
    q_dec = jnp.exp(log_gamma[:, None] * (idx + 1.0))
    k_dec = jnp.exp(log_gamma[:, None] * (RET_CHUNK - 1.0 - idx))
    chunk_dec = jnp.exp(log_gamma * RET_CHUNK)
    kv_chunk = jnp.einsum('bhnkd,bhnke->nbhde', kc * k_dec[:, None, :, None], vc)

    def step(R, kv_i):
        return R * chunk_dec[None, :, None, None] + kv_i, R

    R0 = jnp.zeros((B, RET_HEADS, RET_HEAD_DIM, RET_HEAD_DIM), jnp.float32)
    _, R_prev = lax.scan(step, R0, kv_chunk)
    cross = jnp.einsum('bhnqd,nbhde->bhnqe', qc * q_dec[:, None, :, None], R_prev)
    y = (inner + cross).transpose(0, 2, 3, 1, 4).reshape(B, S, RET_HEADS, RET_HEAD_DIM)
    y = y * lax.rsqrt(jnp.mean(y * y, axis=-1, keepdims=True) + NORM_EPS)
    return jax.nn.silu(g) * y.reshape(B, S, RET_DIM)

def mla_mixer(p, positions, q_norm, kv_norm, w_q_up, w_kv_up):
    B, S, _ = p.shape
    q_lat = p[..., :MLA_Q_RANK]
    kv_lat = p[..., MLA_Q_RANK:MLA_Q_RANK + MLA_KV_RANK]
    k_rope = rope(p[..., MLA_Q_RANK + MLA_KV_RANK:], positions)
    q = (rms_norm_2(q_lat, q_norm) @ w_q_up).reshape(B, S, MLA_HEADS, MLA_NOPE + MLA_ROPE)
    q_nope, q_rope = q[..., :MLA_NOPE], rope(q[..., MLA_NOPE:], positions)
    kv = (rms_norm_2(kv_lat, kv_norm) @ w_kv_up).reshape(B, S, MLA_HEADS, MLA_NOPE + MLA_V)
    k_nope, v = kv[..., :MLA_NOPE], kv[..., MLA_NOPE:]
    scale = (MLA_NOPE + MLA_ROPE) ** -0.5
    n_blocks = S // ATTN_BLOCK
    blk = lambda t: t.reshape(B, n_blocks, ATTN_BLOCK, MLA_HEADS, t.shape[-1]).transpose(1, 0, 3, 2, 4)
    qn_b, qr_b = blk(q_nope), blk(q_rope)
    key_idx = jnp.arange(S)

    def attend(args):
        qn, qr, i = args
        s = (jnp.einsum('bhqd,bkhd->bhqk', qn, k_nope)
             + jnp.einsum('bhqr,bkr->bhqk', qr, k_rope)).astype(jnp.float32) * scale
        q_idx = i * ATTN_BLOCK + jnp.arange(ATTN_BLOCK)
        s = jnp.where(key_idx[None, :] <= q_idx[:, None], s, -jnp.inf)
        pr = jax.nn.softmax(s, axis=-1).astype(v.dtype)
        return jnp.einsum('bhqk,bkhd->bqhd', pr, v)

    o = lax.map(attend, (qn_b, qr_b, jnp.arange(n_blocks)))
    return o.transpose(1, 0, 2, 3, 4).reshape(B, S, MLA_DIM)

def second_inputs(seed: int = 0) -> dict:
    key = jax.random.key(seed)
    keys = jax.random.split(key, 32)
    nrm = lambda i, shape, scale: scale * jax.random.normal(keys[i], shape, jnp.float32)
    L = DEPTH_2
    ch = jnp.linspace(0.0, 1.0, RW_DIM, dtype=jnp.float32)
    return {
        'x': nrm(0, (BATCH, SEQ, D_MODEL), 1.0),
        'positions': jnp.broadcast_to(jnp.arange(SEQ, dtype=jnp.int32), (BATCH, SEQ)),
        'attn_norm': 1.0 + nrm(1, (L, D_MODEL), 0.05),
        'w_in': nrm(2, (L, D_MODEL, IN_DIM), D_MODEL ** -0.5),
        'w_out': nrm(3, (L, MIX_DIM, D_MODEL), MIX_DIM ** -0.5),
        'rw_mu': jax.random.uniform(keys[4], (L, RW_IN), jnp.float32),
        'rw_w0': -6.0 + 5.0 * ch ** 0.85 + nrm(5, (L, RW_DIM), 0.1),
        'rw_w2': nrm(6, (L, RW_DECAY_RANK, RW_DIM), 0.5 * RW_DECAY_RANK ** -0.5),
        'rw_a0': nrm(7, (L, RW_DIM), 0.1),
        'rw_a2': nrm(8, (L, RW_A_RANK, RW_DIM), RW_A_RANK ** -0.5),
        'rw_g2': nrm(9, (L, RW_GATE_RANK, RW_DIM), RW_GATE_RANK ** -0.5),
        'rw_k_k': 0.85 + nrm(10, (L, RW_DIM), 0.05),
        'rw_k_a': 1.0 + nrm(11, (L, RW_DIM), 0.05),
        'rw_r_k': nrm(12, (L, RW_HEADS, RW_HEAD_DIM), 0.1),
        'rw_gn_w': 1.0 + nrm(13, (L, RW_DIM), 0.05),
        'rw_gn_b': nrm(14, (L, RW_DIM), 0.01),
        'rw_v0': 1.0 + nrm(15, (L - 1, RW_DIM), 0.1),
        'rw_v1': nrm(16, (L - 1, RW_DIM, RW_V_RANK), RW_DIM ** -0.5),
        'rw_v2': nrm(17, (L - 1, RW_V_RANK, RW_DIM), 0.5 * RW_V_RANK ** -0.5),
        'mla_q_norm': 1.0 + nrm(18, (L, MLA_Q_RANK), 0.05),
        'mla_kv_norm': 1.0 + nrm(19, (L, MLA_KV_RANK), 0.05),
        'mla_w_q_up': nrm(20, (L, MLA_Q_RANK, MLA_HEADS * (MLA_NOPE + MLA_ROPE)), MLA_Q_RANK ** -0.5),
        'mla_w_kv_up': nrm(21, (L, MLA_KV_RANK, MLA_HEADS * (MLA_NOPE + MLA_V)), MLA_KV_RANK ** -0.5),
        'ffn_norm': 1.0 + nrm(22, (L, D_MODEL), 0.05),
        'w_gate_up': nrm(23, (L, D_MODEL, 2 * D_FF), D_MODEL ** -0.5),
        'w_down': nrm(24, (L, D_FF, D_MODEL), D_FF ** -0.5),
        'final_norm': 1.0 + nrm(25, (D_MODEL,), 0.05),
    }

def second_block(x, positions, attn_norm, w_in, w_out, rw_mu, rw_w0, rw_w2, rw_a0, rw_a2, rw_g2,
              rw_k_k, rw_k_a, rw_r_k, rw_gn_w, rw_gn_b, rw_v0, rw_v1, rw_v2, mla_q_norm, mla_kv_norm,
              mla_w_q_up, mla_w_kv_up, ffn_norm, w_gate_up, w_down, final_norm):
    h = x
    v_first = None
    for l in range(DEPTH_2):
        hn = rms_norm_2(h, attn_norm[l])
        proj = hn @ w_in[l]
        p_a = proj[..., :RW_IN]
        p_b = proj[..., RW_IN:RW_IN + RET_IN]
        p_c = proj[..., RW_IN + RET_IN:]
        v_res = None if l == 0 else (rw_v0[l - 1], rw_v1[l - 1], rw_v2[l - 1])
        y_a, v_first = rwkv7_mixer(p_a, rw_mu[l], rw_w0[l], rw_w2[l], rw_a0[l], rw_a2[l], rw_g2[l],
                                   rw_k_k[l], rw_k_a[l], rw_r_k[l], rw_gn_w[l], rw_gn_b[l], v_first, v_res)
        y_b = retention_mixer(p_b, positions)
        y_c = mla_mixer(p_c, positions, mla_q_norm[l], mla_kv_norm[l], mla_w_q_up[l], mla_w_kv_up[l])
        mix = jnp.concatenate([y_a.astype(h.dtype), y_b.astype(h.dtype), y_c.astype(h.dtype)], axis=-1)
        h = h + mix @ w_out[l]
        hn = rms_norm_2(h, ffn_norm[l])
        gu = hn @ w_gate_up[l]
        h = h + (jax.nn.silu(gu[..., :D_FF]) * gu[..., D_FF:]) @ w_down[l]
    return rms_norm_2(h, final_norm)


def setup_inputs(seed=0):
    out = dict(first_inputs(seed))
    for name, value in second_inputs(seed + 1).items():
        if name != "x":
            out[name + "_2"] = value
    return out


def reference(
    x, positions, norm_mix_w, w_in, conv_w, conv_b, dt_bias, a_log, d_skip, ssd_norm_w,
    lambda_q1, lambda_k1, lambda_q2, lambda_k2, subln_w, w_branch_attn, w_branch_ssd, w_out,
    norm_ffn_w, w_group_router, b_group_router, w_expert_router, b_expert_router, w_expert_gate,
    w_expert_up, w_expert_down, final_norm_w, positions_2, attn_norm_2, w_in_2, w_out_2,
    rw_mu_2, rw_w0_2, rw_w2_2, rw_a0_2, rw_a2_2, rw_g2_2, rw_k_k_2, rw_k_a_2, rw_r_k_2,
    rw_gn_w_2, rw_gn_b_2, rw_v0_2, rw_v1_2, rw_v2_2, mla_q_norm_2, mla_kv_norm_2, mla_w_q_up_2,
    mla_w_kv_up_2, ffn_norm_2, w_gate_up_2, w_down_2, final_norm_2,
):
    x = first_block(
        x, positions, norm_mix_w, w_in, conv_w, conv_b, dt_bias, a_log, d_skip, ssd_norm_w,
        lambda_q1, lambda_k1, lambda_q2, lambda_k2, subln_w, w_branch_attn, w_branch_ssd, w_out,
        norm_ffn_w, w_group_router, b_group_router, w_expert_router, b_expert_router,
        w_expert_gate, w_expert_up, w_expert_down, final_norm_w,
    )
    return second_block(
        x, positions_2, attn_norm_2, w_in_2, w_out_2, rw_mu_2, rw_w0_2, rw_w2_2, rw_a0_2,
        rw_a2_2, rw_g2_2, rw_k_k_2, rw_k_a_2, rw_r_k_2, rw_gn_w_2, rw_gn_b_2, rw_v0_2, rw_v1_2,
        rw_v2_2, mla_q_norm_2, mla_kv_norm_2, mla_w_q_up_2, mla_w_kv_up_2, ffn_norm_2,
        w_gate_up_2, w_down_2, final_norm_2,
    )


_drawn_inputs = setup_inputs


def setup_inputs(seed=0):
    import zlib

    import numpy as np

    out = dict(_drawn_inputs(seed))
    spreads = {}
    factors = {'lambda_q1': 5.032,
     'subln_w': 2.81,
     'b_group_router': 3.638,
     'b_expert_router': 4.984,
     'rw_w2_2': 3.286,
     'rw_a0_2': 3.668,
     'rw_k_k_2': 3.671,
     'rw_gn_w_2': 2.892,
     'rw_gn_b_2': 8.0,
     'rw_v0_2': 200.0,
     'mla_q_norm_2': 7.529,
     'mla_kv_norm_2': 4.118,
     'rw_v1_2': 8.0,
     'rw_v2_2': 8.0}
    for name, (base, spread) in spreads.items():
        noise = np.random.default_rng([zlib.crc32(name.encode()), seed]).standard_normal(out[name].shape)
        drawn = base * np.exp(spread * noise) if base else spread * noise
        out[name] = jnp.asarray(drawn.astype(out[name].dtype))
    for name, factor in factors.items():
        out[name] = (out[name] * factor).astype(out[name].dtype)
    return out
```

```python
from contextlib import ExitStack

import numpy as np
import concourse.bass as bass
from concourse import mybir

F32 = mybir.dt.float32
I32 = mybir.dt.int32
U32 = mybir.dt.uint32
ACT = mybir.ActivationFunctionType
ALU = mybir.AluOpType
AX = mybir.AxisListType.X
ds = bass.ds

P = 128
T = 512
NT = T // P
D = 1024
KD = D // P
PI = float(np.pi)
LAM_INIT = 0.8 - 0.6


def shape_constants():
    f = np.float32
    r, c = np.arange(P)[:, None], np.arange(P)[None, :]
    parts = {}
    parts["ident"] = (r == c)
    for name, hd in (("turn64", 64), ("turn32", 32)):
        half = hd // 2
        low = (c % hd) < half
        parts[name] = np.where(low & (r == c + half), -1.0, 0.0) + np.where(~low & (r == c - half), 1.0, 0.0)
    parts["neg_wide"] = np.concatenate([np.zeros((P, 384)), np.where(c > r, -1e30, 0.0)], 1)
    parts["upto"] = (r <= c)
    parts["before"] = (r < c)
    parts["neg_after"] = np.where(r > c, -1e30, 0.0)
    parts["ones"] = np.ones((P, P))
    parts["same_head"] = (r // 64 == c // 64)
    same = r // 64 == c // 64
    parts["rw_before"] = (r < c) & same
    parts["rw_upto"] = (r <= c) & same
    for lv in range(6):
        n = 1 << lv
        parts[f"rw_level{lv}"] = (r // (2 * n) == c // (2 * n)) & ((r // n) % 2 == 0) & ((c // n) % 2 == 1)
    parts["rw_level0_t"] = parts["rw_level0"].T
    lg = np.log(1.0 - 2.0 ** (-5.0 - np.arange(4, dtype=f))).astype(f)
    parts["ret_decay"] = np.concatenate([np.where(c >= r, np.exp(lg[h] * np.maximum(c - r, 0).astype(f)) * 0.125, 0.0) for h in range(4)], 1)
    head_of = np.arange(P) // 64
    for b in range(2):
        g = lg[2 * b + head_of][:, None]
        parts[f"ret_q{b}"] = np.exp(g * (c + 1.0))
        parts[f"ret_k{b}"] = np.exp(g * (P - 1.0 - c)) * 64 ** -0.5
    parts["ret_state"] = np.stack([np.exp(lg[2 * b + head_of] * 128) for b in range(2)], 1)
    p1 = np.arange(P)
    parts["freq64"] = (1.0 / (f(10000.0) ** ((2 * (p1 % 32)).astype(f) / f(64)))).astype(f)[:, None]
    parts["freq32"] = (1.0 / (f(10000.0) ** ((2 * (p1 % 16)).astype(f) / f(32)))).astype(f)[:, None]
    parts["rank"] = p1[:, None].astype(f)
    parts["expert_slot"] = np.broadcast_to(np.arange(64)[None, :] * 128.0, (P, 64))
    parts["rw_keep"] = np.broadcast_to((np.arange(T) % 64 != 0)[None, :], (P, T))
    at, where = 0, {}
    for k, v in parts.items():
        where[k] = (at, v.shape[1])
        at += v.shape[1]
    return np.concatenate([np.broadcast_to(v, (P, v.shape[1])).astype(f) for v in parts.values()], 1), where


CONST_COLS = shape_constants()[0].shape[1]
WHERE = shape_constants()[1]


class Core:

    def __init__(self, nc, ctx, consts):
        self.nc, self.ctx = nc, ctx
        self.const_dram = consts
        self.sems = []
        self.consts = self.sb("consts", [P, CONST_COLS])
        self.x = self.sb("x_res", [P, NT, D])
        self.hT = self.sb("hT", [P, KD, T])
        self.cos = self.sb("cos_t", [P, T])
        self.sin = self.sb("sin_t", [P, T])

    def sb(self, name, shape, dt=F32, ctx=None):
        return (ctx or self.ctx).enter_context(self.nc.sbuf_tensor(name, shape, dt))

    def banks(self, ctx, n, tag):
        return [ctx.enter_context(self.nc.psum_tensor(f"{tag}{i}", [P, 512], F32)) for i in range(n)]

    def sem(self, name):
        self.sems.append(self.nc.alloc_semaphore(name=name))
        return self.sems[-1]

    def end_stage(self):
        if self.sems:
            self.nc.clear_and_free_semaphores(self.sems)
            self.nc.all_engine_barrier()
            self.sems = []

    def c(self, name, lo=0, hi=None):
        at, n = WHERE[name]
        return self.consts[:, at + lo:at + (n if hi is None else hi)]


def stage(build):
    def built(k, *args, **kw):
        build(k, *args, **kw)
        k.end_stage()
    return built


def row_bc(v, n=P):
    return v.rearrange("(a n) -> a n", a=1).broadcast_to([n, v.shape[0]])


@stage
def stage_load(k, x):
    nc = k.nc
    loaded = k.sem("start_loaded")
    with nc.Block() as block:
        @block.sync
        def _(sp):
            sp.dma_start(k.consts[:], k.const_dram).then_inc(loaded, 16)
            sp.dma_start(k.x[:], x[0].rearrange("(t p) d -> p t d", p=P)).then_inc(loaded, 16)
            sp.wait_ge(loaded, 32)


@stage
def stage_rope_tables(k, tag, positions, freq, cos_out, sin_out):
    nc = k.nc
    with ExitStack() as ctx:
        pos_i = k.sb(f"{tag}_pos_i", [P, T], I32, ctx)
        pos_f = k.sb(f"{tag}_pos_f", [P, T], F32, ctx)
        turns = k.sb(f"{tag}_turns", [P, T], F32, ctx)
        ang = k.sb(f"{tag}_ang", [P, 2, T], F32, ctx)
        pos_loaded = k.sem(f"{tag}_pos_loaded")
        ang_ready = k.sem(f"{tag}_ang_ready")
        two_pi = 2 * np.pi
        c1 = 6.28125
        c2 = float(np.float32(np.round((two_pi - c1) * 2 ** 20) / 2 ** 20))
        c3 = two_pi - c1 - c2
        big = 12582912.0
        with nc.Block() as block:
            @block.sync
            def _(sp):
                sp.dma_start(pos_i[:], row_bc(positions[0])).then_inc(pos_loaded, 16)

            @block.vector
            def _(v):
                v.wait_ge(pos_loaded, 16)
                v.tensor_copy(pos_f[:], pos_i[:])
                v.drain()
                v.tensor_scalar(pos_f[:], pos_f[:], k.c(freq), None, ALU.mult)
                v.drain()
                for n, quarter in ((0, 0.25), (1, 0.0)):
                    v.tensor_scalar(turns[:], pos_f[:], 1.0 / two_pi, quarter, ALU.mult, ALU.add)
                    v.drain()
                    v.tensor_scalar(turns[:], turns[:], big, -big, ALU.add, ALU.add)
                    v.drain()
                    v.scalar_tensor_tensor(ang[:, n, :], turns[:], -c1, pos_f[:], ALU.mult, ALU.add)
                    for c in (c2, c3):
                        v.drain()
                        v.scalar_tensor_tensor(ang[:, n, :], turns[:], -c, ang[:, n, :], ALU.mult, ALU.add)
                    v.drain()
                    if n == 0:
                        v.tensor_scalar(ang[:, n, :], ang[:, n, :], PI / 2, None, ALU.add)
                        v.drain()
                    v.tensor_scalar(ang[:, n, :], ang[:, n, :], 3.1415925, -3.1415925, ALU.min, ALU.max).then_inc(ang_ready, 1)

            @block.scalar
            def _(a):
                a.wait_ge(ang_ready, 1)
                a.activation(cos_out[:], ang[:, 0, :], ACT.Sin)
                a.wait_ge(ang_ready, 2)
                a.activation(sin_out[:], ang[:, 1, :], ACT.Sin)


@stage
def stage_norm(k, tag, weight, keep=None, transposed=True, eps=1e-6):
    nc = k.nc
    with ExitStack() as ctx:
        wbc = k.sb(f"{tag}_w", [P, D], F32, ctx)
        h = keep if keep is not None else k.sb(f"{tag}_h", [P, NT, D], F32, ctx)
        sq = k.sb(f"{tag}_sq", [P, D], F32, ctx)
        ss = k.sb(f"{tag}_ss", [P, NT], F32, ctx)
        tp = k.banks(ctx, 4, f"{tag}_tp")
        w_loaded, ss_ready, mean_ready = k.sem(f"{tag}_w_loaded"), k.sem(f"{tag}_ss_ready"), k.sem(f"{tag}_mean")
        root_ready, h_ready = k.sem(f"{tag}_root"), k.sem(f"{tag}_h_ready")
        turned, taken = k.sem(f"{tag}_turned"), k.sem(f"{tag}_taken")
        with nc.Block() as block:
            @block.sync
            def _(sp):
                sp.dma_start(wbc[:], row_bc(weight)).then_inc(w_loaded, 16)

            @block.scalar
            def _(a):
                for t in range(NT):
                    a.activation(sq[:], k.x[:, t, :], ACT.Square, accum_out=ss[:, t:t + 1])
                    a.drain()
                a.drain().then_inc(ss_ready, 1)
                a.wait_ge(mean_ready, 1)
                a.activation(ss[:], ss[:], ACT.Sqrt).then_inc(root_ready, 1)
                if transposed:
                    for n in range(KD):
                        a.wait_ge(turned, n + 1)
                        a.activation(k.hT[:, n, :], tp[n % 4][:], ACT.Copy).then_inc(taken, 1)

            @block.vector
            def _(v):
                v.wait_ge(ss_ready, 1)
                v.tensor_scalar(ss[:], ss[:], 1.0 / D, eps, ALU.mult, ALU.add).then_inc(mean_ready, 1)
                v.wait_ge(root_ready, 1)
                v.reciprocal(ss[:], ss[:])
                v.drain()
                v.wait_ge(w_loaded, 16)
                for t in range(NT):
                    v.scalar_tensor_tensor(h[:, t, :], k.x[:, t, :], ss[:, t:t + 1], wbc[:], ALU.mult, ALU.mult).then_inc(h_ready, 1)

            if transposed:
                @block.tensor
                def _(pe):
                    pe.wait_ge(h_ready, NT)
                    for n in range(KD):
                        if n >= 4:
                            pe.wait_ge(taken, n - 3)
                        for t in range(NT):
                            ins = pe.transpose(tp[n % 4][:, t * P:(t + 1) * P], h[:, t, n * P:(n + 1) * P], k.c("ident"))
                        ins.then_inc(turned, 1)


@stage
def stage_qk(k, tag, w_in, qkT):
    nc = k.nc
    with ExitStack() as ctx:
        W = [k.sb(f"{tag}_W{i}", [P, KD, 512], F32, ctx) for i in range(2)]
        raw = [k.sb(f"{tag}_raw{i}", [P, T], F32, ctx) for i in range(2)]
        straight = [k.sb(f"{tag}_straight{i}", [P, T], F32, ctx) for i in range(2)]
        turn = [k.sb(f"{tag}_turn{i}", [P, T], F32, ctx) for i in range(2)]
        acc = k.banks(ctx, 2, f"{tag}_acc")
        half = k.banks(ctx, 2, f"{tag}_half")
        w_loaded = [k.sem(f"{tag}_w_loaded{i}") for i in range(2)]
        slab_used, acc_ready, raw_ready = k.sem(f"{tag}_slab_used"), k.sem(f"{tag}_acc_ready"), k.sem(f"{tag}_raw_ready")
        half_ready, out_ready = k.sem(f"{tag}_half_ready"), k.sem(f"{tag}_out_ready")
        with nc.Block() as block:
            @block.sync
            def _(sp):
                with sp.Fori(0, 2) as i:
                    for b in range(2):
                        sp.wait_ge(slab_used, i * 2 + b + 1)
                        sp.dma_start(W[b][:], w_in[:, ds(i * 1024 + b * 512, 512)].rearrange("(k p) n -> p k n", p=P)).then_inc(w_loaded[b], 16)

            @block.tensor
            def _(pe):
                pe.sem_inc(slab_used, 2)
                pe.sem_inc(acc_ready, 2)
                with pe.Fori(0, 2) as i:
                    for b in range(2):
                        pe.wait_ge(w_loaded[b], i * 16 + 16)
                        for m in range(4):
                            u = i * 8 + b * 4 + m
                            pe.wait_ge(raw_ready, u + 1)
                            for n in range(KD):
                                ins = pe.matmul(acc[m % 2][:], W[b][:, n, m * P:(m + 1) * P], k.hT[:, n, :], start=(n == 0), stop=(n == KD - 1))
                            ins.then_inc(acc_ready, 1)
                            pe.wait_ge(raw_ready, u + 3)
                            pe.wait_ge(out_ready, u + 1)
                            pe.matmul(half[m % 2][:], k.c("turn64"), raw[m % 2][:], start=True, stop=True).then_inc(half_ready, 1)
                        pe.drain().then_inc(slab_used, 1)

            @block.scalar
            def _(a):
                a.sem_inc(raw_ready, 2)
                with a.Fori(0, 2) as i:
                    for m in range(8):
                        u = i * 8 + m
                        a.wait_ge(acc_ready, u + 3)
                        a.wait_ge(out_ready, u + 1)
                        a.activation(raw[m % 2][:], acc[m % 2][:], ACT.Copy).then_inc(raw_ready, 1)

            @block.vector
            def _(v):
                v.sem_inc(out_ready, 2)
                with v.Fori(0, 2) as i:
                    for m in range(8):
                        u = i * 8 + m
                        v.wait_ge(raw_ready, u + 3)
                        v.tensor_tensor(straight[m % 2][:], raw[m % 2][:], k.cos[:], ALU.mult)
                        v.wait_ge(half_ready, u + 1)
                        v.tensor_tensor(turn[m % 2][:], half[m % 2][:], k.sin[:], ALU.mult)
                        v.drain()
                        v.tensor_tensor(qkT[:, ds(u, 1), :], straight[m % 2][:].rearrange("p (a n) -> p a n", a=1),
                                        turn[m % 2][:].rearrange("p (a n) -> p a n", a=1), ALU.add).then_inc(out_ready, 1)


@stage
def stage_token_major(k, tag, w, col0, slabs, finish, lhs=None, kt=KD, ncol=512):
    nc = k.nc
    lhs = k.hT if lhs is None else lhs
    with ExitStack() as ctx:
        W = [k.sb(f"{tag}_W{i}", [P, kt, ncol], F32, ctx) for i in range(2)]
        acc = k.banks(ctx, 4, f"{tag}_acc")
        w_loaded = [k.sem(f"{tag}_w_loaded{i}") for i in range(2)]
        slab_used, acc_ready, taken = k.sem(f"{tag}_slab_used"), k.sem(f"{tag}_acc_ready"), k.sem(f"{tag}_taken")
        with nc.Block() as block:
            @block.sync
            def _(sp):
                with sp.Fori(0, slabs // 2) as i:
                    for b in range(2):
                        sp.wait_ge(slab_used, i * 2 + b + 1)
                        sp.dma_start(W[b][:], w[:, ds(i * (2 * ncol) + (col0 + b * ncol), ncol)].rearrange("(k p) n -> p k n", p=P)).then_inc(w_loaded[b], 16)

            @block.tensor
            def _(pe):
                pe.sem_inc(slab_used, 2)
                with pe.Fori(0, slabs // 2) as i:
                    for b in range(2):
                        pe.wait_ge(w_loaded[b], i * 16 + 16)
                        for t in range(NT):
                            pe.wait_ge(taken, i * 8 + b * 4 + t + 1)
                            for n in range(kt):
                                ins = pe.matmul(acc[t][:, 0:ncol], lhs[:, n, t * P:(t + 1) * P], W[b][:, n, :], start=(n == 0), stop=(n == kt - 1))
                            ins.then_inc(acc_ready, 1)
                        pe.drain().then_inc(slab_used, 1)

            @block.scalar
            def _(a):
                a.sem_inc(taken, 4)
                with a.Fori(0, slabs // 2) as i:
                    for b in range(2):
                        for t in range(NT):
                            a.wait_ge(acc_ready, i * 8 + b * 4 + t + 1)
                            finish(a, acc[t], i * 2 + b, t).then_inc(taken, 1)


@stage
def stage_lambda(k, lams, lam_neg, lam_init):
    nc = k.nc
    with ExitStack() as ctx:
        rows = k.sb("lam_rows", [P, 4, 64], F32, ctx)
        prod = k.sb("lam_prod", [P, 2, 64], F32, ctx)
        dots = k.sb("lam_dots", [P, 2], F32, ctx)
        rows_loaded, dots_ready, exp_ready = k.sem("lam_rows_loaded"), k.sem("lam_dots_ready"), k.sem("lam_exp_ready")
        with nc.Block() as block:
            @block.sync
            def _(sp):
                for n, l in enumerate(lams):
                    sp.dma_start(rows[:, n, :], row_bc(l[0])).then_inc(rows_loaded, 16)

            @block.vector
            def _(v):
                v.wait_ge(rows_loaded, 64)
                v.tensor_tensor(prod[:], rows[:, 0::2, :], rows[:, 1::2, :], ALU.mult)
                v.drain()
                v.tensor_reduce(dots[:], prod[:], AX, ALU.add).then_inc(dots_ready, 1)
                v.wait_ge(exp_ready, 1)
                v.tensor_tensor(lam_neg[:], dots[:, 1:2], dots[:, 0:1], ALU.subtract)
                v.drain()
                v.tensor_scalar(lam_neg[:], lam_neg[:], -lam_init, None, ALU.add)

            @block.scalar
            def _(a):
                a.wait_ge(dots_ready, 1)
                a.activation(dots[:], dots[:], ACT.Exp).then_inc(exp_ready, 1)


@stage
def stage_diff_attention(k, qkT, v_tok, att, ss, lam_neg):
    nc = k.nc
    scale = 64 ** -0.5
    with ExitStack() as ctx:
        Q = [k.sb(f"at_q{i}", [P, T], F32, ctx) for i in range(2)]
        K = [k.sb(f"at_k{i}", [P, T], F32, ctx) for i in range(2)]
        S = [k.sb(f"at_s{i}", [P, 2, T], F32, ctx) for i in range(2)]
        mx = [k.sb(f"at_mx{i}", [P, 2], F32, ctx) for i in range(2)]
        sm = [k.sb(f"at_sm{i}", [P, 2], F32, ctx) for i in range(2)]
        W = [k.sb(f"at_w{i}", [P, T], F32, ctx) for i in range(2)]
        WT = [k.sb(f"at_wt{i}", [P, T], F32, ctx) for i in range(2)]
        sq = k.sb("at_sq", [P, P], F32, ctx)
        sc = k.banks(ctx, 4, "at_sc")
        tp = k.banks(ctx, 2, "at_tp")
        ob = k.banks(ctx, 2, "at_ob")
        staged, heads_used = k.sem("at_staged"), k.sem("at_heads_used")
        scores_done, masked, bias_ready, exp_done = k.sem("at_scores"), k.sem("at_masked"), k.sem("at_bias"), k.sem("at_exp")
        w_ready, turned, wt_ready, out_done, out_taken = (k.sem("at_w_ready"), k.sem("at_turned"), k.sem("at_wt_ready"),
                                                         k.sem("at_out_done"), k.sem("at_out_taken"))
        with nc.Block() as block:
            @block.gpsimd
            def _(g):
                with g.Fori(0, 4) as i:
                    for b in range(2):
                        g.wait_ge(heads_used, i * 2 + b + 1)
                        h = i * 2 + b
                        g.tensor_copy(Q[b][:].rearrange("p (a n) -> p a n", a=1), qkT[:, ds(h, 1), :])
                        g.tensor_copy(K[b][:].rearrange("p (a n) -> p a n", a=1), qkT[:, ds(h + 8, 1), :])
                        g.drain().then_inc(staged, 1)

            @block.tensor
            def _(pe):
                pe.sem_inc(heads_used, 2)
                pe.sem_inc(turned, 2)
                pe.sem_inc(out_done, 2)
                with pe.Fori(0, 4) as i:
                    def scores(s):
                        b, t, u = s // 4, s % 4, i * 8 + s
                        if t == 0:
                            pe.wait_ge(staged, i * 2 + b + 1)
                        pe.wait_ge(masked, u + 1)
                        for c in range(2):
                            ins = pe.matmul(sc[2 * (t % 2) + c][:, 0:(t + 1) * P], Q[b][64 * c:64 * c + 64, t * P:(t + 1) * P],
                                            K[b][64 * c:64 * c + 64, 0:(t + 1) * P], start=True, stop=True)
                        ins.then_inc(scores_done, 1)
                        if t == NT - 1:
                            pe.drain().then_inc(heads_used, 1)

                    scores(0)
                    for s in range(8):
                        b, t, u = s // 4, s % 4, i * 8 + s
                        if s < 7:
                            scores(s + 1)
                        pe.wait_ge(w_ready, u + 3)
                        pe.wait_ge(wt_ready, u + 1)
                        for j in range(t + 1):
                            ins = pe.transpose(tp[t % 2][:, j * P:(j + 1) * P], W[t % 2][:, j * P:(j + 1) * P], k.c("ident"))
                        ins.then_inc(turned, 1)
                        pe.wait_ge(wt_ready, u + 3)
                        pe.wait_ge(out_taken, u + 1)
                        for j in range(t + 1):
                            ins = pe.matmul(ob[t % 2][:, 0:P], WT[t % 2][:, j * P:(j + 1) * P],
                                            v_tok[:, j, ds(i * 256 + b * P, P)], start=(j == 0), stop=(j == t))
                        ins.then_inc(out_done, 1)

            @block.vector
            def _(v):
                v.sem_inc(masked, 2)
                v.sem_inc(w_ready, 2)
                with v.Fori(0, 4) as i:
                    def mask_and_max(s):
                        t, par, u = s % 4, s % 2, i * 8 + s
                        v.wait_ge(scores_done, u + 1)
                        n = (t + 1) * P
                        for c in range(2):
                            ins = v.tensor_tensor(S[par][:, c, 0:n], sc[2 * par + c][:, 0:n], k.c("neg_wide", 512 - n), ALU.add)
                        ins.then_inc(masked, 1)
                        v.drain()
                        v.tensor_reduce(mx[par][:], S[par][:, :, 0:n], AX, ALU.max)
                        v.drain()
                        v.tensor_scalar(mx[par][:], mx[par][:], -scale, None, ALU.mult).then_inc(bias_ready, 1)

                    mask_and_max(0)
                    for s in range(8):
                        if s < 7:
                            mask_and_max(s + 1)
                        t, par, u = s % 4, s % 2, i * 8 + s
                        n = (t + 1) * P
                        v.wait_ge(exp_done, u + 1)
                        v.reciprocal(sm[par][:], sm[par][:])
                        v.drain()
                        v.tensor_tensor(sm[par][:, 1:2], sm[par][:, 1:2], lam_neg[:], ALU.mult)
                        v.wait_ge(turned, u + 1)
                        v.tensor_scalar(W[par][:, 0:n], S[par][:, 0, 0:n], sm[par][:, 0:1], None, ALU.mult)
                        v.drain()
                        v.scalar_tensor_tensor(W[par][:, 0:n], S[par][:, 1, 0:n], sm[par][:, 1:2], W[par][:, 0:n], ALU.mult, ALU.add).then_inc(w_ready, 1)

            @block.scalar
            def _(a):
                a.sem_inc(wt_ready, 2)
                a.sem_inc(out_taken, 2)
                with a.Fori(0, 4) as i:
                    def exps(s):
                        par, u, n = s % 2, i * 8 + s, (s % 4 + 1) * P
                        a.wait_ge(bias_ready, u + 1)
                        for c in range(2):
                            ins = a.activation(S[par][:, c, 0:n], S[par][:, c, 0:n], ACT.Exp, bias=mx[par][:, c:c + 1], scale=scale,
                                               accum_out=sm[par][:, c:c + 1])
                        a.drain().then_inc(exp_done, 1)

                    def take_out(s):
                        par, u, t = s % 2, i * 8 + s, s % 4
                        hb = i * 2 + s // 4
                        a.wait_ge(out_done, u + 3)
                        a.activation(att[:, t, ds(i * 256 + (s // 4) * P, P)], ob[par][:, 0:P], ACT.Copy)
                        a.activation(sq[:], ob[par][:, 0:P], ACT.Square, accum_out=ss[:, t, ds(hb, 1)])
                        a.drain().then_inc(out_taken, 1)

                    exps(0)
                    for s in range(8):
                        par, u, n = s % 2, i * 8 + s, (s % 4 + 1) * P
                        if s < 7:
                            exps(s + 1)
                        a.wait_ge(turned, u + 3)
                        a.wait_ge(out_done, u + 1)
                        a.activation(WT[par][:, 0:n], tp[par][:, 0:n], ACT.Copy).then_inc(wt_ready, 1)
                        if s >= 1:
                            take_out(s - 1)
                    take_out(7)


@stage
def stage_scale_and_turn(k, tag, y, ss, groups, width, eps, w_col_src, outT, gain=1.0):
    nc = k.nc
    tiles = groups * width // P
    wc = w_col_src.shape[0] // P
    with ExitStack() as ctx:
        wcol = k.sb(f"{tag}_wcol", [P, wc], F32, ctx)
        tp = k.banks(ctx, 4, f"{tag}_tp")
        w_loaded, mean_ready, root_ready, y_ready = (k.sem(f"{tag}_w_loaded"), k.sem(f"{tag}_mean"), k.sem(f"{tag}_root"), k.sem(f"{tag}_y_ready"))
        turned, taken = k.sem(f"{tag}_turned"), k.sem(f"{tag}_taken")
        with nc.Block() as block:
            @block.sync
            def _(sp):
                with nc.allow_non_contiguous_dma("one column of weights"):
                    sp.dma_start(wcol[:], w_col_src.rearrange("(a p) -> p a", p=P)).then_inc(w_loaded, 16)

            @block.vector
            def _(v):
                v.tensor_scalar(ss[:], ss[:], 1.0 / (width * gain * gain), eps / (gain * gain), ALU.mult, ALU.add).then_inc(mean_ready, 1)
                v.wait_ge(root_ready, 1)
                v.reciprocal(ss[:], ss[:])
                v.drain()
                for t in range(NT):
                    yt = y[:, t, :].rearrange("p (g w) -> p g w", g=groups)
                    v.tensor_tensor(yt, yt, ss[:, t, :].rearrange("p (g a) -> p g a", a=1).broadcast_to([P, groups, width]), ALU.mult).then_inc(y_ready, 1)

            @block.tensor
            def _(pe):
                pe.wait_ge(y_ready, NT)
                for n in range(tiles):
                    if n >= 4:
                        pe.wait_ge(taken, n - 3)
                    for t in range(NT):
                        ins = pe.transpose(tp[n % 4][:, t * P:(t + 1) * P], y[:, t, n * P:(n + 1) * P], k.c("ident"))
                    ins.then_inc(turned, 1)

            @block.scalar
            def _(a):
                a.wait_ge(mean_ready, 1)
                a.activation(ss[:], ss[:], ACT.Sqrt).then_inc(root_ready, 1)
                a.wait_ge(w_loaded, 16)
                for n in range(tiles):
                    a.wait_ge(turned, n + 1)
                    a.activation(outT[:, n, :], tp[n % 4][:], ACT.Copy, scale=wcol[:, n % wc:n % wc + 1]).then_inc(taken, 1)


XBC0 = 3 * 1024 + 2048
Z0 = 3 * 1024
DT0 = XBC0 + 4096
GA0 = DT0 + 32


@stage
def stage_conv(k, w_in, conv_w, conv_b, xbcT):
    nc = k.nc
    with ExitStack() as ctx:
        W = [k.sb(f"cv_W{i}", [P, KD, 512], F32, ctx) for i in range(2)]
        u = [k.sb(f"cv_u{i}", [P, T + 3], F32, ctx) for i in range(2)]
        y = [k.sb(f"cv_y{i}", [P, T], F32, ctx) for i in range(2)]
        taps = k.sb("cv_taps", [P, 4, 32], F32, ctx)
        bias = k.sb("cv_bias", [P, 32], F32, ctx)
        acc = k.banks(ctx, 4, "cv_acc")
        w_loaded = [k.sem(f"cv_w_loaded{i}") for i in range(2)]
        taps_loaded, slab_used, acc_ready, u_ready, y_ready, out_ready = (k.sem("cv_taps_loaded"), k.sem("cv_slab_used"), k.sem("cv_acc_ready"),
                                                                     k.sem("cv_u_ready"), k.sem("cv_y_ready"), k.sem("cv_out_ready"))
        pad_zero = k.sem("cv_pad_zero")
        with nc.Block() as block:
            @block.sync
            def _(sp):
                with nc.allow_non_contiguous_dma("a column of taps per block of channels"):
                    for n in range(4):
                        sp.dma_start(taps[:, n, :], conv_w[n].rearrange("(a p) -> p a", p=P)).then_inc(taps_loaded, 16)
                    sp.dma_start(bias[:], conv_b.rearrange("(a p) -> p a", p=P)).then_inc(taps_loaded, 16)
                with sp.Fori(0, 4) as i:
                    for b in range(2):
                        sp.wait_ge(slab_used, i * 2 + b + 1)
                        sp.dma_start(W[b][:], w_in[:, ds(i * 1024 + (XBC0 + b * 512), 512)].rearrange("(k p) n -> p k n", p=P)).then_inc(w_loaded[b], 16)

            @block.tensor
            def _(pe):
                pe.sem_inc(slab_used, 2)
                with pe.Fori(0, 4) as i:
                    for b in range(2):
                        pe.wait_ge(w_loaded[b], i * 16 + 16)
                        for m in range(4):
                            pe.wait_ge(u_ready, i * 8 + b * 4 + m + 1)
                            for n in range(KD):
                                ins = pe.matmul(acc[m][:], W[b][:, n, m * P:(m + 1) * P], k.hT[:, n, :], start=(n == 0), stop=(n == KD - 1))
                            ins.then_inc(acc_ready, 1)
                        pe.drain().then_inc(slab_used, 1)

            @block.scalar
            def _(a):
                a.sem_inc(u_ready, 4)
                a.sem_inc(out_ready, 2)
                a.wait_ge(pad_zero, 1)
                with a.Fori(0, 4) as i:
                    def silu(m):
                        a.wait_ge(y_ready, i * 8 + m + 3)
                        a.activation(xbcT[:, ds(i * 8 + m, 1), :], y[m % 2][:].rearrange("p (a n) -> p a n", a=1), ACT.Silu).then_inc(out_ready, 1)

                    for m in range(8):
                        a.wait_ge(acc_ready, i * 8 + m + 1)
                        a.wait_ge(y_ready, i * 8 + m + 1)
                        a.activation(u[m % 2][:, 3:], acc[m % 4][:], ACT.Copy).then_inc(u_ready, 1)
                        if m >= 1:
                            silu(m - 1)
                    silu(7)

            @block.vector
            def _(v):
                v.memset(u[0][:, 0:3], 0.0)
                v.memset(u[1][:, 0:3], 0.0)
                v.drain().then_inc(pad_zero, 1)
                v.sem_inc(y_ready, 2)
                v.wait_ge(taps_loaded, 80)
                with v.Fori(0, 4) as i:
                    for m in range(8):
                        c = i * 8 + m
                        uu, yy = u[m % 2], y[m % 2]
                        v.wait_ge(u_ready, c + 5)
                        v.wait_ge(out_ready, c + 1)
                        v.tensor_scalar(yy[:], uu[:, 3:], taps[:, 3, ds(c, 1)], bias[:, ds(c, 1)], ALU.mult, ALU.add)
                        for n in range(3):
                            v.drain()
                            ins = v.scalar_tensor_tensor(yy[:], uu[:, n:n + T], taps[:, n, ds(c, 1)], yy[:], ALU.mult, ALU.add)
                        ins.then_inc(y_ready, 1)


@stage
def stage_turn(k, tag, src, tiles, dst):
    nc = k.nc
    with ExitStack() as ctx:
        tp = k.banks(ctx, 8, f"{tag}_tp")
        turned, taken_a, taken_v = k.sem(f"{tag}_turned"), k.sem(f"{tag}_taken_a"), k.sem(f"{tag}_taken_v")
        groups = [(t, q) for q in range(tiles // 4) for t in range(NT)]
        with nc.Block() as block:
            @block.tensor
            def _(pe):
                for n, (t, q) in enumerate(groups):
                    if n >= 8:
                        pe.wait_ge(taken_v if n % 2 else taken_a, n // 2 - 3)
                    for j in range(4):
                        ins = pe.transpose(tp[n % 8][:, j * P:(j + 1) * P], src[:, 4 * q + j, t * P:(t + 1) * P], k.c("ident"))
                    ins.then_inc(turned, 1)

            @block.scalar
            def _(a):
                for n, (t, q) in enumerate(groups):
                    if n % 2 == 0:
                        a.wait_ge(turned, n + 1)
                        a.activation(dst[:, t, q * 512:(q + 1) * 512], tp[n % 8][:], ACT.Copy).then_inc(taken_a, 1)

            @block.vector
            def _(v):
                for n, (t, q) in enumerate(groups):
                    if n % 2 == 1:
                        v.wait_ge(turned, n + 1)
                        v.tensor_copy(dst[:, t, q * 512:(q + 1) * 512], tp[n % 8][:]).then_inc(taken_v, 1)


@stage
def stage_ssd_steps(k, w_in, dt_bias, a_log, dt, cum, ecum, wtail, etot, adt):
    nc = k.nc
    H = 32
    with ExitStack() as ctx:
        W = k.sb("sd_W", [P, KD, H], F32, ctx)
        bias = k.sb("sd_bias", [P, H], F32, ctx)
        al = k.sb("sd_alog", [P, H], F32, ctx)
        raw = k.sb("sd_raw", [P, NT, H], F32, ctx)
        mag = k.sb("sd_mag", [P, NT, H], F32, ctx)
        tot = k.sb("sd_tot", [P, NT, H], F32, ctx)
        acc = k.banks(ctx, 3, "sd_acc")
        loaded, raw_mm, mag_ready, ln_ready = k.sem("sd_loaded"), k.sem("sd_raw_mm"), k.sem("sd_mag_ready"), k.sem("sd_ln_ready")
        adt_ready, sums_ready, cum_ready = k.sem("sd_adt_ready"), k.sem("sd_sums_ready"), k.sem("sd_cum_ready")
        with nc.Block() as block:
            @block.sync
            def _(sp):
                sp.dma_start(W[:], w_in[:, DT0:DT0 + H].rearrange("(k p) n -> p k n", p=P)).then_inc(loaded, 16)
                sp.dma_start(bias[:], row_bc(dt_bias)).then_inc(loaded, 16)
                sp.dma_start(al[:], row_bc(a_log)).then_inc(loaded, 16)

            @block.tensor
            def _(pe):
                pe.wait_ge(loaded, 48)
                for t in range(NT):
                    for n in range(KD):
                        ins = pe.matmul(acc[0][:, t * H:(t + 1) * H], k.hT[:, n, t * P:(t + 1) * P], W[:, n, :], start=(n == 0), stop=(n == KD - 1))
                ins.then_inc(raw_mm, 1)
                pe.wait_ge(adt_ready, 1)
                flat = adt[:].rearrange("p c h -> p (c h)")
                pe.matmul(acc[1][:, 0:NT * H], k.c("upto"), flat, start=True, stop=True)
                pe.matmul(acc[2][:, 0:NT * H], k.c("ones"), flat, start=True, stop=True).then_inc(sums_ready, 1)

            @block.vector
            def _(v):
                bc = lambda t: t[:].rearrange("p (a h) -> p a h", a=1).broadcast_to([P, NT, H])
                ps = lambda n: acc[n][:, 0:NT * H].rearrange("p (c h) -> p c h", h=H)
                v.wait_ge(raw_mm, 1)
                v.tensor_tensor(raw[:], ps(0), bc(bias), ALU.add)
                v.drain()
                v.scalar_tensor_tensor(mag[:], raw[:], -1.0, raw[:], ALU.mult, ALU.min).then_inc(mag_ready, 1)
                v.wait_ge(ln_ready, 1)
                v.scalar_tensor_tensor(dt[:], raw[:], 0.0, mag[:], ALU.max, ALU.add)
                v.drain()
                v.scalar_tensor_tensor(adt[:], dt[:], -1.0, bc(al), ALU.mult, ALU.mult).then_inc(adt_ready, 1)
                v.wait_ge(sums_ready, 1)
                v.tensor_copy(cum[:], ps(1))
                v.tensor_copy(tot[:], ps(2))
                v.drain()
                v.tensor_tensor(wtail[:], tot[:], cum[:], ALU.subtract).then_inc(cum_ready, 1)

            @block.scalar
            def _(a):
                a.wait_ge(loaded, 48)
                a.activation(al[:], al[:], ACT.Exp)
                a.wait_ge(mag_ready, 1)
                a.activation(mag[:], mag[:], ACT.Exp)
                a.drain()
                a.activation(mag[:], mag[:], ACT.Ln, bias=1.0).then_inc(ln_ready, 1)
                a.wait_ge(cum_ready, 1)
                a.activation(ecum[:], cum[:], ACT.Exp)
                a.activation(etot[:], tot[:], ACT.Exp)
                a.activation(wtail[:], wtail[:], ACT.Exp)


@stage
def stage_ssd(k, xbcT, xs, btok, zs, dt, cum, ecum, wtail, etot, adt, d_skip, ss):
    nc = k.nc
    HG, N = 4, 256
    with ExitStack() as ctx:
        BT = [k.sb(f"ss_bt{i}", [P, T], F32, ctx) for i in range(1)]
        CT = [k.sb(f"ss_ct{i}", [P, T], F32, ctx) for i in range(1)]
        BK = [k.sb(f"ss_bk{i}", [P, NT, P], F32, ctx) for i in range(1)]
        xdt = [k.sb(f"ss_xdt{i}", [P, HG, 64], F32, ctx) for i in range(2)]
        xw = [k.sb(f"ss_xw{i}", [P, HG, 64], F32, ctx) for i in range(2)]
        rows = [k.sb(f"ss_rows{i}", [P, HG, P], F32, ctx) for i in range(2)]
        dec = [k.sb(f"ss_dec{i}", [P, HG, P], F32, ctx) for i in range(2)]
        state = k.sb("ss_state", [P, HG, 64], F32, ctx)
        yo = k.sb("ss_yo", [P, HG, 64], F32, ctx)
        xd = k.sb("ss_xd", [P, HG, 64], F32, ctx)
        dsk = k.sb("ss_dsk", [P, 32], F32, ctx)
        sq = k.sb("ss_sq", [P, N], F32, ctx)
        cb_b = k.banks(ctx, 2, "ss_cb")
        cs_b = k.banks(ctx, 2, "ss_cs")
        yd_b = k.banks(ctx, 2, "ss_yd")
        st_b = k.banks(ctx, 2, "ss_st")
        sem = lambda n: k.sem("ss_" + n)
        dsk_loaded, staged, rows_ready, sums_ready, seg_ready, exp_ready, dec_ready, y_ready, state_ready, chunk_done = map(
            sem, ("dsk_loaded", "staged", "rows_ready", "sums_ready", "seg_ready", "exp_ready", "dec_ready", "y_ready", "state_ready", "chunk_done"))
        group_used = sem("group_used")
        bc = lambda ap: ap.rearrange("p (h a) -> p h a", a=1).broadcast_to([P, HG, 64])
        hv = lambda ap: ap.rearrange("p (h e) -> p h e", h=HG)
        with nc.Block() as block:
            @block.sync
            def _(sp):
                sp.dma_start(dsk[:], row_bc(d_skip)).then_inc(dsk_loaded, 16)

            @block.gpsimd
            def _(g):
                with g.Fori(0, 8) as i:
                    g.wait_ge(group_used, i + 1)
                    one = lambda t: t[:].rearrange("p (a n) -> p a n", a=1)
                    g.tensor_copy(one(BT[0]), xbcT[:, ds(i + 16, 1), :])
                    g.tensor_copy(one(CT[0]), xbcT[:, ds(i + 24, 1), :])
                    g.tensor_copy(BK[0][:], btok[:, :, ds(i * P, P)])
                    g.drain().then_inc(staged, 1)

            @block.tensor
            def _(pe):
                pe.sem_inc(group_used, 1)
                with pe.Fori(0, 8) as i:
                    pe.wait_ge(staged, i + 1)

                    def head_part(c):
                        u = i * 4 + c
                        pe.wait_ge(rows_ready, u + 1)
                        pe.matmul(cs_b[c % 2][:], k.c("ones"), rows[c % 2][:].rearrange("p h n -> p (h n)"), start=True, stop=True)
                        pe.matmul(cb_b[c % 2][:, 0:P], BT[0][:, c * P:(c + 1) * P], CT[0][:, c * P:(c + 1) * P], start=True, stop=True).then_inc(sums_ready, 1)

                    head_part(0)
                    for c in range(NT):
                        u = i * 4 + c
                        if c < NT - 1:
                            head_part(c + 1)
                        pe.wait_ge(dec_ready, u + 1)
                        for h in range(HG):
                            pe.matmul(yd_b[c % 2][:, h * 64:(h + 1) * 64], dec[c % 2][:, h, :], xdt[c % 2][:, h, :], start=True, stop=True)
                        if c < NT - 1:
                            pe.matmul(st_b[c % 2][:, 0:N], BK[0][:, c, :], xw[c % 2][:].rearrange("p h e -> p (h e)"), start=True, stop=True)
                        if c > 0:
                            pe.wait_ge(state_ready, i * 3 + c)
                            pe.matmul(yd_b[c % 2][:, N:2 * N], CT[0][:, c * P:(c + 1) * P], state[:].rearrange("p h e -> p (h e)"), start=True, stop=True)
                        pe.drain().then_inc(y_ready, 1)
                    pe.drain().then_inc(group_used, 1)

            @block.vector
            def _(v):
                v.wait_ge(dsk_loaded, 16)
                with v.Fori(0, 8) as i:
                    xv = lambda c: hv(xs[:, c, ds(i * N, N)])
                    hs = ds(i * HG, HG)

                    def make_rows(c):
                        for h in range(HG):
                            ins = v.tensor_scalar(rows[c % 2][:, h, :], k.c("upto"), adt[:, c, ds(i * HG + h, 1)], None, ALU.mult)
                        ins.then_inc(rows_ready, 1)

                    def decays(c):
                        u = i * 4 + c
                        v.wait_ge(sums_ready, u + 1)
                        for h in range(HG):
                            ins = v.scalar_tensor_tensor(dec[c % 2][:, h, :], cs_b[c % 2][:, h * P:(h + 1) * P], cum[:, c, ds(i * HG + h, 1)],
                                                         k.c("neg_after"), ALU.subtract, ALU.add)
                        ins.then_inc(seg_ready, 1)
                        v.tensor_tensor(xdt[c % 2][:], xv(c), bc(dt[:, c, hs]), ALU.mult)
                        v.drain()
                        v.tensor_tensor(xw[c % 2][:], xdt[c % 2][:], bc(wtail[:, c, hs]), ALU.mult)
                        v.wait_ge(exp_ready, u + 1)
                        v.tensor_tensor(dec[c % 2][:], dec[c % 2][:], cb_b[c % 2][:, 0:P].rearrange("p (a n) -> p a n", a=1).broadcast_to([P, HG, P]),
                                        ALU.mult).then_inc(dec_ready, 1)

                    def outputs(c):
                        u = i * 4 + c
                        v.drain()
                        v.tensor_tensor(xd[:], xv(c), bc(dsk[:, hs]), ALU.mult)
                        v.drain()
                        v.wait_ge(y_ready, u + 1)
                        if c < NT - 1:
                            if c > 0:
                                v.tensor_tensor(state[:], state[:], bc(etot[:, c, hs]), ALU.mult)
                                v.drain()
                                v.tensor_tensor(state[:], state[:], hv(st_b[c % 2][:, 0:N]), ALU.add).then_inc(state_ready, 1)
                            else:
                                v.tensor_copy(state[:], hv(st_b[c % 2][:, 0:N])).then_inc(state_ready, 1)
                        v.tensor_tensor(xd[:], xd[:], hv(yd_b[c % 2][:, 0:N]), ALU.add)
                        if c > 0:
                            v.tensor_tensor(yo[:], hv(yd_b[c % 2][:, N:2 * N]), bc(ecum[:, c, hs]), ALU.mult)
                            v.drain()
                            v.tensor_tensor(xd[:], xd[:], yo[:], ALU.add)
                        v.drain()
                        v.tensor_tensor(xv(c), xd[:], hv(zs[:, c, ds(i * N, N)]), ALU.mult).then_inc(chunk_done, 1)

                    make_rows(0)
                    make_rows(1)
                    decays(0)
                    for c in range(NT):
                        if c + 1 < NT:
                            if c + 2 < NT:
                                make_rows(c + 2)
                            decays(c + 1)
                        outputs(c)

            @block.scalar
            def _(a):
                with a.Fori(0, 8) as i:
                    def square(c):
                        a.wait_ge(chunk_done, i * 4 + c + 1)
                        a.activation(sq[:], xs[:, c, ds(i * N, N)], ACT.Square, accum_out=ss[:, c, ds(i, 1)])
                        a.drain()

                    for c in range(NT):
                        a.wait_ge(seg_ready, i * 4 + c + 1)
                        a.activation(dec[c % 2][:], dec[c % 2][:], ACT.Exp).then_inc(exp_ready, 1)
                        if c >= 1:
                            square(c - 1)
                    square(NT - 1)


E = 64
EH = 512
CAP = 128
XB = 7
NA = 2 * T
SLOTS = (E + XB) * CAP
FAR = 4096


@stage
def stage_merge(k, w_in, w_att, w_ssd, attT, yT, mergedT):
    nc = k.nc
    CW = P
    with ExitStack() as ctx:
        WA = [k.sb(f"mg_WA{i}", [P, 3, KD, CW], F32, ctx) for i in range(2)]
        WS = [k.sb(f"mg_WS{i}", [P, 16, CW], F32, ctx) for i in range(2)]
        sig = [k.sb(f"mg_sig{i}", [P, 2, T], F32, ctx) for i in range(2)]
        part = [k.sb(f"mg_part{i}", [P, 2, T], F32, ctx) for i in range(2)]
        acc = [k.banks(ctx, 2, f"mg_acc{n}_") for n in range(4)]
        w_loaded = [k.sem(f"mg_w_loaded{i}") for i in range(2)]
        slab_used, gates_ready, outs_ready, sig_ready, out_taken = (k.sem("mg_slab_used"), k.sem("mg_gates_ready"), k.sem("mg_outs_ready"),
                                                                k.sem("mg_sig_ready"), k.sem("mg_out_taken"))
        with nc.Block() as block:
            @block.sync
            def _(sp):
                with sp.Fori(0, 4) as i:
                    for b in range(2):
                        sp.wait_ge(slab_used, i * 2 + b + 1)
                        col = lambda off: ds(i * (2 * CW) + (off + b * CW), CW)
                        for n, (w, off) in enumerate(((w_in, GA0), (w_in, GA0 + D), (w_att, 0))):
                            sp.dma_start(WA[b][:, n], w[:, col(off)].rearrange("(k p) n -> p k n", p=P)).then_inc(w_loaded[b], 16)
                        sp.dma_start(WS[b][:], w_ssd[:, col(0)].rearrange("(k p) n -> p k n", p=P)).then_inc(w_loaded[b], 16)

            @block.tensor
            def _(pe):
                pe.sem_inc(slab_used, 2)
                with pe.Fori(0, 4) as i:
                    for b in range(2):
                        pe.wait_ge(w_loaded[b], i * 64 + 64)
                        u = i * 2 + b
                        pe.wait_ge(sig_ready, u + 1)
                        for g in range(2):
                            for n in range(KD):
                                ins = pe.matmul(acc[g][b][:], WA[b][:, g, n, :], k.hT[:, n, :], start=(n == 0), stop=(n == KD - 1))
                        ins.then_inc(gates_ready, 1)
                        pe.wait_ge(out_taken, u + 1)
                        for n in range(KD):
                            pe.matmul(acc[2][b][:], WA[b][:, 2, n, :], attT[:, n, :], start=(n == 0), stop=(n == KD - 1))
                        for n in range(16):
                            ins = pe.matmul(acc[3][b][:], WS[b][:, n, :], yT[:, n, :], start=(n == 0), stop=(n == 15))
                        ins.then_inc(outs_ready, 1)
                        pe.drain().then_inc(slab_used, 1)

            @block.scalar
            def _(a):
                a.sem_inc(sig_ready, 2)
                with a.Fori(0, 4) as i:
                    for m in range(2):
                        u = i * 2 + m
                        a.wait_ge(gates_ready, u + 1)
                        a.wait_ge(out_taken, u + 1)
                        for g in range(2):
                            ins = a.activation(sig[m][:, g, :], acc[g][m][:], ACT.Sigmoid)
                        ins.then_inc(sig_ready, 1)

            @block.vector
            def _(v):
                v.sem_inc(out_taken, 2)
                with v.Fori(0, 4) as i:
                    for m in range(2):
                        u = i * 2 + m
                        v.wait_ge(sig_ready, u + 3)
                        v.wait_ge(outs_ready, u + 1)
                        for g in range(2):
                            ins = v.tensor_tensor(part[m][:, g, :], sig[m][:, g, :], acc[2 + g][m][:], ALU.mult)
                        ins.then_inc(out_taken, 1)
                        v.drain()
                        v.tensor_tensor(mergedT[:, ds(u, 1), :], part[m][:, 0:1, :], part[m][:, 1:2, :], ALU.add)


@stage
def stage_residual(k, tag, w, lhs, kt=KD):
    nc = k.nc
    RT = 8
    with ExitStack() as ctx:
        W = [k.sb(f"{tag}_W{i}", [P, RT, 512], F32, ctx) for i in range(2)]
        acc = k.banks(ctx, 8, f"{tag}_acc")
        w_loaded = [k.sem(f"{tag}_w_loaded{i}") for i in range(2)]
        slab_used, acc_ready = k.sem(f"{tag}_slab_used"), k.sem(f"{tag}_acc_ready")
        steps = [(s, r) for s in range(2) for r in range(0, kt, RT)]
        with nc.Block() as block:
            @block.sync
            def _(sp):
                for n, (s, r) in enumerate(steps):
                    if n >= 2:
                        sp.wait_ge(slab_used, n - 1)
                    hi = min(r + RT, kt)
                    sp.dma_start(W[n % 2][:, 0:hi - r, :], w[r * P:hi * P, s * 512:(s + 1) * 512].rearrange("(k p) n -> p k n", p=P)).then_inc(w_loaded[n % 2], 16)

            @block.tensor
            def _(pe):
                for n, (s, r) in enumerate(steps):
                    pe.wait_ge(w_loaded[n % 2], 16 * (n // 2 + 1))
                    hi = min(r + RT, kt)
                    for t in range(NT):
                        for q in range(r, hi):
                            ins = pe.matmul(acc[s * 4 + t][:], lhs[:, q, t * P:(t + 1) * P], W[n % 2][:, q - r, :], start=(q == 0), stop=(q == kt - 1))
                        if hi == kt:
                            ins.then_inc(acc_ready, 1)
                    pe.drain().then_inc(slab_used, 1)

            @block.vector
            def _(v):
                for n in range(8):
                    s, t = n // 4, n % 4
                    v.wait_ge(acc_ready, n + 1)
                    v.tensor_tensor(k.x[:, t, s * 512:(s + 1) * 512], k.x[:, t, s * 512:(s + 1) * 512], acc[n][:], ALU.add)


@stage
def stage_route(k, w_gr, b_gr, w_er, b_er, h2, h2_rows, slot_list, gidx, sidx, xexp, weights):
    nc = k.nc
    G, J, A = 8, 8, 8
    with ExitStack() as ctx:
        t_ = lambda n, s, dt=F32: k.sb("rt_" + n, s, dt, ctx)
        W, bias = t_("W", [P, KD, 72]), t_("bias", [P, 72])
        lg = t_("lg", [P, NT, 72])
        m1, m2, cand, sel = t_("m1", [P, NT]), t_("m2", [P, NT]), t_("cand", [P, NT, 8]), t_("sel", [P, NT])
        go, eo = t_("go", [P, NT, G]), t_("eo", [P, 2, NT, J])
        prod, esel = t_("prod", [P, NT, J, G]), t_("esel", [P, NT, J])
        gs, gex, ex = t_("gs", [P, NT]), t_("gex", [P, NT, G]), t_("ex", [P, NT])
        O, before = t_("O", [P, A, E]), t_("before", [P, A, E])
        tmp, rank, da, db = t_("tmp", [P, A, E]), t_("rank", [P, A]), t_("da", [P, A]), t_("db", [P, A])
        cnt, xb, xend, xbase = t_("cnt", [P, E]), t_("xb", [P, E]), t_("xend", [P, E]), t_("xbase", [P, E])
        dest, ids = t_("dest", [P, A], U32), t_("ids", [P, A], I32)
        empty = t_("empty", [E + XB, P], I32)
        lst_i, lst_f = t_("lst_i", [E + XB, P], I32), t_("lst_f", [E + XB, P])
        gf, sf, far = t_("gf", [P, E + XB]), t_("sf", [P, E + XB]), t_("far", [P, E + XB])
        xe = t_("xe", [1, 8])
        xcmp = t_("xcmp", [1, E])
        eight = t_("eight", [P, 8])
        one64 = t_("one64", [P, E])
        acc = k.banks(ctx, 4, "rt_acc")
        (loaded, lg_mm, gmax_ready, gexp_ready, emax_ready, eexp_ready, sums_in, sums_ready, empty_ready, empty_stored, dest_ready,
         scattered, list_loaded, list_f, list_turned, rows_stored) = (k.sem("rt_" + n) for n in (
             "loaded", "lg_mm", "gmax", "gexp", "emax", "eexp", "sums_in", "sums_ready", "empty_ready", "empty_stored", "dest_ready",
             "scattered", "list_loaded", "list_f", "list_turned", "rows_stored"))
        with nc.Block() as block:
            @block.sync
            def _(sp):
                sp.dma_start(W[:, :, 0:8], w_gr.rearrange("(k p) n -> p k n", p=P)).then_inc(loaded, 16)
                sp.dma_start(W[:, :, 8:72], w_er.rearrange("(k p) n -> p k n", p=P)).then_inc(loaded, 16)
                sp.dma_start(bias[:, 0:8], row_bc(b_gr)).then_inc(loaded, 16)
                sp.dma_start(bias[:, 8:72], row_bc(b_er)).then_inc(loaded, 16)
                sp.dma_start(h2_rows.rearrange("(t p) d -> p t d", p=P), h2[:]).then_inc(rows_stored, 16)
                sp.wait_ge(empty_ready, 1)
                sp.dma_start(slot_list.rearrange("(b p) a -> b (p a)", p=P), empty[:]).then_inc(empty_stored, 16)
                sp.wait_ge(scattered, 16 * A)
                sp.dma_start(lst_i[:], slot_list.rearrange("(b p) a -> b (p a)", p=P)).then_inc(list_loaded, 16)
                sp.wait_ge(rows_stored, 16)

            @block.gpsimd
            def _(g):
                g.wait_ge(empty_stored, 16)
                g.wait_ge(dest_ready, 1)
                for a in range(A):
                    g.indirect_dma_start(slot_list, bass.IndirectOffsetOnAxis(dest[:, a:a + 1], 0), ids[:, a:a + 1], None,
                                         bounds_check=SLOTS - 1, oob_is_err=False).then_inc(scattered, 16)

            @block.tensor
            def _(pe):
                pe.wait_ge(loaded, 64)
                for t in range(NT):
                    for n in range(KD):
                        ins = pe.matmul(acc[0][:, t * 72:(t + 1) * 72], k.hT[:, n, t * P:(t + 1) * P], W[:, n, :], start=(n == 0), stop=(n == KD - 1))
                ins.then_inc(lg_mm, 1)
                pe.wait_ge(sums_in, 1)
                flat = lambda t: t[:].rearrange("p a e -> p (a e)")
                pe.matmul(acc[1][:], k.c("before"), flat(O), start=True, stop=False)
                pe.matmul(acc[1][:], k.c("ones"), flat(before), start=False, stop=True)
                pe.matmul(acc[2][:, 0:E], k.c("ones"), cnt[:], start=True, stop=True).then_inc(sums_ready, 1)
                pe.wait_ge(list_f, 1)
                pe.transpose(acc[3][:, 0:E + XB], lst_f[:], k.c("ident")[0:E + XB, 0:E + XB]).then_inc(list_turned, 1)

            @block.scalar
            def _(a):
                a.wait_ge(gmax_ready, 1)
                a.activation(gex[:], gex[:], ACT.Exp).then_inc(gexp_ready, 1)
                a.wait_ge(emax_ready, 1)
                a.activation(ex[:], ex[:], ACT.Exp).then_inc(eexp_ready, 1)

            @block.vector
            def _(v):
                def do(f, *args, **kw):
                    ins = f(*args, **kw)
                    v.drain()
                    return ins

                bc3 = lambda ap, n: ap.rearrange("p (t a) -> p t a", a=1).broadcast_to([P, ap.shape[1], n])
                iota8 = eight[:].rearrange("p (a j) -> p a j", a=1).broadcast_to([P, NT, 8])

                def first_max(vals, best, onehot):
                    do(v.tensor_reduce, best[:], vals, AX, ALU.max)
                    do(v.tensor_tensor, cand[:], vals, bc3(best[:], 8), ALU.is_equal)
                    do(v.tensor_scalar, cand[:], cand[:], -100.0, 100.0, ALU.mult, ALU.add)
                    do(v.tensor_tensor, cand[:], cand[:], iota8, ALU.add)
                    do(v.tensor_reduce, sel[:], cand[:], AX, ALU.min)
                    do(v.tensor_tensor, onehot, iota8, bc3(sel[:], 8), ALU.is_equal)

                v.memset(empty[:], FAR)
                v.drain().then_inc(empty_ready, 1)
                v.memset(far[:], 0.0)
                v.memset(one64[:], 1.0)
                for j in range(8):
                    v.memset(eight[:, j:j + 1], float(j))
                for a in range(A):
                    v.tensor_scalar(ids[:, a:a + 1], k.c("rank"), float(a * P), None, ALU.add)
                v.wait_ge(loaded, 64)
                v.wait_ge(lg_mm, 1)
                do(v.tensor_tensor, lg[:], acc[0][:, 0:NT * 72].rearrange("p (t n) -> p t n", n=72),
                   bias[:].rearrange("p (a n) -> p a n", a=1).broadcast_to([P, NT, 72]), ALU.add)
                first_max(lg[:, :, 0:8], m1, go[:])
                do(v.tensor_tensor, gex[:], lg[:, :, 0:8], bc3(m1[:], 8), ALU.subtract).then_inc(gmax_ready, 1)
                el = lg[:, :, 8:72].rearrange("p t (g j) -> p t j g", g=G)
                for t in range(NT):
                    v.tensor_tensor(prod[:, t], el[:, t], go[:, t:t + 1, :].broadcast_to([P, J, G]), ALU.mult)
                v.drain()
                do(v.tensor_reduce, esel[:], prod[:], AX, ALU.add)
                first_max(esel[:], m1, eo[:, 0])
                do(v.scalar_tensor_tensor, esel[:], eo[:, 0], -3e38, esel[:], ALU.mult, ALU.add)
                first_max(esel[:], m2, eo[:, 1])
                do(v.tensor_tensor, ex[:], m2[:], m1[:], ALU.subtract).then_inc(emax_ready, 1)
                v.wait_ge(gexp_ready, 1)
                do(v.tensor_reduce, gs[:], gex[:], AX, ALU.add)
                v.wait_ge(eexp_ready, 1)
                do(v.tensor_scalar, sel[:], ex[:], 1.0, None, ALU.add)
                do(v.tensor_tensor, sel[:], sel[:], gs[:], ALU.mult)
                do(v.reciprocal, weights[:, 0, :], sel[:])
                do(v.tensor_tensor, weights[:, 1, :], weights[:, 0, :], ex[:], ALU.mult)
                for c in range(2):
                    for t in range(NT):
                        v.tensor_tensor(O[:, c * NT + t].rearrange("p (g j) -> p g j", g=G),
                                        go[:, t].rearrange("p (g a) -> p g a", a=1).broadcast_to([P, G, J]),
                                        eo[:, c, t:t + 1, :].broadcast_to([P, G, J]), ALU.mult)
                v.memset(before[:, 0], 0.0)
                v.drain()
                for a in range(1, A):
                    do(v.tensor_tensor, before[:, a], before[:, a - 1], O[:, a - 1], ALU.add)
                do(v.tensor_tensor, cnt[:], before[:, A - 1], O[:, A - 1], ALU.add).then_inc(sums_in, 1)
                v.wait_ge(sums_ready, 1)
                ps1 = acc[1][:].rearrange("p (a e) -> p a e", e=E)
                do(v.tensor_tensor, tmp[:], O[:], ps1, ALU.mult)
                do(v.tensor_reduce, rank[:], tmp[:], AX, ALU.add)
                do(v.tensor_copy, cnt[:], acc[2][:, 0:E])
                do(v.tensor_scalar, xb[:], cnt[:], float(CAP), None, ALU.is_gt)
                for m in (2, 3):
                    do(v.scalar_tensor_tensor, xb[:], cnt[:], float(m * CAP), xb[:], ALU.is_gt, ALU.add)
                do(v.tensor_tensor_scan, xend[:], one64[:], xb[:], 0.0, ALU.mult, ALU.add)
                do(v.tensor_tensor, xbase[:], xend[:], xb[:], ALU.subtract)
                do(v.tensor_scalar, xbase[:], xbase[:], float(CAP), float((E - 1) * CAP), ALU.mult, ALU.add)
                bce = lambda ap: ap.rearrange("p (a e) -> p a e", a=1).broadcast_to([P, A, E])
                do(v.tensor_tensor, tmp[:], O[:], bce(k.c("expert_slot")), ALU.mult)
                do(v.tensor_reduce, da[:], tmp[:], AX, ALU.add)
                do(v.tensor_tensor, tmp[:], O[:], bce(xbase[:]), ALU.mult)
                do(v.tensor_reduce, db[:], tmp[:], AX, ALU.add)
                do(v.tensor_tensor, db[:], db[:], da[:], ALU.subtract)
                do(v.tensor_tensor, da[:], da[:], rank[:], ALU.add)
                do(v.scalar_tensor_tensor, db[:], rank[:], float(CAP), db[:], ALU.is_ge, ALU.mult)
                do(v.tensor_tensor, da[:], da[:], db[:], ALU.add)
                v.tensor_copy(dest[:], da[:])
                v.drain().then_inc(dest_ready, 1)
                v.memset(xe[:], 0.0)
                v.drain()
                for b in range(XB):
                    do(v.tensor_scalar, xcmp[:], xend[0:1, :], float(b), None, ALU.is_le)
                    do(v.tensor_reduce, xe[:, b:b + 1], xcmp[:], AX, ALU.add)
                do(v.tensor_scalar, xe[:], xe[:], float(E - 1), None, ALU.min)
                do(v.tensor_copy, xe[:, XB:XB + 1], xend[0:1, E - 1:E])
                v.tensor_copy(xexp[:], xe[:])
                v.wait_ge(list_loaded, 16)
                v.tensor_copy(lst_f[:], lst_i[:])
                v.drain().then_inc(list_f, 1)
                v.wait_ge(list_turned, 1)
                do(v.tensor_copy, sf[:], acc[3][:, 0:E + XB])
                do(v.tensor_scalar, gf[:], sf[:], float(T), -float(T), ALU.is_ge, ALU.mult)
                do(v.tensor_tensor, gf[:], gf[:], sf[:], ALU.add)
                v.tensor_copy(gidx[:, 0:E + XB], gf[:])
                v.tensor_copy(sidx[:, 0:E + XB], sf[:])


@stage
def stage_experts(k, w_gate, w_up, w_down, h2_rows, y_rows, gidx, sidx, xexp):
    nc = k.nc
    HT = EH // P
    with ExitStack() as ctx:
        dbl = lambda n, s, dt=F32: [k.sb(f"ex_{n}{i}", s, dt, ctx) for i in range(2)]
        WG, WU, WD = dbl("WG", [P, KD, EH]), dbl("WU", [P, KD, EH]), dbl("WD", [P, HT, D])
        X, XT, Y = dbl("X", [P, D]), dbl("XT", [P, KD, P]), dbl("Y", [P, D])
        gi, si = dbl("gi", [P, 1], U32), dbl("si", [P, 1], U32)
        sg, hid, hT = k.sb("ex_sg", [P, EH], F32, ctx), k.sb("ex_hid", [P, EH], F32, ctx), k.sb("ex_hT", [P, HT, P], F32, ctx)
        xt_ps, g_ps, u_ps, h_ps, y_ps = k.banks(ctx, 2, "ex_xtp"), k.banks(ctx, 1, "ex_gp")[0], k.banks(ctx, 1, "ex_up")[0], k.banks(ctx, 1, "ex_hp")[0], k.banks(ctx, 2, "ex_yp")
        sem = lambda n: k.sem("ex_" + n)
        g_loaded, u_loaded, d_loaded = ([sem(f"{n}_loaded{i}") for i in range(2)] for n in "gud")
        gathered, scattered = ([sem(f"{n}{i}") for i in range(2)] for n in ("gathered", "scattered"))
        g_used, u_used, d_used, x_turned = (sem(n) for n in ("g_used", "u_used", "d_used", "x_turned"))
        xt_taken, silu_done, hid_ready, h_turned, ht_taken, y_ready, y_taken_v, y_taken_a = (sem(n) for n in (
            "xt_taken", "silu_done", "hid_ready", "h_turned", "ht_taken", "y_ready", "y_taken_v", "y_taken_a"))
        g_ready, u_ready, gi_ready, si_ready = (sem(n) for n in ("g_ready", "u_ready", "gi_ready", "si_ready"))
        gather_due, scatter_due = sem("gather_due"), sem("scatter_due")

        def has_before(n):
            return not isinstance(n, int) or n >= 2

        def units(pair):
            return ((pair * 2 + 1, 1, pair), (pair * 2 + 2, 0, pair + 1))

        def load(sp, n, b, e, used, dst, w, loaded):
            sp.wait_ge(used, n + 1)
            sp.dma_start(dst[b][:].rearrange("p (a k) n -> p a k n", a=1), w[ds(e, 1)].rearrange("a (p k) n -> p a k n", p=P)).then_inc(loaded[b], 16)

        def load_in(sp, unit, e):
            n, b, rnd = unit
            load(sp, n, b, e, g_used, WG, w_gate, g_loaded)
            load(sp, n, b, e, u_used, WU, w_up, u_loaded)

        def load_down(sp, unit, e):
            n, b, rnd = unit
            load(sp, n, b, e, d_used, WD, w_down, d_loaded)

        def gather(g, n, b, rnd):
            g.wait_ge(x_turned, n + 1)
            if has_before(n):
                g.wait_ge(gathered[b], rnd * 16)
            g.tensor_copy(gi[b][:], gidx[:, ds(n, 1)]).then_inc(gi_ready, 1)
            g.wait_ge(gi_ready, n + 1)
            g.sem_inc(gather_due, 1)
            g.indirect_dma_start(X[b][:], None, h2_rows, bass.IndirectOffsetOnAxis(gi[b][:], 0), bounds_check=T - 1, oob_is_err=False).then_inc(gathered[b], 16)

        def scatter(g, n, b, rnd):
            if has_before(n):
                g.wait_ge(scattered[b], rnd * 16)
            g.tensor_copy(si[b][:], sidx[:, ds(n, 1)]).then_inc(si_ready, 1)
            g.wait_ge(si_ready, n + 1)
            g.wait_ge(y_taken_v, n + 2)
            g.wait_ge(y_taken_a, n + 2)
            g.sem_inc(scatter_due, 1)
            g.indirect_dma_start(y_rows, bass.IndirectOffsetOnAxis(si[b][:], 0), Y[b][:], None, bounds_check=NA - 1, oob_is_err=False).then_inc(scattered[b], 16)

        def turn_x(pe, n, b, rnd):
            pe.wait_ge(gathered[b], rnd * 16 + 16)
            pe.wait_ge(xt_taken, n + 1)
            for q in range(KD):
                ins = pe.transpose(xt_ps[q // 4][:, (q % 4) * P:(q % 4 + 1) * P], X[b][:, q::KD], k.c("ident"))
            ins.then_inc(x_turned, 1)

        def gate_up(pe, n, b, rnd):
            pe.wait_ge(xt_taken, n + 2)
            for loaded, free, ps, W, ready, used in ((g_loaded, silu_done, g_ps, WG, g_ready, g_used), (u_loaded, hid_ready, u_ps, WU, u_ready, u_used)):
                pe.wait_ge(loaded[b], rnd * 16 + 16)
                pe.wait_ge(free, n + 1)
                for q in range(KD):
                    ins = pe.matmul(ps[:], XT[b][:, q, :], W[b][:, q, :], start=(q == 0), stop=(q == KD - 1))
                ins.then_inc(ready, 1)
                pe.drain().then_inc(used, 1)

        def down(pe, n, b, rnd):
            pe.wait_ge(hid_ready, n + 2)
            pe.wait_ge(ht_taken, n + 1)
            for q in range(HT):
                ins = pe.transpose(h_ps[:, q * P:(q + 1) * P], hid[:, q::HT], k.c("ident"))
            ins.then_inc(h_turned, 1)
            pe.wait_ge(d_loaded[b], rnd * 16 + 16)
            pe.wait_ge(y_taken_v, n + 1)
            pe.wait_ge(y_taken_a, n + 1)
            pe.wait_ge(ht_taken, n + 2)
            for s in range(2):
                for q in range(HT):
                    ins = pe.matmul(y_ps[s][:], hT[:, q, :], WD[b][:, q, s * 512:(s + 1) * 512], start=(q == 0), stop=(q == HT - 1))
            ins.then_inc(y_ready, 1)
            pe.drain().then_inc(d_used, 1)

        def take_x(v, n, b, rnd):
            v.wait_ge(x_turned, n + 3)
            for s in range(2):
                ins = v.tensor_copy(XT[b][:, s * 4:s * 4 + 4, :], xt_ps[s][:].rearrange("p (q n) -> p q n", q=4))
            ins.then_inc(xt_taken, 1)

        def make_hid(v, n, b, rnd):
            v.wait_ge(u_ready, n + 1)
            v.wait_ge(silu_done, n + 2)
            v.wait_ge(h_turned, n + 1)
            v.tensor_tensor(hid[:], sg[:], u_ps[:], ALU.mult).then_inc(hid_ready, 1)

        def take_y(e, copy, s, taken, n, b, rnd):
            e.wait_ge(y_ready, n + 2)
            if has_before(n):
                e.wait_ge(scattered[b], rnd * 16)
            copy(Y[b][:, s * 512:(s + 1) * 512], y_ps[s][:]).then_inc(taken, 1)

        def silu(a, n, b, rnd):
            a.wait_ge(g_ready, n + 1)
            a.wait_ge(hid_ready, n + 1)
            a.activation(sg[:], g_ps[:], ACT.Silu).then_inc(silu_done, 1)

        def take_h(a, n, b, rnd):
            a.wait_ge(h_turned, n + 2)
            a.wait_ge(y_ready, n + 1)
            a.activation(hT[:].rearrange("p q n -> p (q n)"), h_ps[:], ACT.Copy).then_inc(ht_taken, 1)

        LAST = (E - 1, 1, (E - 1) // 2)

        def run(eng, first, steady, drain):
            def pair(j):
                one, two = units(j)
                steady(one, (j * 2, 0, j), two)
                steady(two, one, (j * 2 + 3, 1, j + 1))

            first((0, 0, 0), (1, 1, 0))
            pair(0)
            with eng.Fori(1, (E - 2) // 2) as j:
                pair(j)
            drain(LAST, (E - 2, 0, (E - 2) // 2))

        def further(eng, body):
            count = eng.value_load(xexp[0:1, XB:XB + 1], min_val=0, max_val=XB)
            with eng.Fori(0, (XB + 1) // 2) as j:
                for b in range(2):
                    with eng.If(j * 2 + b < count):
                        body((j * 2 + (E + b), b, j + E // 2), j * 2 + b)

        with nc.Block() as block:
            @block.sync
            def _(sp):
                def first(u, nxt):
                    load_in(sp, u, u[0])
                def steady(u, prev, nxt):
                    load_in(sp, u, u[0])
                    load_down(sp, prev, prev[0])
                def drain(u, prev):
                    load_in(sp, u, u[0])
                    load_down(sp, prev, prev[0])
                    load_down(sp, u, u[0])
                run(sp, first, steady, drain)

                def body(unit, nth):
                    e = sp.value_load(xexp[0:1, ds(nth, 1)], min_val=0, max_val=E - 1)
                    load_in(sp, unit, e)
                    load_down(sp, unit, e)
                further(sp, body)

            @block.gpsimd
            def _(g):
                g.memset(X[0][:], 0.0)
                g.memset(X[1][:], 0.0)
                g.drain()
                def first(u, nxt):
                    gather(g, *u)
                    gather(g, *nxt)
                def steady(u, prev, nxt):
                    gather(g, *nxt)
                    scatter(g, *prev)
                def drain(u, prev):
                    scatter(g, *prev)
                    scatter(g, *u)
                run(g, first, steady, drain)
                further(g, lambda unit, nth: (gather(g, *unit), scatter(g, *unit)))
                n_more = g.value_load(xexp[0:1, XB:XB + 1], min_val=0, max_val=XB)
                g.wait_ge(scattered[0], E // 2 * 16 + ((n_more + 1) // 2) * 16)
                g.wait_ge(scattered[1], E // 2 * 16 + (n_more // 2) * 16)

            @block.tensor
            def _(pe):
                for s in (g_used, u_used, d_used, x_turned):
                    pe.sem_inc(s, 2)
                for s in (h_turned, y_ready):
                    pe.sem_inc(s, 1)
                def first(u, nxt):
                    turn_x(pe, *u)
                    gate_up(pe, *u)
                    turn_x(pe, *nxt)
                def steady(u, prev, nxt):
                    gate_up(pe, *u)
                    turn_x(pe, *nxt)
                    down(pe, *prev)
                def drain(u, prev):
                    gate_up(pe, *u)
                    down(pe, *prev)
                    down(pe, *u)
                run(pe, first, steady, drain)
                further(pe, lambda unit, nth: (turn_x(pe, *unit), gate_up(pe, *unit), down(pe, *unit)))

            @block.vector
            def _(v):
                for s in (xt_taken, hid_ready, y_taken_v):
                    v.sem_inc(s, 1)
                take = lambda u: take_y(v, lambda o, i: v.tensor_copy(o, i), 0, y_taken_v, *u)
                def first(u, nxt):
                    take_x(v, *u)
                    make_hid(v, *u)
                    take_x(v, *nxt)
                def steady(u, prev, nxt):
                    make_hid(v, *u)
                    take_x(v, *nxt)
                    take(prev)
                def drain(u, prev):
                    make_hid(v, *u)
                    take(prev)
                    take(u)
                run(v, first, steady, drain)
                further(v, lambda unit, nth: (take_x(v, *unit), make_hid(v, *unit), take(unit)))

            @block.scalar
            def _(a):
                for s in (silu_done, ht_taken, y_taken_a):
                    a.sem_inc(s, 1)
                take = lambda u: take_y(a, lambda o, i: a.activation(o, i, ACT.Copy), 1, y_taken_a, *u)
                def first(u, nxt):
                    silu(a, *u)
                def steady(u, prev, nxt):
                    silu(a, *u)
                    take_h(a, *prev)
                    take(prev)
                def drain(u, prev):
                    silu(a, *u)
                    take_h(a, *prev)
                    take(prev)
                    take_h(a, *u)
                    take(u)
                run(a, first, steady, drain)
                further(a, lambda unit, nth: (silu(a, *unit), take_h(a, *unit), take(unit)))


@stage
def stage_combine(k, y_rows, weights):
    nc = k.nc
    with ExitStack() as ctx:
        Y = k.sb("cb_Y", [P, 2 * NT, D], F32, ctx)
        loaded = k.sem("cb_loaded")
        with nc.Block() as block:
            @block.sync
            def _(sp):
                sp.dma_start(Y[:], y_rows.rearrange("(a p) d -> p a d", p=P)).then_inc(loaded, 16)

            @block.vector
            def _(v):
                v.wait_ge(loaded, 16)
                for c in range(2):
                    for t in range(NT):
                        v.scalar_tensor_tensor(k.x[:, t, :], Y[:, c * NT + t, :], weights[:, c, t:t + 1], k.x[:, t, :], ALU.mult, ALU.add)
                    v.drain()


RW = 256
RW_IN = 3 * RW + 128
CH = 64
MH = 8
MQ, MKV = 384, 256
DFF = 2816


def col(v):
    return v.rearrange("(a p) -> p a", p=P)


@stage
def stage_features(k, l, w_in, mu, rkv, rqk, krT, cos32, sin32):
    nc = k.nc
    with ExitStack() as ctx:
        W = [k.sb(f"ft{l}_W{i}", [P, KD, 512], F32, ctx) for i in range(2)]
        WK = k.sb(f"ft{l}_WK", [P, KD, 32], F32, ctx)
        mus = k.sb(f"ft{l}_mu", [P, 7], F32, ctx)
        u = [k.sb(f"ft{l}_u{i}", [P, T + 1], F32, ctx) for i in range(2)]
        d = k.sb(f"ft{l}_d", [P, T], F32, ctx)
        e = k.sb(f"ft{l}_e", [P, T], F32, ctx)
        acc = k.banks(ctx, 4, f"ft{l}_acc")
        half = k.banks(ctx, 2, f"ft{l}_half")
        small_loaded, slab_used, acc_ready, u_ready, half_ready, out_ready, pad_zero = (k.sem(f"ft{l}_" + n) for n in (
            "small_loaded", "slab_used", "acc_ready", "u_ready", "half_ready", "out_ready", "pad_zero"))
        w_loaded = [k.sem(f"ft{l}_w_loaded{i}") for i in range(2)]
        slabs = [(0, 512), (512, 512), (1024, 384)]
        KROPE = 1920 + MQ + MKV
        rows = lambda m: slice(0, P) if m < 11 else slice(64, 96)
        with nc.Block() as block:
            @block.sync
            def _(sp):
                with nc.allow_non_contiguous_dma("columns"):
                    sp.dma_start(mus[:], col(mu)).then_inc(small_loaded, 16)
                sp.dma_start(WK[:], w_in[:, KROPE:KROPE + 32].rearrange("(k p) n -> p k n", p=P)).then_inc(small_loaded, 16)
                for n, (lo, w) in enumerate(slabs):
                    if n >= 2:
                        sp.wait_ge(slab_used, n - 1)
                    sp.dma_start(W[n % 2][:, :, 0:w], w_in[:, lo:lo + w].rearrange("(k p) n -> p k n", p=P)).then_inc(w_loaded[n % 2], 16)

            @block.tensor
            def _(pe):
                def turn(m):
                    if m < 7:
                        return
                    pe.wait_ge(u_ready, m + 1)
                    if m >= 9:
                        pe.wait_ge(out_ready, m - 1)
                    r = rows(m)
                    turner = k.c("turn64") if m < 11 else k.c("turn32")[r, 64:96]
                    pe.matmul(half[m % 2][r, :], turner, u[m % 2][r, 1:], start=True, stop=True).then_inc(half_ready, 1)

                for m in range(12):
                    if m % 4 == 0 and m < 12:
                        pe.wait_ge(w_loaded[(m // 4) % 2], 16 * (m // 8 + 1))
                    if m == 11:
                        pe.wait_ge(small_loaded, 32)
                    if m >= 4:
                        pe.wait_ge(u_ready, m - 3)
                    for n in range(KD):
                        w = W[(m // 4) % 2][:, n, (m % 4) * P:(m % 4 + 1) * P] if m < 11 else WK[:, n, :]
                        ins = pe.matmul(acc[m % 4][rows(m), :], w, k.hT[:, n, :], start=(n == 0), stop=(n == KD - 1))
                    ins.then_inc(acc_ready, 1)
                    if m % 4 == 3:
                        pe.drain().then_inc(slab_used, 1)
                    if m >= 1:
                        turn(m - 1)
                turn(11)

            @block.scalar
            def _(a):
                a.wait_ge(pad_zero, 1)
                for m in range(12):
                    a.wait_ge(acc_ready, m + 1)
                    if m >= 2:
                        a.wait_ge(out_ready, m - 1)
                    a.activation(u[m % 2][rows(m), 1:], acc[m % 4][rows(m), :], ACT.Copy).then_inc(u_ready, 1)

            @block.vector
            def _(v):
                v.memset(u[0][:, 0:1], 0.0)
                v.memset(u[1][:, 0:1], 0.0)
                v.drain().then_inc(pad_zero, 1)
                v.wait_ge(small_loaded, 32)
                for m in range(12):
                    v.wait_ge(u_ready, m + 1)
                    uu, r = u[m % 2], rows(m)
                    v.drain()
                    if m < 7:
                        v.tensor_tensor(d[:], uu[:, 0:T], uu[:, 1:], ALU.subtract)
                        v.drain()
                        v.scalar_tensor_tensor(rkv[:, m, :], d[:], mus[:, m:m + 1], uu[:, 1:], ALU.mult, ALU.add).then_inc(out_ready, 1)
                    else:
                        cos, sin = (k.cos, k.sin) if m < 11 else (cos32, sin32)
                        out = rqk[:, m - 7, :] if m < 11 else krT[r, :]
                        v.tensor_tensor(d[r, :], uu[r, 1:], cos[r, :], ALU.mult)
                        v.wait_ge(half_ready, m - 6)
                        v.tensor_tensor(e[r, :], half[m % 2][r, :], sin[r, :], ALU.mult)
                        v.drain()
                        v.tensor_tensor(out, d[r, :], e[r, :], ALU.add).then_inc(out_ready, 1)


@stage
def stage_tokens(k, l, w_in, vg, lat, ssl):
    nc = k.nc
    base = RW_IN + 2 * RW
    slabs = [(base, 512), (base + 512, MQ), (base + 512 + MQ, MKV)]
    with ExitStack() as ctx:
        W = [k.sb(f"tk{l}_W{i}", [P, KD, w], F32, ctx) for i, (_, w) in enumerate(slabs)]
        sq = k.sb(f"tk{l}_sq", [P, MQ], F32, ctx)
        acc = k.banks(ctx, 4, f"tk{l}_acc")
        w_loaded = [k.sem(f"tk{l}_w_loaded{i}") for i in range(3)]
        acc_ready, taken = k.sem(f"tk{l}_acc_ready"), k.sem(f"tk{l}_taken")
        with nc.Block() as block:
            @block.sync
            def _(sp):
                for n, (lo, w) in enumerate(slabs):
                    sp.dma_start(W[n][:], w_in[:, lo:lo + w].rearrange("(k p) n -> p k n", p=P)).then_inc(w_loaded[n], 16)

            @block.tensor
            def _(pe):
                for n, (lo, w) in enumerate(slabs):
                    pe.wait_ge(w_loaded[n], 16)
                    for t in range(NT):
                        if n > 0:
                            pe.wait_ge(taken, n * 4 + t - 3)
                        for q in range(KD):
                            ins = pe.matmul(acc[t][:, 0:w], k.hT[:, q, t * P:(t + 1) * P], W[n][:, q, :], start=(q == 0), stop=(q == KD - 1))
                        ins.then_inc(acc_ready, 1)

            @block.scalar
            def _(a):
                for n, (lo, w) in enumerate(slabs):
                    for t in range(NT):
                        a.wait_ge(acc_ready, n * 4 + t + 1)
                        if n == 0:
                            a.activation(vg[:, t, 0:RW], acc[t][:, 0:RW], ACT.Copy)
                            a.activation(vg[:, t, RW:], acc[t][:, RW:], ACT.Silu).then_inc(taken, 1)
                        else:
                            off = 0 if n == 1 else MQ
                            a.activation(lat[:, t, off:off + w], acc[t][:, 0:w], ACT.Copy)
                            a.activation(sq[:, 0:w], acc[t][:, 0:w], ACT.Square, accum_out=ssl[:, t, n - 1:n])
                            a.drain().then_inc(taken, 1)


@stage
def stage_latents(k, l, lat, ssl, q_norm, kv_norm, latT):
    nc = k.nc
    with ExitStack() as ctx:
        wcol = k.sb(f"la{l}_wcol", [P, 5], F32, ctx)
        tp = k.banks(ctx, 5, f"la{l}_tp")
        w_loaded, mean_ready, root_ready, y_ready, turned = (k.sem(f"la{l}_" + n) for n in ("w_loaded", "mean", "root", "y_ready", "turned"))
        with nc.Block() as block:
            @block.sync
            def _(sp):
                with nc.allow_non_contiguous_dma("columns"):
                    sp.dma_start(wcol[:, 0:3], col(q_norm)).then_inc(w_loaded, 16)
                    sp.dma_start(wcol[:, 3:5], col(kv_norm)).then_inc(w_loaded, 16)

            @block.vector
            def _(v):
                v.tensor_scalar(ssl[:, :, 0:1], ssl[:, :, 0:1], 1.0 / MQ, 1e-6, ALU.mult, ALU.add)
                v.tensor_scalar(ssl[:, :, 1:2], ssl[:, :, 1:2], 1.0 / MKV, 1e-6, ALU.mult, ALU.add)
                v.drain().then_inc(mean_ready, 1)
                v.wait_ge(root_ready, 1)
                v.reciprocal(ssl[:], ssl[:])
                v.drain()
                for t in range(NT):
                    v.tensor_scalar(lat[:, t, 0:MQ], lat[:, t, 0:MQ], ssl[:, t, 0:1], None, ALU.mult)
                    v.tensor_scalar(lat[:, t, MQ:], lat[:, t, MQ:], ssl[:, t, 1:2], None, ALU.mult)
                    v.drain().then_inc(y_ready, 1)

            @block.tensor
            def _(pe):
                pe.wait_ge(y_ready, NT)
                for n in range(5):
                    for t in range(NT):
                        ins = pe.transpose(tp[n][:, t * P:(t + 1) * P], lat[:, t, n * P:(n + 1) * P], k.c("ident"))
                    ins.then_inc(turned, 1)

            @block.scalar
            def _(a):
                a.wait_ge(mean_ready, 1)
                a.activation(ssl[:], ssl[:], ACT.Sqrt).then_inc(root_ready, 1)
                a.wait_ge(w_loaded, 32)
                for n in range(5):
                    a.wait_ge(turned, n + 1)
                    a.activation(latT[:, n, :], tp[n][:], ACT.Copy, scale=wcol[:, n:n + 1])


@stage
def stage_retention(k, l, rqk, vg, mix):
    nc = k.nc
    with ExitStack() as ctx:
        kd = k.sb(f"re{l}_kd", [P, 2, T], F32, ctx)
        qd = k.sb(f"re{l}_qd", [P, 2, T], F32, ctx)
        kt = k.sb(f"re{l}_kt", [P, NT, RW], F32, ctx)
        inn = [k.sb(f"re{l}_in{i}", [P, 4, P], F32, ctx) for i in range(2)]
        R = k.sb(f"re{l}_R", [P, NT, 2, 64], F32, ctx)
        y = k.sb(f"re{l}_y", [P, NT, 4, 64], F32, ctx)
        yc = k.sb(f"re{l}_yc", [P, NT, 4, 64], F32, ctx)
        ss = k.sb(f"re{l}_ss", [P, NT, 4], F32, ctx)
        bk = k.banks(ctx, 8, f"re{l}_bk")
        tp, kv = bk[0:2], bk[2]
        yi, yx, sc = bk[0:2], bk[2:4], (bk[4:6], bk[6:8])
        (dec_ready, turned, kt_ready, kv_ready, R_ready, sc_ready, inn_ready, y_ready, y_taken, mean_ready, root_ready) = (k.sem(f"re{l}_" + n) for n in (
            "dec_ready", "turned", "kt_ready", "kv_ready", "R_ready", "sc_ready", "inn_ready", "y_ready", "y_taken", "mean", "root"))
        lane = lambda h: slice(64 * (h % 2), 64 * (h % 2) + 64)
        with nc.Block() as block:
            @block.vector
            def _(v):
                ch = lambda ap: ap.rearrange("p (c n) -> p c n", n=P)
                over = lambda ap: ap.rearrange("p (a n) -> p a n", a=1).broadcast_to([P, NT, P])
                for b in range(2):
                    v.tensor_tensor(ch(kd[:, b, :]), ch(rqk[:, 2 + b, :]), over(k.c(f"ret_k{b}")), ALU.mult)
                    v.tensor_tensor(ch(qd[:, b, :]), ch(rqk[:, b, :]), over(k.c(f"ret_q{b}")), ALU.mult)
                v.memset(R[:, 0], 0.0)
                v.drain().then_inc(dec_ready, 1)
                for t in range(NT):
                    v.wait_ge(turned, t + 1)
                    v.tensor_copy(kt[:, t, :], tp[t % 2][:, 0:RW]).then_inc(kt_ready, 1)
                v.wait_ge(kv_ready, 1)
                for t in range(NT - 1):
                    v.drain()
                    for b in range(2):
                        v.scalar_tensor_tensor(R[:, t + 1, b, :], R[:, t, b, :], k.c("ret_state", b, b + 1), kv[:, (t * 2 + b) * 64:(t * 2 + b) * 64 + 64],
                                               ALU.mult, ALU.add)
                v.drain().then_inc(R_ready, 1)

                def take_y(t):
                    v.wait_ge(y_ready, t + 1)
                    v.tensor_copy(y[:, t].rearrange("p h e -> p (h e)"), yi[t % 2][:, 0:RW])
                    v.drain()
                    for side in range(2):
                        v.tensor_tensor(y[:, t, side::2, :], y[:, t, side::2, :], yx[side][:, 0:P].rearrange("p (h n) -> p h n", h=2), ALU.add)
                    v.drain().then_inc(y_taken, 1)

                for t in range(NT):
                    v.wait_ge(sc_ready, t + 1)
                    if t >= 2:
                        v.wait_ge(y_ready, t - 1)
                    for side in range(2):
                        ins = v.tensor_tensor(inn[t % 2][:, side::2, :], sc[t % 2][side][:, 0:2 * P].rearrange("p (h n) -> p h n", h=2),
                                              k.c("ret_decay").rearrange("p (h n) -> p h n", h=4)[:, side::2, :], ALU.mult)
                    ins.then_inc(inn_ready, 1)
                    if t >= 1:
                        take_y(t - 1)
                take_y(NT - 1)
                v.drain()
                fl = lambda t: t[:].rearrange("p c h e -> p (c h) e")
                v.tensor_tensor(yc[:], y[:], y[:], ALU.mult)
                v.drain()
                v.tensor_reduce(ss[:].rearrange("p c h -> p (c h)"), fl(yc), AX, ALU.add)
                v.drain()
                v.tensor_scalar(ss[:], ss[:], 1.0 / 64, 1e-6, ALU.mult, ALU.add).then_inc(mean_ready, 1)
                v.wait_ge(root_ready, 1)
                v.reciprocal(ss[:], ss[:])
                v.drain()
                v.tensor_tensor(fl(y), fl(y), ss[:].rearrange("p c h -> p (c h)").rearrange("p (n a) -> p n a", a=1).broadcast_to([P, 16, 64]), ALU.mult)
                v.drain()
                v.tensor_tensor(mix[:, :, RW:2 * RW], y[:].rearrange("p c h e -> p c (h e)"), vg[:, :, RW:], ALU.mult)

            @block.scalar
            def _(a):
                a.wait_ge(mean_ready, 1)
                a.activation(ss[:], ss[:], ACT.Sqrt).then_inc(root_ready, 1)

            @block.tensor
            def _(pe):
                pe.wait_ge(dec_ready, 1)
                for t in range(NT):
                    if t >= 2:
                        pe.wait_ge(kt_ready, t - 1)
                    for b in range(2):
                        ins = pe.transpose(tp[t % 2][:, b * P:(b + 1) * P], kd[:, b, t * P:(t + 1) * P], k.c("ident"))
                    ins.then_inc(turned, 1)
                pe.wait_ge(kt_ready, NT)
                for t in range(NT - 1):
                    for h in range(4):
                        o = (t * 2 + h // 2) * 64
                        ins = pe.matmul(kv[lane(h), o:o + 64], kt[:, t, h * 64:h * 64 + 64], vg[:, t, h * 64:h * 64 + 64], start=True, stop=True)
                ins.then_inc(kv_ready, 1)

                def scores(t):
                    if t >= 2:
                        pe.wait_ge(inn_ready, t - 1)
                    for h in range(4):
                        s = slice(t * P, (t + 1) * P)
                        ins = pe.matmul(sc[t % 2][h % 2][:, (h // 2) * P:(h // 2 + 1) * P], rqk[lane(h), 2 + h // 2, s], rqk[lane(h), h // 2, s], start=True, stop=True)
                    ins.then_inc(sc_ready, 1)

                scores(0)
                pe.wait_ge(R_ready, 1)
                for t in range(NT):
                    if t < NT - 1:
                        scores(t + 1)
                    pe.wait_ge(inn_ready, t + 1)
                    if t >= 1:
                        pe.wait_ge(y_taken, t)
                    for h in range(4):
                        pe.matmul(yi[t % 2][:, h * 64:h * 64 + 64], inn[t % 2][:, h, :], vg[:, t, h * 64:h * 64 + 64], start=True, stop=True)
                    for h in range(4):
                        ins = pe.matmul(yx[h % 2][:, (h // 2) * 64:(h // 2) * 64 + 64], qd[lane(h), h // 2, t * P:(t + 1) * P], R[lane(h), t, h // 2, :],
                                        start=True, stop=True)
                    pe.drain().then_inc(y_ready, 1)


@stage
def stage_mla_up(k, l, latT, krT, w_q_up, w_kv_up, cos32, sin32, QT, KT, v_tok):
    nc = k.nc
    R = slice(64, 96)
    with ExitStack() as ctx:
        WQ, WKV = k.sb(f"mu{l}_WQ", [P, 3, MH * 96], F32, ctx), k.sb(f"mu{l}_WKV", [P, 2, MH * P], F32, ctx)
        d = [k.sb(f"mu{l}_d{i}", [P, T], F32, ctx) for i in range(2)]
        qa, ka, half, va = k.banks(ctx, 2, f"mu{l}_qa"), k.banks(ctx, 2, f"mu{l}_ka"), k.banks(ctx, 2, f"mu{l}_half"), k.banks(ctx, 2, f"mu{l}_va")
        loaded, q_ready, k_ready, q_taken, k_taken, half_ready, rope_done, v_ready, v_taken = (k.sem(f"mu{l}_" + n) for n in (
            "loaded", "q_ready", "k_ready", "q_taken", "k_taken", "half_ready", "rope_done", "v_ready", "v_taken"))
        with nc.Block() as block:
            @block.sync
            def _(sp):
                sp.dma_start(WQ[:], w_q_up.rearrange("(k p) n -> p k n", p=P)).then_inc(loaded, 16)
                sp.dma_start(WKV[:], w_kv_up.rearrange("(k p) n -> p k n", p=P)).then_inc(loaded, 16)

            @block.tensor
            def _(pe):
                pe.wait_ge(loaded, 32)

                def turn(h):
                    pe.wait_ge(q_taken, h + 1)
                    if h >= 2:
                        pe.wait_ge(rope_done, h - 1)
                    pe.matmul(half[h % 2][R, :], k.c("turn32")[R, R], QT[R, h, :], start=True, stop=True).then_inc(half_ready, 1)

                for h in range(MH):
                    if h >= 2:
                        pe.wait_ge(q_taken, h - 1)
                        pe.wait_ge(k_taken, h - 1)
                    for n in range(3):
                        ins = pe.matmul(qa[h % 2][0:96, :], WQ[:, n, h * 96:h * 96 + 96], latT[:, n, :], start=(n == 0), stop=(n == 2))
                    ins.then_inc(q_ready, 1)
                    for n in range(2):
                        ins = pe.matmul(ka[h % 2][0:64, :], WKV[:, n, h * P:h * P + 64], latT[:, 3 + n, :], start=(n == 0), stop=(n == 1))
                    ins.then_inc(k_ready, 1)
                    if h >= 1:
                        turn(h - 1)
                turn(MH - 1)
                for t in range(NT):
                    if t >= 2:
                        pe.wait_ge(v_taken, t - 1)
                    for n in range(2):
                        ins = pe.matmul(va[t % 2][:], latT[:, 3 + n, t * P:(t + 1) * P], WKV[:, n, :].rearrange("p (h c) -> p h c", h=MH)[:, :, 64:],
                                        start=(n == 0), stop=(n == 1))
                    ins.then_inc(v_ready, 1)

            @block.scalar
            def _(a):
                for h in range(MH):
                    a.wait_ge(q_ready, h + 1)
                    a.activation(QT[0:96, h, :], qa[h % 2][0:96, :], ACT.Copy).then_inc(q_taken, 1)
                    a.wait_ge(k_ready, h + 1)
                    a.activation(KT[0:64, h, :], ka[h % 2][0:64, :], ACT.Copy).then_inc(k_taken, 1)
                    a.activation(KT[R, h, :], krT[R, :], ACT.Copy)
                for t in range(NT):
                    a.wait_ge(v_ready, t + 1)
                    a.activation(v_tok[:, t, :], va[t % 2][:], ACT.Copy).then_inc(v_taken, 1)

            @block.vector
            def _(v):
                for h in range(MH):
                    v.wait_ge(half_ready, h + 1)
                    v.drain()
                    v.tensor_tensor(QT[R, h, :], QT[R, h, :], cos32[R, :], ALU.mult)
                    v.tensor_tensor(d[h % 2][R, :], half[h % 2][R, :], sin32[R, :], ALU.mult)
                    v.drain()
                    v.tensor_tensor(QT[R, h, :], QT[R, h, :], d[h % 2][R, :], ALU.add).then_inc(rope_done, 1)


@stage
def stage_mla_attention(k, l, QT, KT, v_tok, mix):
    nc = k.nc
    scale = 96 ** -0.5
    with ExitStack() as ctx:
        two = lambda n, s: [k.sb(f"ml{l}_{n}{i}", s, F32, ctx) for i in range(2)]
        Q, K, S, mx, sm, rs, WT = two("q", [96, T]), two("k", [96, T]), two("s", [P, T]), two("mx", [P, 1]), two("sm", [P, 1]), two("rs", [P, 1]), two("wt", [P, T])
        sc, tp, ob = k.banks(ctx, 2, f"ml{l}_sc"), k.banks(ctx, 2, f"ml{l}_tp"), k.banks(ctx, 2, f"ml{l}_ob")
        staged, heads_used, scores_done, masked, bias_ready, exp_done, turned, wt_ready, sum_ready, out_done, out_taken = (k.sem(f"ml{l}_" + n) for n in (
            "staged", "heads_used", "scores", "masked", "bias", "exp", "turned", "wt_ready", "sum_ready", "out_done", "out_taken"))
        with nc.Block() as block:
            @block.gpsimd
            def _(g):
                with g.Fori(0, MH // 2) as i:
                    for b in range(2):
                        g.wait_ge(heads_used, i * 2 + b + 1)
                        for dst, src in ((Q, QT), (K, KT)):
                            g.tensor_copy(dst[b][:].rearrange("p (a n) -> p a n", a=1), src[0:96, ds(i * 2 + b, 1), :])
                        g.drain().then_inc(staged, 1)

            @block.tensor
            def _(pe):
                for s in (heads_used, turned, out_done):
                    pe.sem_inc(s, 2)
                with pe.Fori(0, MH // 2) as i:
                    def scores(s):
                        b, t, u = s // 4, s % 4, i * 8 + s
                        if t == 0:
                            pe.wait_ge(staged, i * 2 + b + 1)
                        pe.wait_ge(masked, u + 1)
                        pe.matmul(sc[t % 2][:, 0:(t + 1) * P], Q[b][:, t * P:(t + 1) * P], K[b][:, 0:(t + 1) * P], start=True, stop=True).then_inc(scores_done, 1)
                        if t == NT - 1:
                            pe.drain().then_inc(heads_used, 1)

                    scores(0)
                    for s in range(8):
                        b, t, u = s // 4, s % 4, i * 8 + s
                        if s < 7:
                            scores(s + 1)
                        pe.wait_ge(exp_done, u + 1)
                        pe.wait_ge(wt_ready, u + 1)
                        for j in range(t + 1):
                            ins = pe.transpose(tp[t % 2][:, j * P:(j + 1) * P], S[t % 2][:, j * P:(j + 1) * P], k.c("ident"))
                        ins.then_inc(turned, 1)
                        pe.wait_ge(wt_ready, u + 3)
                        pe.wait_ge(out_taken, u + 1)
                        for j in range(t + 1):
                            ins = pe.matmul(ob[t % 2][:, 0:64], WT[t % 2][:, j * P:(j + 1) * P], v_tok[:, j, ds(i * 128 + b * 64, 64)], start=(j == 0), stop=(j == t))
                        ins.then_inc(out_done, 1)

            @block.vector
            def _(v):
                v.sem_inc(masked, 2)
                with v.Fori(0, MH // 2) as i:
                    def mask_and_max(s):
                        t, par, u = s % 4, s % 2, i * 8 + s
                        n = (t + 1) * P
                        v.wait_ge(scores_done, u + 1)
                        v.wait_ge(turned, u + 1)
                        v.tensor_tensor(S[par][:, 0:n], sc[par][:, 0:n], k.c("neg_wide", 512 - n), ALU.add).then_inc(masked, 1)
                        v.drain()
                        v.tensor_reduce(mx[par][:], S[par][:, 0:n], AX, ALU.max)
                        v.drain()
                        v.tensor_scalar(mx[par][:], mx[par][:], -scale, None, ALU.mult).then_inc(bias_ready, 1)

                    mask_and_max(0)
                    for s in range(8):
                        if s < 7:
                            mask_and_max(s + 1)
                        par, u = s % 2, i * 8 + s
                        v.wait_ge(exp_done, u + 1)
                        v.wait_ge(out_taken, u + 1)
                        v.reciprocal(rs[par][:], sm[par][:]).then_inc(sum_ready, 1)

            @block.scalar
            def _(a):
                a.sem_inc(wt_ready, 2)
                a.sem_inc(out_taken, 2)
                with a.Fori(0, MH // 2) as i:
                    def exps(s):
                        par, u, n = s % 2, i * 8 + s, (s % 4 + 1) * P
                        a.wait_ge(bias_ready, u + 1)
                        a.activation(S[par][:, 0:n], S[par][:, 0:n], ACT.Exp, bias=mx[par][:], scale=scale, accum_out=sm[par][:])
                        a.drain().then_inc(exp_done, 1)

                    def take_out(s):
                        par, u, t = s % 2, i * 8 + s, s % 4
                        a.wait_ge(out_done, u + 3)
                        a.wait_ge(sum_ready, u + 1)
                        a.activation(mix[:, t, ds(i * 128 + (2 * RW + (s // 4) * 64), 64)], ob[par][:, 0:64], ACT.Copy, scale=rs[par][:]).then_inc(out_taken, 1)

                    exps(0)
                    for s in range(8):
                        par, u, n = s % 2, i * 8 + s, (s % 4 + 1) * P
                        if s < 7:
                            if s >= 1:
                                a.wait_ge(sum_ready, u)
                            exps(s + 1)
                        a.wait_ge(turned, u + 3)
                        a.wait_ge(out_done, u + 1)
                        a.activation(WT[par][:, 0:n], tp[par][:, 0:n], ACT.Copy).then_inc(wt_ready, 1)
                        if s >= 1:
                            take_out(s - 1)
                    take_out(7)


@stage
def stage_ffn_up(k, l, w_gate_up, fT):
    nc = k.nc
    CW = 256
    with ExitStack() as ctx:
        W = [k.sb(f"ff{l}_W{i}", [P, 2, KD, CW], F32, ctx) for i in range(2)]
        sg = [k.sb(f"ff{l}_sg{i}", [P, T], F32, ctx) for i in range(2)]
        acc = [k.banks(ctx, 2, f"ff{l}_acc{n}_") for n in range(2)]
        w_loaded = [k.sem(f"ff{l}_w_loaded{i}") for i in range(2)]
        slab_used, g_ready, u_ready, sg_ready, out_taken = (k.sem(f"ff{l}_" + n) for n in ("slab_used", "g_ready", "u_ready", "sg_ready", "out_taken"))
        SL = DFF // CW

        def all_slabs(eng, body):
            with eng.Fori(0, SL // 2) as i:
                for b in range(2):
                    body(i * 2 + b, b, i)
            body(SL - 1, 0, SL // 2)

        with nc.Block() as block:
            @block.sync
            def _(sp):
                def body(s, b, rnd):
                    sp.wait_ge(slab_used, s + 1)
                    for n in range(2):
                        sp.dma_start(W[b][:, n], w_gate_up[:, ds(s * CW + n * DFF, CW)].rearrange("(k p) n -> p k n", p=P)).then_inc(w_loaded[b], 16)
                all_slabs(sp, body)

            @block.tensor
            def _(pe):
                pe.sem_inc(slab_used, 2)
                def body(s, b, rnd):
                    pe.wait_ge(w_loaded[b], rnd * 32 + 32)
                    for m in range(2):
                        u = s * 2 + m
                        for free, n, ready in ((sg_ready, 0, g_ready), (out_taken, 1, u_ready)):
                            pe.wait_ge(free, u + 1)
                            for q in range(KD):
                                ins = pe.matmul(acc[n][m][:], W[b][:, n, q, m * P:(m + 1) * P], k.hT[:, q, :], start=(q == 0), stop=(q == KD - 1))
                            ins.then_inc(ready, 1)
                    pe.drain().then_inc(slab_used, 1)
                all_slabs(pe, body)

            @block.scalar
            def _(a):
                a.sem_inc(sg_ready, 2)
                def body(s, b, rnd):
                    for m in range(2):
                        u = s * 2 + m
                        a.wait_ge(g_ready, u + 1)
                        a.wait_ge(out_taken, u + 1)
                        a.activation(sg[m][:], acc[0][m][:], ACT.Silu).then_inc(sg_ready, 1)
                all_slabs(a, body)

            @block.vector
            def _(v):
                v.sem_inc(out_taken, 2)
                def body(s, b, rnd):
                    for m in range(2):
                        u = s * 2 + m
                        v.wait_ge(u_ready, u + 1)
                        v.wait_ge(sg_ready, u + 3)
                        one = lambda ap: ap.rearrange("p (a n) -> p a n", a=1)
                        v.tensor_tensor(fT[:, ds(u, 1), :], one(sg[m][:]), one(acc[1][m][:]), ALU.mult).then_inc(out_taken, 1)
                all_slabs(v, body)


@stage
def stage_rwkv_prep(k, rkv, w, v_first, out, eb, vt, gt, bonus, layer):
    nc = k.nc
    A_, R_, B_, K_ = out
    Be, Ke, pc = eb
    with ExitStack() as ctx:
        names = ["w0", "a0", "k_k", "k_a", "r_k"] + (["v0"] if layer else [])
        cols = k.sb(f"rp{layer}_cols", [P, 7, 2], F32, ctx)
        wl = k.sb(f"rp{layer}_wl", [P, RW], F32, ctx)
        big = lambda n: k.sb(f"rp{layer}_" + n, [P, 2, T], F32, ctx)
        sgw, av, kk, t1, cum, e1 = (big(n) for n in ("sgw", "av", "kk", "t1", "cum", "e1"))
        if layer:
            v1, v2, low = k.sb(f"rp{layer}_v1", [P, 2, 32], F32, ctx), k.sb(f"rp{layer}_v2", [32, RW], F32, ctx), k.sb(f"rp{layer}_low", [32, T], F32, ctx)
        bk = k.banks(ctx, 8, f"rp{layer}_bk")
        (loaded, low_ready, wa_ready, sig_ready, v1_ready, low_v_ready, v2_ready, vsig_ready, v_done, sq_ready, norm_ready, root_in, root_ready,
         cum_ready, exp_ready, exp_used, tok_in, tok_ready, rk_in) = (k.sem(f"rp{layer}_" + n) for n in (
             "loaded", "low_ready", "wa_ready", "sig_ready", "v1_ready", "low_v_ready", "v2_ready", "vsig_ready", "v_done", "sq_ready", "norm_ready",
             "root_in", "root_ready", "cum_ready", "exp_ready", "exp_used", "tok_in", "tok_ready", "rk_in"))
        n_loads = len(names) + 3 + (2 if layer else 0)
        r, kx, vx, lowrank = rkv[:, 0:2, :], rkv[:, 2:4, :], rkv[:, 4:6, :], rkv[:, 6, :]
        chunks = lambda ap: ap.rearrange("p b (c n) -> p (b c) n", n=CH)
        with nc.Block() as block:
            @block.sync
            def _(sp):
                with nc.allow_non_contiguous_dma("columns"):
                    for n, name in enumerate(names):
                        sp.dma_start(cols[:, n, :], col(w[name])).then_inc(loaded, 16)
                sp.dma_start(wl[0:32, :], w["w2"]).then_inc(loaded, 16)
                sp.dma_start(wl[32:64, :], w["a2"]).then_inc(loaded, 16)
                sp.dma_start(wl[64:128, :], w["g2"]).then_inc(loaded, 16)
                if layer:
                    sp.dma_start(v1[:], w["v1"].rearrange("(k p) n -> p k n", p=P)).then_inc(loaded, 16)
                    sp.dma_start(v2[:], w["v2"]).then_inc(loaded, 16)

            @block.tensor
            def _(pe):
                pe.wait_ge(loaded, 16 * n_loads)
                pe.wait_ge(low_ready, 1)
                for b in range(2):
                    pe.matmul(bk[b][:], wl[0:32, b * P:(b + 1) * P], rkv[0:32, 6, :], start=True, stop=True)
                    ins = pe.matmul(bk[2 + b][:], wl[32:64, b * P:(b + 1) * P], rkv[32:64, 6, :], start=True, stop=True)
                ins.then_inc(wa_ready, 1)
                for t in range(NT):
                    ins = pe.matmul(bk[4 + t // 2][:, (t % 2) * RW:(t % 2) * RW + RW], rkv[64:128, 6, t * P:(t + 1) * P], wl[64:128, :], start=True, stop=True)
                ins.then_inc(wa_ready, 1)
                if layer:
                    for b in range(2):
                        ins = pe.matmul(bk[6][0:32, :], v1[:, b, :], rkv[:, 4 + b, :], start=(b == 0), stop=(b == 1))
                    ins.then_inc(v1_ready, 1)
                    pe.wait_ge(low_v_ready, 1)
                    pe.wait_ge(sig_ready, 1)
                    for b in range(2):
                        ins = pe.matmul(bk[b][:], v2[:, b * P:(b + 1) * P], low[:], start=True, stop=True)
                    ins.then_inc(v2_ready, 1)
                pe.wait_ge(sq_ready, 1)
                pe.wait_ge(sig_ready, 1)
                for b in range(2):
                    ins = pe.matmul(bk[2 + b][:], k.c("same_head"), t1[:, b, :], start=True, stop=True)
                ins.then_inc(norm_ready, 1)
                pe.wait_ge(v_done, 1)
                pe.wait_ge(tok_in, 1)
                for t in range(NT):
                    for b in range(2):
                        ins = pe.transpose(bk[4 + t // 2][:, (t % 2) * RW + b * P:(t % 2) * RW + (b + 1) * P], rkv[:, 4 + b, t * P:(t + 1) * P], k.c("ident"))
                ins.then_inc(tok_ready, 1)
                pe.wait_ge(rk_in, 1)
                for t in range(NT):
                    for b in range(2):
                        ins = pe.matmul(bk[7][:, t * 4 + 2 * b:t * 4 + 2 * b + 2], t1[:, b, t * P:(t + 1) * P], k.c("same_head")[:, 0:P:64], start=True, stop=True)
                ins.then_inc(tok_ready, 1)

            @block.scalar
            def _(a):
                a.activation(rkv[0:32, 6, :], rkv[0:32, 6, :], ACT.Tanh)
                a.activation(rkv[64:128, 6, :], rkv[64:128, 6, :], ACT.Sigmoid)
                a.drain().then_inc(low_ready, 1)
                a.wait_ge(loaded, 16 * n_loads)
                a.wait_ge(wa_ready, 1)
                for b in range(2):
                    a.activation(sgw[:, b, :], bk[b][:], ACT.Sigmoid, bias=cols[:, 0, b:b + 1])
                    a.activation(av[:, b, :], bk[2 + b][:], ACT.Sigmoid, bias=cols[:, 1, b:b + 1])
                a.drain().then_inc(sig_ready, 1)
                if layer:
                    a.wait_ge(v1_ready, 1)
                    a.activation(low[:], bk[6][0:32, :], ACT.Copy).then_inc(low_v_ready, 1)
                    a.wait_ge(v2_ready, 1)
                    for b in range(2):
                        ins = a.activation(e1[:, b, :], bk[b][:], ACT.Sigmoid, bias=cols[:, 5, b:b + 1])
                    a.drain().then_inc(vsig_ready, 1)
                a.wait_ge(root_in, 1)
                a.activation(kk[:], kk[:], ACT.Sqrt).then_inc(root_ready, 1)
                for n in range(4):
                    a.wait_ge(cum_ready, n + 1)
                    if n:
                        a.wait_ge(exp_used, n)
                    a.activation(e1[:], t1[:] if n >= 2 else cum[:], ACT.Exp, scale=-1.0 if n == 1 else 1.0).then_inc(exp_ready, 1)

            @block.vector
            def _(v):
                def do(f, *args, **kw):
                    ins = f(*args, **kw)
                    v.drain()
                    return ins

                c = lambda n, b: cols[:, n, b:b + 1]
                v.wait_ge(loaded, 16 * n_loads)
                for b in range(2):
                    v.tensor_scalar(kk[:, b, :], rkv[:, 2 + b, :], c(2, b), None, ALU.mult)
                v.drain()
                do(v.tensor_tensor, t1[:], kk[:], kk[:], ALU.mult).then_inc(sq_ready, 1)
                v.wait_ge(wa_ready, 2)
                for h in range(2):
                    v.tensor_copy(gt[:, 2 * h:2 * h + 2, :].rearrange("p t n -> p (t n)"), bk[4 + h][:])
                v.drain().then_inc(tok_in, 1)
                v.wait_ge(sig_ready, 1)
                do(v.tensor_scalar, sgw[:], sgw[:], -float(np.exp(-0.5)), None, ALU.mult)
                for b in range(2):
                    v.tensor_tensor_scan(cum[:, b, :], k.c("rw_keep"), sgw[:, b, :], 0.0, ALU.mult, ALU.add)
                v.drain()
                if layer:
                    v.wait_ge(vsig_ready, 1)
                    v.wait_ge(norm_ready, 1)
                    do(v.tensor_tensor, t1[:], v_first[:], vx, ALU.subtract)
                    do(v.tensor_tensor, t1[:], t1[:], e1[:], ALU.mult)
                    do(v.tensor_tensor, vx, vx, t1[:], ALU.add)
                else:
                    do(v.tensor_copy, v_first[:], vx)
                v.drain().then_inc(v_done, 1)
                v.drain().then_inc(cum_ready, 1)
                v.wait_ge(norm_ready, 1)
                for b in range(2):
                    v.tensor_copy(t1[:, b, :], kk[:, b, :])
                    v.drain()
                    v.tensor_scalar(kk[:, b, :], bk[2 + b][:], 1e-24, None, ALU.max)
                v.drain().then_inc(root_in, 1)
                v.wait_ge(root_ready, 1)
                do(v.reciprocal, kk[:], kk[:])
                do(v.tensor_tensor, kk[:], kk[:], t1[:], ALU.mult)
                for b in range(2):
                    v.tensor_scalar(t1[:, b, :], av[:, b, :], -1.0, c(3, b), ALU.add, ALU.mult)
                v.drain()
                do(v.scalar_tensor_tensor, kx, t1[:], 1.0, kx, ALU.add, ALU.mult)
                do(v.tensor_tensor, av[:], kk[:], av[:], ALU.mult)
                v.wait_ge(exp_ready, 1)
                v.tensor_tensor(R_[:], r, e1[:], ALU.mult)
                v.tensor_copy(pc[:], chunks(e1[:])[:, :, CH - 1])
                v.drain().then_inc(exp_used, 1)
                v.drain().then_inc(cum_ready, 1)
                v.wait_ge(exp_ready, 2)
                v.tensor_tensor(B_[:], av[:], e1[:], ALU.mult)
                v.tensor_tensor(K_[:], kx, e1[:], ALU.mult)
                do(v.tensor_tensor, t1[:], cum[:], sgw[:], ALU.subtract)
                v.drain().then_inc(exp_used, 1)
                v.drain().then_inc(cum_ready, 1)
                v.wait_ge(exp_ready, 3)
                v.tensor_tensor(A_[:], kk[:], e1[:], ALU.mult)
                v.drain().then_inc(exp_used, 1)
                do(v.tensor_tensor, chunks(t1[:]), chunks(cum[:])[:, :, CH - 1:CH].broadcast_to([P, 16, CH]), chunks(cum[:]), ALU.subtract)
                v.drain().then_inc(cum_ready, 1)
                v.wait_ge(exp_ready, 4)
                v.tensor_tensor(Be[:], av[:], e1[:], ALU.mult)
                v.tensor_tensor(Ke[:], kx, e1[:], ALU.mult)
                v.wait_ge(tok_ready, 1)
                for h in range(2):
                    v.tensor_copy(vt[:, 2 * h:2 * h + 2, :].rearrange("p t n -> p (t n)"), bk[4 + h][:])
                do(v.tensor_tensor, t1[:], r, kx, ALU.mult)
                for b in range(2):
                    v.tensor_scalar(t1[:, b, :], t1[:, b, :], c(4, b), None, ALU.mult)
                v.drain().then_inc(rk_in, 1)
                v.wait_ge(tok_ready, 2)
                v.tensor_copy(bonus[:], bk[7][:, 0:16])


@stage
def stage_rwkv_chunks(k, l, out, eb, vt, y, spent):
    nc = k.nc
    A_, R_, B_, K_ = out
    Be, Ke, pc = eb
    HH = 4
    W4 = HH * P
    with ExitStack() as ctx:
        grid = lambda n, w=P: k.sb(f"rc{l}_" + n, [P, NT, HH, w], F32, ctx)
        LT, MT = (k.hT[:, 4 * n:4 * n + 4, :].rearrange("p t (h n) -> p t h n", h=HH) for n in range(2))
        Ti, TT, RB, RK = (grid(n) for n in ("Ti", "TT", "RB", "RK"))
        tok = k.sb(f"rc{l}_tok", [P, NT, 3, RW], F32, ctx)
        AM, TW = grid("AM"), grid("TW")
        Lm = [k.sb(f"rc{l}_Lm{i}", [P, W4], F32, ctx) for i in range(2)]
        X = [k.sb(f"rc{l}_X{i}", [P, W4], F32, ctx) for i in range(2)]
        G = spent[:, 0:2, :]
        H, Z = (spent[:, 2 * n:2 * n + 2, :].rearrange("p b (c n) -> p b c n", c=8) for n in (1, 2))
        S = k.sb(f"rc{l}_S", [P, 8, 2, CH], F32, ctx)
        bk = k.banks(ctx, 8, f"rc{l}_bk")
        lane = lambda h: slice(64 * (h % 2), 64 * (h % 2) + 64)
        pair = lambda p: (2 * (p % 3), 2 * (p % 3) + 1)
        s_ = {n: k.sem(f"rc{l}_" + n) for n in ("prod", "masked", "turned", "tok_taken", "lm", "x_mm", "x_sb", "y_mm", "t_new", "mv", "am", "tw_mm", "tw",
                                               "gh_mm", "gh", "s_mm", "s_new", "yo_mm", "yo_taken", "zero")}
        with nc.Block() as block:
            @block.tensor
            def _(pe):
                pe.sem_inc(s_["y_mm"], 2)
                for t in range(NT):
                    sl = slice(t * P, (t + 1) * P)
                    for n, (lhs, rhs) in enumerate(((B_, A_), (A_, B_), (K_, A_), (B_, R_), (K_, R_))):
                        if 5 * t + n >= 3:
                            pe.wait_ge(s_["masked"], 5 * t + n - 2)
                        for h in range(HH):
                            o = bk[pair(5 * t + n)[h % 2]][:, (h // 2) * P:(h // 2 + 1) * P]
                            ins = pe.matmul(o, lhs[lane(h), h // 2, sl], rhs[lane(h), h // 2, sl], start=True, stop=True)
                        pe.drain().then_inc(s_["prod"], 1)
                    if t:
                        pe.wait_ge(s_["tok_taken"], 2 * t)
                    for n, src in enumerate((A_, Be, Ke)):
                        for b in range(2):
                            o = n * RW + b * P
                            ins = pe.transpose(bk[6 + o // 512][:, o % 512:o % 512 + P], src[:, b, sl], k.c("ident"))
                    ins.then_inc(s_["turned"], 1)
                pe.wait_ge(s_["masked"], 5 * NT)
                with pe.Fori(0, 5) as lv:
                    def second(t):
                        u = lv * 4 + t
                        pe.wait_ge(s_["x_sb"], u + 1)
                        pe.wait_ge(s_["t_new"], u + 1)
                        for h in range(HH):
                            hs = slice(h * P, (h + 1) * P)
                            pe.matmul(bk[2 + t % 2][:, hs], TT[:, t, h, :], X[t % 2][:, hs], start=True, stop=True)
                            ins = pe.matmul(bk[4 + t % 2][:, hs], X[t % 2][:, hs], TT[:, t, h, :], start=True, stop=True)
                        ins.then_inc(s_["y_mm"], 1)

                    for t in range(NT):
                        u = lv * 4 + t
                        pe.wait_ge(s_["lm"], u + 1)
                        pe.wait_ge(s_["t_new"], lv * 4 + 2)
                        for h in range(HH):
                            hs = slice(h * P, (h + 1) * P)
                            ins = pe.matmul(bk[t % 2][:, hs], Lm[t % 2][:, hs], Ti[:, t, h, :], start=True, stop=True)
                        ins.then_inc(s_["x_mm"], 1)
                        if t:
                            second(t - 1)
                    second(NT - 1)
                pe.wait_ge(s_["t_new"], 2 + 5 * NT)
                for t in range(NT):
                    if t >= 2:
                        pe.wait_ge(s_["am"], t - 1)
                    for h in range(HH):
                        ins = pe.matmul(bk[t % 2][:, h * 64:h * 64 + 64], MT[:, t, h, :], vt[:, t, h * 64:h * 64 + 64], start=True, stop=True)
                    ins.then_inc(s_["mv"], 1)
                for t in range(NT):
                    pe.wait_ge(s_["am"], t + 1)
                    if t >= 2:
                        pe.wait_ge(s_["tw"], t - 1)
                    for h in range(HH):
                        ins = pe.matmul(bk[2 + t % 2][:, h * P:(h + 1) * P], TT[:, t, h, :], AM[:, t, h, :], start=True, stop=True)
                    ins.then_inc(s_["tw_mm"], 1)
                for t in range(NT):
                    pe.wait_ge(s_["tw"], t + 1)
                    if t:
                        pe.wait_ge(s_["gh"], t)
                    for h in range(HH):
                        v_h = vt[:, t, h * 64:h * 64 + 64]
                        pe.matmul(bk[4][lane(h), (h // 2) * P:(h // 2 + 1) * P], TW[:, t, h, 0:64], RB[:, t, h, :], start=True, stop=True)
                        pe.matmul(bk[7][:, h * 64:h * 64 + 64], RK[:, t, h, :], v_h, start=True, stop=False)
                        pe.matmul(bk[7][:, h * 64:h * 64 + 64], RB[:, t, h, :], TW[:, t, h, 64:128], start=False, stop=True)
                    for h in range(HH):
                        for c in range(2):
                            rows = slice(64 * c, 64 * c + 64)
                            o = (h // 2) * 64
                            f = slice(h * 64, h * 64 + 64)
                            pe.matmul(bk[c][lane(h), o:o + 64], TW[rows, t, h, 0:64], tok[rows, t, 1, f], start=True, stop=True)
                            pe.matmul(bk[5 + c][lane(h), o:o + 64], tok[rows, t, 2, f], vt[rows, t, f], start=True, stop=False)
                            ins = pe.matmul(bk[5 + c][lane(h), o:o + 64], tok[rows, t, 1, f], TW[rows, t, h, 64:128], start=False, stop=True)
                    pe.drain().then_inc(s_["gh_mm"], 1)
                for c in range(7):
                    pe.wait_ge(s_["s_new"], c + 1)
                    for h in range(HH):
                        ins = pe.matmul(bk[c % 2][lane(h), (h // 2) * 64:(h // 2) * 64 + 64], H[lane(h), h // 2, c, :], S[lane(h), c, h // 2, :], start=True, stop=True)
                    pe.drain().then_inc(s_["s_mm"], 1)
                pe.wait_ge(s_["s_new"], 8)
                for t in range(NT):
                    if t >= 2:
                        pe.wait_ge(s_["yo_taken"], t - 1)
                    for h in range(HH):
                        for c in range(2):
                            ins = pe.matmul(bk[2 + 2 * (t % 2) + h % 2][64 * c:64 * c + 64, (h // 2) * 64:(h // 2) * 64 + 64], G[lane(h), h // 2, t * P + 64 * c:t * P + 64 * c + 64],
                                            S[lane(h), 2 * t + c, h // 2, :], start=True, stop=True)
                    pe.drain().then_inc(s_["yo_mm"], 1)

            @block.scalar
            def _(a):
                for t in range(NT):
                    a.wait_ge(s_["turned"], t + 1)
                    flat = tok[:, t].rearrange("p n f -> p (n f)")
                    a.activation(flat[:, 0:512], bk[6][:], ACT.Copy).then_inc(s_["tok_taken"], 1)
                    a.activation(flat[:, 512:768], bk[7][:, 0:RW], ACT.Copy).then_inc(s_["tok_taken"], 1)
                with a.Fori(0, 5) as lv:
                    for t in range(NT):
                        a.wait_ge(s_["x_mm"], lv * 4 + t + 1)
                        a.wait_ge(s_["y_mm"], lv * 4 + t + 1)
                        a.activation(X[t % 2][:], bk[t % 2][:], ACT.Copy).then_inc(s_["x_sb"], 1)
                for t in range(NT):
                    a.activation(AM[:, t, :, 0:64], tok[:, t, 0, :].rearrange("p (h n) -> p h n", h=HH), ACT.Copy)
                    a.wait_ge(s_["mv"], t + 1)
                    a.activation(AM[:, t, :, 64:128], bk[t % 2][:, 0:RW].rearrange("p (h n) -> p h n", h=HH), ACT.Copy)
                    a.drain().then_inc(s_["am"], 1)

            @block.vector
            def _(v):
                over = lambda name: k.c(name).rearrange("p (a n) -> p a n", a=1).broadcast_to([P, HH, P])
                v3 = lambda b: bk[b][:].rearrange("p (h n) -> p h n", h=HH)
                v.memset(S[:, 0], 0.0)
                v.drain()
                for t in range(NT):
                    for n, (dst, mask) in enumerate(((LT[:, t], "rw_before"), (Ti[:, t], "rw_level0_t"), (MT[:, t], "rw_before"), (RB[:, t], "rw_upto"), (RK[:, t], "rw_upto"))):
                        v.wait_ge(s_["prod"], 5 * t + n + 1)
                        for side in range(2):
                            ins = v.tensor_tensor(dst[:, side::2, :], bk[pair(5 * t + n)[side]][:, 0:2 * P].rearrange("p (h n) -> p h n", h=2),
                                                  over(mask)[:, 0:2, :], ALU.mult)
                        ins.then_inc(s_["masked"], 1)
                    v.drain()
                    v.tensor_tensor(Ti[:, t], over("ident"), Ti[:, t], ALU.subtract)
                    v.tensor_tensor(TT[:, t], LT[:, t], over("rw_level0"), ALU.mult)
                    v.drain()
                    v.tensor_tensor(TT[:, t], over("ident"), TT[:, t], ALU.subtract)
                v.drain()
                v.sem_inc(s_["t_new"], 2)
                at1 = WHERE["rw_level1"][0]
                with v.Fori(0, 5) as lv:
                    def mask(t):
                        v.wait_ge(s_["x_mm"], lv * 4 + max(t - 1, 0))
                        v.tensor_tensor(Lm[t % 2][:].rearrange("p (h n) -> p h n", h=HH), LT[:, t],
                                        k.consts[:, ds(lv * P + at1, P)].rearrange("p (a n) -> p a n", a=1).broadcast_to([P, HH, P]), ALU.mult).then_inc(s_["lm"], 1)

                    mask(0)
                    mask(1)
                    for t in range(NT):
                        if t + 2 < NT:
                            mask(t + 2)
                        v.wait_ge(s_["y_mm"], lv * 4 + t + 3)
                        v.tensor_tensor(Ti[:, t], Ti[:, t], v3(2 + t % 2), ALU.subtract)
                        v.tensor_tensor(TT[:, t], TT[:, t], v3(4 + t % 2), ALU.subtract)
                        v.drain().then_inc(s_["t_new"], 1)
                for t in range(NT):
                    v.wait_ge(s_["tw_mm"], t + 1)
                    v.tensor_copy(TW[:, t, :, 0:64], v3(2 + t % 2)[:, :, 0:64])
                    v.tensor_scalar(TW[:, t, :, 64:128], v3(2 + t % 2)[:, :, 64:128], -1.0, None, ALU.mult)
                    v.drain().then_inc(s_["tw"], 1)
                for t in range(NT):
                    v.wait_ge(s_["gh_mm"], t + 1)
                    sl = slice(t * P, (t + 1) * P)
                    v.tensor_tensor(G[:, :, sl], R_[:, :, sl], bk[4][:, 0:RW].rearrange("p (b n) -> p b n", b=2), ALU.subtract)
                    v.tensor_copy(y[:, t, :], bk[7][:, 0:RW])
                    half = lambda n: bk[n][:, 0:P].rearrange("p (b n) -> p b n", b=2)
                    for b in range(2):
                        for c in range(2):
                            for side in range(2):
                                r = slice(64 * side, 64 * side + 64)
                                v.scalar_tensor_tensor(H[r, b, 2 * t + c, :], k.c("ident")[r, r], pc[r, b * 8 + 2 * t + c:b * 8 + 2 * t + c + 1], half(c)[r, b, :], ALU.mult, ALU.subtract)
                    for c in range(2):
                        v.tensor_copy(Z[:, :, 2 * t + c, :], half(5 + c))
                    v.drain().then_inc(s_["gh"], 1)
                v.drain().then_inc(s_["s_new"], 1)
                for c in range(7):
                    v.wait_ge(s_["s_mm"], c + 1)
                    v.tensor_tensor(S[:, c + 1], bk[c % 2][:, 0:P].rearrange("p (b n) -> p b n", b=2), Z[:, :, c, :], ALU.add).then_inc(s_["s_new"], 1)
                for t in range(NT):
                    v.wait_ge(s_["yo_mm"], t + 1)
                    yh = y[:, t, :].rearrange("p (h n) -> p h n", h=HH)
                    for side in range(2):
                        ins = v.tensor_tensor(yh[:, side::2, :], yh[:, side::2, :], bk[2 + 2 * (t % 2) + side][:, 0:P].rearrange("p (h n) -> p h n", h=2), ALU.add)
                    ins.then_inc(s_["yo_taken"], 1)


@stage
def stage_rwkv_out(k, l, y, vt, gt, bonus, gn_w, gn_b, mix):
    nc = k.nc
    with ExitStack() as ctx:
        wb = k.sb(f"ro_{l}wb", [P, 2, RW], F32, ctx)
        sq = k.sb(f"ro_{l}sq", [P, NT, RW], F32, ctx)
        mean, var = k.sb(f"ro_{l}mean", [P, 16], F32, ctx), k.sb(f"ro_{l}var", [P, 16], F32, ctx)
        loaded, var_ready, root_ready = k.sem(f"ro_{l}loaded"), k.sem(f"ro_{l}var_ready"), k.sem(f"ro_{l}root")
        with nc.Block() as block:
            @block.sync
            def _(sp):
                sp.dma_start(wb[:, 0, :], row_bc(gn_w)).then_inc(loaded, 16)
                sp.dma_start(wb[:, 1, :], row_bc(gn_b)).then_inc(loaded, 16)

            @block.scalar
            def _(a):
                a.wait_ge(var_ready, 1)
                a.activation(var[:], var[:], ACT.Sqrt).then_inc(root_ready, 1)

            @block.vector
            def _(v):
                def do(f, *args, **kw):
                    ins = f(*args, **kw)
                    v.drain()
                    return ins

                hv = lambda t: t[:].rearrange("p t (h n) -> p (t h) n", n=64)
                bc = lambda t: t[:].rearrange("p (g a) -> p g a", a=1).broadcast_to([P, 16, 64])
                do(v.tensor_reduce, mean[:], hv(y), AX, ALU.add)
                do(v.tensor_scalar, mean[:], mean[:], 1.0 / 64, None, ALU.mult)
                do(v.tensor_tensor, hv(y), hv(y), bc(mean), ALU.subtract)
                do(v.tensor_tensor, sq[:], y[:], y[:], ALU.mult)
                do(v.tensor_reduce, var[:], hv(sq), AX, ALU.add)
                do(v.tensor_scalar, var[:], var[:], 1.0 / 64, 64e-5, ALU.mult, ALU.add).then_inc(var_ready, 1)
                do(v.tensor_tensor, hv(sq), hv(vt), bc(bonus), ALU.mult)
                v.wait_ge(root_ready, 1)
                do(v.reciprocal, var[:], var[:])
                do(v.tensor_tensor, hv(y), hv(y), bc(var), ALU.mult)
                v.wait_ge(loaded, 32)
                for n, op in ((0, ALU.mult), (1, ALU.add)):
                    do(v.tensor_tensor, y[:], y[:], wb[:, n:n + 1, :].broadcast_to([P, NT, RW]), op)
                do(v.tensor_tensor, y[:], y[:], sq[:], ALU.add)
                v.tensor_tensor(mix[:, :, 0:RW], y[:], gt[:], ALU.mult)


def second_layer(k, l, ap, cos32, sin32, v_first):
    g = lambda n: ap[n + "_2"][l]
    with ExitStack() as c0:
        mix = k.sb(f"mix{l}", [P, NT, D], F32, c0)
        stage_norm(k, f"na{l}", g("attn_norm"))
        rkv = k.sb(f"rkv{l}", [P, 7, T], F32, c0)
        with ExitStack() as c1:
            sb = lambda n, s: k.sb(f"{n}{l}", s, F32, c1)
            rqk, krT, vg, lat, ssl, latT = (sb("rqk", [P, 4, T]), sb("krT", [P, T]), sb("vg", [P, NT, 2 * RW]), sb("lat", [P, NT, MQ + MKV]),
                                            sb("ssl", [P, NT, 2]), sb("latT", [P, 5, T]))
            stage_features(k, l, g("w_in"), g("rw_mu"), rkv, rqk, krT, cos32, sin32)
            stage_tokens(k, l, g("w_in"), vg, lat, ssl)
            stage_latents(k, l, lat, ssl, g("mla_q_norm"), g("mla_kv_norm"), latT)
            stage_retention(k, l, rqk, vg, mix)
            QT, KT, v_tok = sb("QT", [P, MH, T]), sb("KT", [P, MH, T]), sb("mv_tok", [P, NT, 512])
            stage_mla_up(k, l, latT, krT, g("mla_w_q_up"), g("mla_w_kv_up"), cos32, sin32, QT, KT, v_tok)
            stage_mla_attention(k, l, QT, KT, v_tok, mix)
        with ExitStack() as c1:
            sb = lambda n, s: k.sb(f"rw_{n}{l}", s, F32, c1)
            out = tuple(sb(n, [P, 2, T]) for n in "ARBK")
            eb = (sb("Be", [P, 2, T]), sb("Ke", [P, 2, T]), sb("pc", [P, 16]))
            vt, gt, bonus, y = sb("vt", [P, NT, RW]), sb("gt", [P, NT, RW]), sb("bonus", [P, 16]), sb("y", [P, NT, RW])
            w = {n: g("rw_" + n) for n in ("w0", "w2", "a0", "a2", "g2", "k_k", "k_a")}
            w["r_k"] = g("rw_r_k").rearrange("h n -> (h n)")
            if l:
                w.update({n: ap[f"rw_{n}_2"][l - 1] for n in ("v0", "v1", "v2")})
            stage_rwkv_prep(k, rkv, w, v_first, out, eb, vt, gt, bonus, l)
            stage_rwkv_chunks(k, l, out, eb, vt, y, rkv)
            stage_rwkv_out(k, l, y, vt, gt, bonus, g("rw_gn_w"), g("rw_gn_b"), mix)
        mixT = k.sb(f"mixT{l}", [P, KD, T], F32, c0)
        stage_turn_back(k, l, mix, mixT)
        stage_residual(k, f"ro{l}", g("w_out"), mixT)
    stage_norm(k, f"nf{l}", g("ffn_norm"))
    with ExitStack() as c0:
        fT = k.sb(f"fT{l}", [P, DFF // P, T], F32, c0)
        stage_ffn_up(k, l, g("w_gate_up"), fT)
        stage_residual(k, f"fd{l}", g("w_down"), fT, DFF // P)


@stage
def stage_turn_back(k, l, src, dst):
    nc = k.nc
    with ExitStack() as ctx:
        tp = k.banks(ctx, KD, f"tb{l}_tp")
        turned = k.sem(f"tb{l}_turned")
        with nc.Block() as block:
            @block.tensor
            def _(pe):
                for n in range(KD):
                    for t in range(NT):
                        ins = pe.transpose(tp[n][:, t * P:(t + 1) * P], src[:, t, n * P:(n + 1) * P], k.c("ident"))
                    ins.then_inc(turned, 1)

            @block.scalar
            def _(a):
                for n in range(0, KD, 2):
                    a.wait_ge(turned, n + 1)
                    a.activation(dst[:, n, :], tp[n][:], ACT.Copy)

            @block.vector
            def _(v):
                for n in range(1, KD, 2):
                    v.wait_ge(turned, n + 1)
                    v.tensor_copy(dst[:, n, :], tp[n][:])


def first_block(k, ap):
    nc = k.nc
    w_in = ap["w_in"][0]
    stage_rope_tables(k, "r1", ap["positions"], "freq64", k.cos, k.sin)
    stage_norm(k, "n1", ap["norm_mix_w"][0])
    with ExitStack() as mix_ctx:
        attT = k.sb("attT", [P, KD, T], F32, mix_ctx)
        with ExitStack() as ctx:
            qkT, v_tok = k.sb("qkT", [P, 16, T], F32, ctx), k.sb("v_tok", [P, NT, D], F32, ctx)
            att, att_ss, lam = k.sb("att", [P, NT, D], F32, ctx), k.sb("att_ss", [P, NT, 8], F32, ctx), k.sb("lam", [P, 1], F32, ctx)
            stage_qk(k, "qk", w_in, qkT)
            stage_token_major(k, "v", w_in, 2048, 2, lambda a, ps, s, t: a.activation(v_tok[:, t, ds(s * 512, 512)], ps[:], ACT.Copy))
            stage_lambda(k, [ap[n] for n in ("lambda_q1", "lambda_k1", "lambda_q2", "lambda_k2")], lam, LAM_INIT)
            stage_diff_attention(k, qkT, v_tok, att, att_ss, lam)
            stage_scale_and_turn(k, "an", att, att_ss, 8, 128, 1e-5, ap["subln_w"][0], attT, gain=1.0 - LAM_INIT)
        xbcT = k.sb("xbcT", [P, 32, T], F32, mix_ctx)
        zs = xbcT[:, 0:16, :].rearrange("p (t a) n -> p t (a n)", t=NT)
        yT, mergedT = xbcT[:, 16:32, :], xbcT[:, 0:KD, :]
        stage_conv(k, w_in, ap["conv_w"][0], ap["conv_b"][0], xbcT)
        with ExitStack() as ctx:
            xs, ssd_ss = k.sb("xs", [P, NT, 2048], F32, ctx), k.sb("ssd_ss", [P, NT, 8], F32, ctx)
            steps = [k.sb("sd_" + n, [P, NT, 32], F32, ctx) for n in ("dt", "cum", "ecum", "wtail", "etot", "adt")]
            stage_ssd_steps(k, w_in, ap["dt_bias"][0], ap["a_log"][0], *steps)
            stage_turn(k, "tx", xbcT, 16, xs)
            stage_token_major(k, "z", w_in, Z0, 4, lambda a, ps, s, t: a.activation(zs[:, t, ds(s * 512, 512)], ps[:], ACT.Silu))
            with ExitStack() as scan_ctx:
                btok = k.sb("btok", [P, NT, 1024], F32, scan_ctx)
                stage_turn(k, "tb", xbcT[:, 16:24, :], 8, btok)
                stage_ssd(k, xbcT, xs, btok, zs, *steps, ap["d_skip"][0], ssd_ss)
            stage_scale_and_turn(k, "sn", xs, ssd_ss, 8, 256, 1e-5, ap["ssd_norm_w"][0], yT)
        stage_merge(k, w_in, ap["w_branch_attn"][0], ap["w_branch_ssd"][0], attT, yT, mergedT)
        stage_residual(k, "wo", ap["w_out"][0], mergedT)
    h2_rows = nc.dram_tensor("h2_rows", (T, D), F32, kind="Internal").ap()
    y_rows = nc.dram_tensor("y_rows", (NA, D), F32, kind="Internal").ap()
    slot_list = nc.dram_tensor("slot_list", (SLOTS, 1), I32, kind="Internal").ap()
    with ExitStack() as moe_ctx:
        gidx, sidx = (k.sb(n, [P, E + XB + 1], U32, moe_ctx) for n in ("gidx", "sidx"))
        xexp, weights = k.sb("xexp", [1, 8], I32, moe_ctx), k.sb("moe_w", [P, 2, NT], F32, moe_ctx)
        with ExitStack() as ctx:
            h2 = k.sb("h2", [P, NT, D], F32, ctx)
            stage_norm(k, "n2", ap["norm_ffn_w"][0], keep=h2)
            stage_route(k, ap["w_group_router"][0], ap["b_group_router"][0], ap["w_expert_router"][0], ap["b_expert_router"][0],
                        h2, h2_rows, slot_list, gidx, sidx, xexp, weights)
        stage_experts(k, ap["w_expert_gate"][0], ap["w_expert_up"][0], ap["w_expert_down"][0], h2_rows, y_rows, gidx, sidx, xexp)
        stage_combine(k, y_rows, weights)
    stage_norm(k, "nb", ap["final_norm_w"], keep=k.x, transposed=False)


def second_block(k, ap):
    with ExitStack() as ctx:
        cos32, sin32 = k.sb("cos32", [P, T], F32, ctx), k.sb("sin32", [P, T], F32, ctx)
        v_first = k.sb("v_first", [P, 2, T], F32, ctx)
        stage_rope_tables(k, "r2", ap["positions_2"], "freq64", k.cos, k.sin)
        stage_rope_tables(k, "r3", ap["positions_2"], "freq32", cos32, sin32)
        for l in range(2):
            second_layer(k, l, ap, cos32, sin32, v_first)
    stage_norm(k, "ne", ap["final_norm_2"], keep=k.x, transposed=False)


@stage
def stage_store(k, out):
    nc = k.nc
    stored = k.sem("result_stored")
    with nc.Block() as block:
        @block.sync
        def _(sp):
            sp.dma_start(out[0].rearrange("(t p) d -> p t d", p=P), k.x[:]).then_inc(stored, 16)
            sp.wait_ge(stored, 16)


def build(nc, ap, consts, out):
    with ExitStack() as ctx:
        k = Core(nc, ctx, consts)
        stage_load(k, ap["x"])
        first_block(k, ap)
        second_block(k, ap)
        stage_store(k, out)


def kernel(**inputs):
    import numpy as _np
    import concourse.bacc as _bacc
    from concourse import mybir as _mybir
    from concourse.bass_utils import run_bass_kernel_spmd as _run

    nc = _bacc.Bacc("TRN2", target_bir_lowering=False, num_devices=1)
    arrays, ap = {}, {}
    for name, value in inputs.items():
        a = _np.ascontiguousarray(value)
        arrays[f"in_{name}_dram"] = a
        ap[name] = nc.dram_tensor(f"in_{name}_dram", a.shape, _mybir.dt.from_np(a.dtype), kind="ExternalInput").ap()
    arrays["in_shape_constants_dram"] = shape_constants()[0]
    consts = nc.dram_tensor("in_shape_constants_dram", (P, CONST_COLS), F32, kind="ExternalInput").ap()
    out = nc.dram_tensor("out_0_dram", (1, T, D), F32, kind="ExternalOutput").ap()
    build(nc, ap, consts, out)
    r = _run(nc, [arrays], core_ids=[0])
    return r.results[0]["out_0_dram"]
```

```python
from contextlib import ExitStack

import numpy as np
import concourse.bass as bass
from concourse import mybir

F32 = mybir.dt.float32
I32 = mybir.dt.int32
U32 = mybir.dt.uint32
F32R = mybir.dt.float32r
ACT = mybir.ActivationFunctionType
ALU = mybir.AluOpType
AX = mybir.AxisListType.X
ds = bass.ds

P = 128
T = 512
NT = T // P
D = 1024
KD = D // P
PI = float(np.pi)
LAM_INIT = 0.8 - 0.6


def shape_constants():
    f = np.float32
    r, c = np.arange(P)[:, None], np.arange(P)[None, :]
    parts = {}
    parts["ident"] = (r == c)
    for name, hd in (("turn64", 64), ("turn32", 32)):
        half = hd // 2
        low = (c % hd) < half
        parts[name] = np.where(low & (r == c + half), -1.0, 0.0) + np.where(~low & (r == c - half), 1.0, 0.0)
    parts["neg_wide"] = np.concatenate([np.zeros((P, 384)), np.where(c > r, -1e30, 0.0)], 1)
    parts["upto"] = (r <= c)
    parts["before"] = (r < c)
    parts["neg_after"] = np.where(r > c, -1e30, 0.0)
    parts["ones"] = np.ones((P, P))
    parts["same_head"] = (r // 64 == c // 64)
    same = r // 64 == c // 64
    parts["rw_before"] = (r < c) & same
    parts["rw_upto"] = (r <= c) & same
    for lv in range(6):
        n = 1 << lv
        parts[f"rw_level{lv}"] = (r // (2 * n) == c // (2 * n)) & ((r // n) % 2 == 0) & ((c // n) % 2 == 1)
    parts["rw_level0_t"] = parts["rw_level0"].T
    lg = np.log(1.0 - 2.0 ** (-5.0 - np.arange(4, dtype=f))).astype(f)
    parts["ret_decay"] = np.concatenate([np.where(c >= r, np.exp(lg[h] * np.maximum(c - r, 0).astype(f)) * 0.125, 0.0) for h in range(4)], 1)
    head_of = np.arange(P) // 64
    for b in range(2):
        g = lg[2 * b + head_of][:, None]
        parts[f"ret_q{b}"] = np.exp(g * (c + 1.0))
        parts[f"ret_k{b}"] = np.exp(g * (P - 1.0 - c)) * 64 ** -0.5
    parts["ret_state"] = np.stack([np.exp(lg[2 * b + head_of] * 128) for b in range(2)], 1)
    p1 = np.arange(P)
    parts["freq64"] = (1.0 / (f(10000.0) ** ((2 * (p1 % 32)).astype(f) / f(64)))).astype(f)[:, None]
    parts["freq32"] = (1.0 / (f(10000.0) ** ((2 * (p1 % 16)).astype(f) / f(32)))).astype(f)[:, None]
    parts["rank"] = p1[:, None].astype(f)
    parts["expert_slot"] = np.broadcast_to(np.arange(64)[None, :] * 128.0, (P, 64))
    parts["rw_keep"] = np.broadcast_to((np.arange(T) % 64 != 0)[None, :], (P, T))
    at, where = 0, {}
    for k, v in parts.items():
        where[k] = (at, v.shape[1])
        at += v.shape[1]
    return np.concatenate([np.broadcast_to(v, (P, v.shape[1])).astype(f) for v in parts.values()], 1), where


CONST_COLS = shape_constants()[0].shape[1]
WHERE = shape_constants()[1]


class Core:

    def __init__(self, nc, ctx, consts):
        self.nc, self.ctx = nc, ctx
        self.const_dram = consts
        self.sems = []
        self.consts = self.sb("consts", [P, CONST_COLS])
        self.x = self.sb("x_res", [P, NT, D])
        self.h_hi = self.h_lo = None
        self.cos = self.sb("cos_t", [P, T])
        self.sin = self.sb("sin_t", [P, T])

    def sb(self, name, shape, dt=F32, ctx=None):
        return (ctx or self.ctx).enter_context(self.nc.sbuf_tensor(name, shape, dt))

    def pair(self, name, tiles, ctx):
        return [self.sb(f"{name}_{part}", [P, tiles, T], F32R, ctx) for part in ("hi", "lo")]

    def make_room_for_h(self, tag, ctx):
        self.h_hi, self.h_lo = self.pair(f"h_{tag}", KD, ctx)

    def banks(self, ctx, n, tag):
        return [ctx.enter_context(self.nc.psum_tensor(f"{tag}{i}", [P, 512], F32)) for i in range(n)]

    def sem(self, name):
        self.sems.append(self.nc.alloc_semaphore(name=name))
        return self.sems[-1]

    def end_stage(self):
        if self.sems:
            self.nc.clear_and_free_semaphores(self.sems)
            self.nc.all_engine_barrier()
            self.sems = []

    def c(self, name, lo=0, hi=None):
        at, n = WHERE[name]
        return self.consts[:, at + lo:at + (n if hi is None else hi)]


class Weights:

    def __init__(self, k, ctx, tag, tiles, cols, n_raw=2):
        self.n_raw = n_raw
        self.raw = [k.sb(f"{tag}_raw{i}", [P, tiles, cols], F32, ctx) for i in range(n_raw)]
        self.hi = [k.sb(f"{tag}_hi{i}", [P, tiles, cols], F32R, ctx) for i in range(2)]
        self.lo = [k.sb(f"{tag}_lo{i}", [P, tiles, cols], F32R, ctx) for i in range(2)]
        self.loaded = [k.sem(f"{tag}_w_loaded{i}") for i in range(n_raw)]
        self.split_ready, self.used, self.load_due = k.sem(f"{tag}_split_ready"), k.sem(f"{tag}_w_used"), k.sem(f"{tag}_load_due")

    def load(self, sp, n, b, src, tiles=None, cols=None):
        sp.wait_ge(self.split_ready, n + 1)
        sp.sem_inc(self.load_due, 1)
        dst = self.raw[b % self.n_raw][:, 0:tiles, 0:cols]
        sp.dma_start(dst, src.rearrange("(k p) n -> p k n", p=P)).then_inc(self.loaded[b % self.n_raw], 16)

    def start_splits(self, v):
        v.sem_inc(self.split_ready, self.n_raw)

    def split(self, v, n, b, rnd, tiles=None, cols=None):
        v.wait_ge(self.loaded[b % self.n_raw], (rnd if self.n_raw == 2 else n) * 16 + 16)
        v.wait_ge(self.used, n + 1)
        at = (slice(None), slice(0, tiles), slice(0, cols))
        split(v, self.hi[b][at], self.lo[b][at], self.raw[b % self.n_raw][at]).then_inc(self.split_ready, 1)

    def start_uses(self, pe):
        pe.sem_inc(self.used, 2)

    def wait(self, pe, n):
        pe.wait_ge(self.split_ready, n + 1 + self.n_raw)

    def done(self, pe):
        pe.drain().then_inc(self.used, 1)

    def tile(self, b, q, cols=slice(None)):
        return self.hi[b][:, q, cols], self.lo[b][:, q, cols]


def both(x, *at):
    return x[0][(slice(None), *at)], x[1][(slice(None), *at)]


def pipeline(eng, steps, width, before, step, after):
    before()
    for n in range(width):
        step(0, n, True, False)
    with eng.Fori(1, steps - 1) as i:
        for n in range(width):
            step(i, n, False, False)
    for n in range(width):
        step(steps - 1, n, False, True)
    after(steps - 1)


def stage(build):
    def built(k, *args, **kw):
        build(k, *args, **kw)
        k.end_stage()
    return built


def split(v, hi, lo, x):
    v.tensor_copy(hi, x)
    v.drain()
    return v.tensor_tensor(lo, x, hi.bitcast(F32), ALU.subtract)


def mm3(pe, out, a, b, first, last):
    pe.matmul(out, a[0], b[0], start=first, stop=False)
    pe.matmul(out, a[0], b[1], start=False, stop=False)
    return pe.matmul(out, a[1], b[0], start=False, stop=last)


def row_bc(v, n=P):
    return v.rearrange("(a n) -> a n", a=1).broadcast_to([n, v.shape[0]])


@stage
def stage_load(k, x):
    nc = k.nc
    loaded = k.sem("start_loaded")
    with nc.Block() as block:
        @block.sync
        def _(sp):
            sp.dma_start(k.consts[:], k.const_dram).then_inc(loaded, 16)
            sp.dma_start(k.x[:], x[0].rearrange("(t p) d -> p t d", p=P)).then_inc(loaded, 16)
            sp.wait_ge(loaded, 32)


@stage
def stage_rope_tables(k, tag, positions, freq, cos_out, sin_out):
    nc = k.nc
    with ExitStack() as ctx:
        pos_i = k.sb(f"{tag}_pos_i", [P, T], I32, ctx)
        pos_f = k.sb(f"{tag}_pos_f", [P, T], F32, ctx)
        turns = k.sb(f"{tag}_turns", [P, T], F32, ctx)
        ang = k.sb(f"{tag}_ang", [P, 2, T], F32, ctx)
        pos_loaded = k.sem(f"{tag}_pos_loaded")
        ang_ready = k.sem(f"{tag}_ang_ready")
        two_pi = 2 * np.pi
        c1 = 6.28125
        c2 = float(np.float32(np.round((two_pi - c1) * 2 ** 20) / 2 ** 20))
        c3 = two_pi - c1 - c2
        big = 12582912.0
        with nc.Block() as block:
            @block.sync
            def _(sp):
                sp.dma_start(pos_i[:], row_bc(positions[0])).then_inc(pos_loaded, 16)

            @block.vector
            def _(v):
                v.wait_ge(pos_loaded, 16)
                v.tensor_copy(pos_f[:], pos_i[:])
                v.drain()
                v.tensor_scalar(pos_f[:], pos_f[:], k.c(freq), None, ALU.mult)
                v.drain()
                for n, quarter in ((0, 0.25), (1, 0.0)):
                    v.tensor_scalar(turns[:], pos_f[:], 1.0 / two_pi, quarter, ALU.mult, ALU.add)
                    v.drain()
                    v.tensor_scalar(turns[:], turns[:], big, -big, ALU.add, ALU.add)
                    v.drain()
                    v.scalar_tensor_tensor(ang[:, n, :], turns[:], -c1, pos_f[:], ALU.mult, ALU.add)
                    for c in (c2, c3):
                        v.drain()
                        v.scalar_tensor_tensor(ang[:, n, :], turns[:], -c, ang[:, n, :], ALU.mult, ALU.add)
                    v.drain()
                    if n == 0:
                        v.tensor_scalar(ang[:, n, :], ang[:, n, :], PI / 2, None, ALU.add)
                        v.drain()
                    v.tensor_scalar(ang[:, n, :], ang[:, n, :], 3.1415925, -3.1415925, ALU.min, ALU.max).then_inc(ang_ready, 1)

            @block.scalar
            def _(a):
                a.wait_ge(ang_ready, 1)
                a.activation(cos_out[:], ang[:, 0, :], ACT.Sin)
                a.wait_ge(ang_ready, 2)
                a.activation(sin_out[:], ang[:, 1, :], ACT.Sin)


@stage
def stage_norm(k, tag, weight, keep=None, transposed=True, eps=1e-6):
    nc = k.nc
    with ExitStack() as ctx:
        wbc = k.sb(f"{tag}_w", [P, D], F32, ctx)
        h = keep if keep is not None else k.sb(f"{tag}_h", [P, NT, D], F32, ctx)
        sq = k.sb(f"{tag}_sq", [P, D], F32, ctx)
        ss = k.sb(f"{tag}_ss", [P, NT], F32, ctx)
        tp = k.banks(ctx, 4, f"{tag}_tp")
        w_loaded, ss_ready, mean_ready = k.sem(f"{tag}_w_loaded"), k.sem(f"{tag}_ss_ready"), k.sem(f"{tag}_mean")
        root_ready, h_ready = k.sem(f"{tag}_root"), k.sem(f"{tag}_h_ready")
        turned, hi_ready, taken = k.sem(f"{tag}_turned"), k.sem(f"{tag}_hi_ready"), k.sem(f"{tag}_taken")
        part = lambda x, g: x[:, (g % 2) * 4:(g % 2) * 4 + 4, (g // 2) * P:(g // 2 + 1) * P]
        tiles = lambda bank: bank[:].rearrange("p (q n) -> p q n", q=4)
        with nc.Block() as block:
            @block.sync
            def _(sp):
                sp.dma_start(wbc[:], row_bc(weight)).then_inc(w_loaded, 16)

            @block.scalar
            def _(a):
                for t in range(NT):
                    a.activation(sq[:], k.x[:, t, :], ACT.Square, accum_out=ss[:, t:t + 1])
                    a.drain()
                a.drain().then_inc(ss_ready, 1)
                a.wait_ge(mean_ready, 1)
                a.activation(ss[:], ss[:], ACT.Sqrt).then_inc(root_ready, 1)
                if transposed:
                    for g in range(2 * NT):
                        a.wait_ge(turned, g + 1)
                        a.activation(part(k.h_hi, g), tiles(tp[g % 4]), ACT.Copy).then_inc(hi_ready, 1)

            @block.vector
            def _(v):
                v.wait_ge(ss_ready, 1)
                v.tensor_scalar(ss[:], ss[:], 1.0 / D, eps, ALU.mult, ALU.add).then_inc(mean_ready, 1)
                v.wait_ge(root_ready, 1)
                v.reciprocal(ss[:], ss[:])
                v.drain()
                v.wait_ge(w_loaded, 16)
                for t in range(NT):
                    v.scalar_tensor_tensor(h[:, t, :], k.x[:, t, :], ss[:, t:t + 1], wbc[:], ALU.mult, ALU.mult).then_inc(h_ready, 1)
                if transposed:
                    for g in range(2 * NT):
                        v.wait_ge(hi_ready, g + 1)
                        v.tensor_tensor(part(k.h_lo, g), tiles(tp[g % 4]), part(k.h_hi, g).bitcast(F32), ALU.subtract).then_inc(taken, 1)

            if transposed:
                @block.tensor
                def _(pe):
                    for g in range(2 * NT):
                        t = g // 2
                        pe.wait_ge(h_ready, t + 1)
                        if g >= 4:
                            pe.wait_ge(taken, g - 3)
                        for q in range(4):
                            f = (g % 2) * 4 + q
                            ins = pe.transpose(tp[g % 4][:, q * P:(q + 1) * P], h[:, t, f * P:(f + 1) * P], k.c("ident"))
                        ins.then_inc(turned, 1)


@stage
def stage_qk(k, tag, w_in, qkT):
    nc = k.nc
    BLOCKS = 16
    with ExitStack() as ctx:
        W = Weights(k, ctx, tag, KD, P)
        plain = [k.sb(f"{tag}_plain{i}", [P, T], F32, ctx) for i in range(2)]
        straight = [k.sb(f"{tag}_straight{i}", [P, T], F32, ctx) for i in range(2)]
        turn = [k.sb(f"{tag}_turn{i}", [P, T], F32, ctx) for i in range(2)]
        acc = k.banks(ctx, 2, f"{tag}_acc")
        half = k.banks(ctx, 2, f"{tag}_half")
        acc_ready, plain_ready, half_ready, out_ready = (k.sem(f"{tag}_{n}") for n in ("acc_ready", "plain_ready", "half_ready", "out_ready"))
        h = (k.h_hi, k.h_lo)
        with nc.Block() as block:
            @block.sync
            def _(sp):
                with sp.Fori(0, BLOCKS // 2) as i:
                    for b in range(2):
                        W.load(sp, i * 2 + b, b, w_in[:, ds(i * (2 * P) + b * P, P)])

            @block.tensor
            def _(pe):
                W.start_uses(pe)

                def products(u, b):
                    W.wait(pe, u)
                    pe.wait_ge(plain_ready, u + 1)
                    for n in range(KD):
                        ins = mm3(pe, acc[b][:], W.tile(b, n), both(h, n), n == 0, n == KD - 1)
                    ins.then_inc(acc_ready, 1)
                    W.done(pe)

                def half_turn(u, b):
                    pe.wait_ge(plain_ready, u + 3)
                    pe.wait_ge(out_ready, u + 1)
                    pe.matmul(half[b][:], k.c("turn64"), plain[b][:], start=True, stop=True).then_inc(half_ready, 1)

                products(0, 0)
                products(1, 1)
                half_turn(0, 0)
                with pe.Fori(1, BLOCKS // 2) as i:
                    products(i * 2, 0)
                    half_turn(i * 2 - 1, 1)
                    products(i * 2 + 1, 1)
                    half_turn(i * 2, 0)
                half_turn(BLOCKS - 1, 1)

            @block.scalar
            def _(a):
                a.sem_inc(plain_ready, 2)
                with a.Fori(0, BLOCKS // 2) as i:
                    for b in range(2):
                        u = i * 2 + b
                        a.wait_ge(acc_ready, u + 1)
                        a.wait_ge(out_ready, u + 1)
                        a.activation(plain[b][:], acc[b][:], ACT.Copy).then_inc(plain_ready, 1)

            @block.vector
            def _(v):
                v.sem_inc(out_ready, 2)
                W.start_splits(v)

                def outputs(u, b):
                    v.wait_ge(plain_ready, u + 3)
                    v.tensor_tensor(straight[b][:], plain[b][:], k.cos[:], ALU.mult)
                    v.wait_ge(half_ready, u + 1)
                    v.tensor_tensor(turn[b][:], half[b][:], k.sin[:], ALU.mult)
                    v.drain()
                    one = lambda t: t[:].rearrange("p (a n) -> p a n", a=1)
                    v.tensor_tensor(qkT[:, ds(u, 1), :], one(straight[b]), one(turn[b]), ALU.add).then_inc(out_ready, 1)

                W.split(v, 0, 0, 0)
                W.split(v, 1, 1, 0)
                with v.Fori(0, BLOCKS // 2 - 1) as i:
                    for b in range(2):
                        W.split(v, i * 2 + (b + 2), b, i + 1)
                        outputs(i * 2 + b, b)
                for b in range(2):
                    outputs(BLOCKS - 2 + b, b)


@stage
def stage_token_major(k, tag, w, col0, slabs, finish, n_raw=2):
    nc = k.nc
    RT = KD // 2
    with ExitStack() as ctx:
        W = Weights(k, ctx, tag, RT, 512, n_raw)
        acc = k.banks(ctx, 8, f"{tag}_acc")
        acc_ready, taken = k.sem(f"{tag}_acc_ready"), k.sem(f"{tag}_taken")
        h = (k.h_hi, k.h_lo)

        def slab_pairs(eng, body):
            with eng.Fori(0, slabs // 2) as i:
                for g in range(2):
                    body(i * 2 + g, g)

        with nc.Block() as block:
            @block.sync
            def _(sp):
                def body(s, g):
                    for b in range(2):
                        W.load(sp, s * 2 + b, b, w[b * RT * P:(b + 1) * RT * P, ds(s * 512 + col0, 512)])
                slab_pairs(sp, body)

            @block.tensor
            def _(pe):
                W.start_uses(pe)

                def body(s, g):
                    for b in range(2):
                        W.wait(pe, s * 2 + b)
                        for t in range(NT):
                            if b == 0:
                                pe.wait_ge(taken, s * 4 + t + 1)
                            for n in range(RT):
                                q = b * RT + n
                                ins = mm3(pe, acc[g * 4 + t][:], both(h, q, slice(t * P, (t + 1) * P)), W.tile(b, n), q == 0, q == KD - 1)
                            if b == 1:
                                ins.then_inc(acc_ready, 1)
                        W.done(pe)
                slab_pairs(pe, body)

            @block.vector
            def _(v):
                W.start_splits(v)

                def body(s, g):
                    for b in range(2):
                        W.split(v, s * 2 + b, b, s)
                slab_pairs(v, body)

            @block.scalar
            def _(a):
                a.sem_inc(taken, 8)

                def body(s, g):
                    for t in range(NT):
                        a.wait_ge(acc_ready, s * 4 + t + 1)
                        finish(a, acc[g * 4 + t], s, t).then_inc(taken, 1)
                slab_pairs(a, body)


@stage
def stage_lambda(k, lams, lam_neg, lam_init):
    nc = k.nc
    with ExitStack() as ctx:
        rows = k.sb("lam_rows", [P, 4, 64], F32, ctx)
        prod = k.sb("lam_prod", [P, 2, 64], F32, ctx)
        dots = k.sb("lam_dots", [P, 2], F32, ctx)
        rows_loaded, dots_ready, exp_ready = k.sem("lam_rows_loaded"), k.sem("lam_dots_ready"), k.sem("lam_exp_ready")
        with nc.Block() as block:
            @block.sync
            def _(sp):
                for n, l in enumerate(lams):
                    sp.dma_start(rows[:, n, :], row_bc(l[0])).then_inc(rows_loaded, 16)

            @block.vector
            def _(v):
                v.wait_ge(rows_loaded, 64)
                v.tensor_tensor(prod[:], rows[:, 0::2, :], rows[:, 1::2, :], ALU.mult)
                v.drain()
                v.tensor_reduce(dots[:], prod[:], AX, ALU.add).then_inc(dots_ready, 1)
                v.wait_ge(exp_ready, 1)
                v.tensor_tensor(lam_neg[:], dots[:, 1:2], dots[:, 0:1], ALU.subtract)
                v.drain()
                v.tensor_scalar(lam_neg[:], lam_neg[:], -lam_init, None, ALU.add)

            @block.scalar
            def _(a):
                a.wait_ge(dots_ready, 1)
                a.activation(dots[:], dots[:], ACT.Exp).then_inc(exp_ready, 1)


@stage
def stage_diff_attention(k, qkT, v_tok, att, ss, lam_neg):
    nc = k.nc
    scale = 64 ** -0.5
    with ExitStack() as ctx:
        Q = [k.sb(f"at_q{i}", [P, T], F32, ctx) for i in range(2)]
        K = [k.sb(f"at_k{i}", [P, T], F32, ctx) for i in range(2)]
        S = [k.sb(f"at_s{i}", [P, 2, T], F32, ctx) for i in range(2)]
        mx = [k.sb(f"at_mx{i}", [P, 2], F32, ctx) for i in range(2)]
        sm = [k.sb(f"at_sm{i}", [P, 2], F32, ctx) for i in range(2)]
        W = [k.sb(f"at_w{i}", [P, T], F32, ctx) for i in range(2)]
        WT = [k.sb(f"at_wt{i}", [P, T], F32, ctx) for i in range(2)]
        sq = k.sb("at_sq", [P, P], F32, ctx)
        sc = k.banks(ctx, 4, "at_sc")
        tp = k.banks(ctx, 2, "at_tp")
        ob = k.banks(ctx, 2, "at_ob")
        staged, heads_used = k.sem("at_staged"), k.sem("at_heads_used")
        scores_done, masked, bias_ready, exp_done = k.sem("at_scores"), k.sem("at_masked"), k.sem("at_bias"), k.sem("at_exp")
        w_ready, turned, wt_ready, out_done, out_taken = (k.sem("at_w_ready"), k.sem("at_turned"), k.sem("at_wt_ready"),
                                                         k.sem("at_out_done"), k.sem("at_out_taken"))
        with nc.Block() as block:
            @block.gpsimd
            def _(g):
                with g.Fori(0, 4) as i:
                    for b in range(2):
                        g.wait_ge(heads_used, i * 2 + b + 1)
                        h = i * 2 + b
                        g.tensor_copy(Q[b][:].rearrange("p (a n) -> p a n", a=1), qkT[:, ds(h, 1), :])
                        g.tensor_copy(K[b][:].rearrange("p (a n) -> p a n", a=1), qkT[:, ds(h + 8, 1), :])
                        g.drain().then_inc(staged, 1)

            @block.tensor
            def _(pe):
                pe.sem_inc(heads_used, 2)
                pe.sem_inc(turned, 2)
                pe.sem_inc(out_done, 2)

                def scores(i, s):
                    t, par, u = s % 4, s % 2, i * 8 + s
                    b = s // 4 % 2
                    if t == 0:
                        pe.wait_ge(staged, i * 2 + s // 4 + 1)
                    pe.wait_ge(masked, u + 1)
                    for c in range(2):
                        ins = pe.matmul(sc[2 * par + c][:, 0:(t + 1) * P], Q[b][64 * c:64 * c + 64, t * P:(t + 1) * P],
                                        K[b][64 * c:64 * c + 64, 0:(t + 1) * P], start=True, stop=True)
                    ins.then_inc(scores_done, 1)
                    if t == NT - 1:
                        pe.drain().then_inc(heads_used, 1)

                def turn_weights(i, s):
                    t, par, u = s % 4, s % 2, i * 8 + s
                    pe.wait_ge(w_ready, u + 3)
                    pe.wait_ge(wt_ready, u + 1)
                    for j in range(t + 1):
                        ins = pe.transpose(tp[par][:, j * P:(j + 1) * P], W[par][:, j * P:(j + 1) * P], k.c("ident"))
                    ins.then_inc(turned, 1)

                def values(i, s):
                    t, par, u = s % 4, s % 2, i * 8 + s
                    pe.wait_ge(wt_ready, u + 3)
                    pe.wait_ge(out_taken, u + 1)
                    for j in range(t + 1):
                        ins = pe.matmul(ob[par][:, 0:P], WT[par][:, j * P:(j + 1) * P],
                                        v_tok[:, j, ds(i * 256 + s // 4 * P, P)], start=(j == 0), stop=(j == t))
                    ins.then_inc(out_done, 1)

                def before():
                    scores(0, 0)
                    scores(0, 1)

                def step(i, s, first, last):
                    if not (last and s >= 6):
                        scores(i, s + 2)
                    turn_weights(i, s)
                    if not (first and s == 0):
                        values(i, s - 1)

                pipeline(pe, 4, 8, before, step, lambda i: values(i, 7))

            @block.vector
            def _(v):
                v.sem_inc(masked, 2)
                v.sem_inc(w_ready, 2)

                def mask_and_max(i, s):
                    t, par, u = s % 4, s % 2, i * 8 + s
                    v.wait_ge(scores_done, u + 1)
                    n = (t + 1) * P
                    for c in range(2):
                        ins = v.tensor_tensor(S[par][:, c, 0:n], sc[2 * par + c][:, 0:n], k.c("neg_wide", 512 - n), ALU.add)
                    ins.then_inc(masked, 1)
                    v.drain()
                    v.tensor_reduce(mx[par][:], S[par][:, :, 0:n], AX, ALU.max)
                    v.drain()
                    v.tensor_scalar(mx[par][:], mx[par][:], -scale, None, ALU.mult).then_inc(bias_ready, 1)

                def combine(i, s):
                    t, par, u = s % 4, s % 2, i * 8 + s
                    n = (t + 1) * P
                    v.wait_ge(exp_done, u + 1)
                    v.reciprocal(sm[par][:], sm[par][:])
                    v.drain()
                    v.tensor_tensor(sm[par][:, 1:2], sm[par][:, 1:2], lam_neg[:], ALU.mult)
                    v.wait_ge(turned, u + 1)
                    v.tensor_scalar(W[par][:, 0:n], S[par][:, 0, 0:n], sm[par][:, 0:1], None, ALU.mult)
                    v.drain()
                    v.scalar_tensor_tensor(W[par][:, 0:n], S[par][:, 1, 0:n], sm[par][:, 1:2], W[par][:, 0:n], ALU.mult, ALU.add).then_inc(w_ready, 1)

                def before():
                    mask_and_max(0, 0)
                    mask_and_max(0, 1)

                def step(i, s, first, last):
                    combine(i, s)
                    if not (last and s >= 6):
                        v.drain()
                        mask_and_max(i, s + 2)

                pipeline(v, 4, 8, before, step, lambda i: None)

            @block.scalar
            def _(a):
                a.sem_inc(wt_ready, 2)
                a.sem_inc(out_taken, 2)

                def exps(i, s):
                    par, u, n = s % 2, i * 8 + s, (s % 4 + 1) * P
                    a.wait_ge(bias_ready, u + 1)
                    for c in range(2):
                        a.activation(S[par][:, c, 0:n], S[par][:, c, 0:n], ACT.Exp, bias=mx[par][:, c:c + 1], scale=scale,
                                     accum_out=sm[par][:, c:c + 1])
                    a.drain().then_inc(exp_done, 1)

                def take_weights(i, s):
                    par, u, n = s % 2, i * 8 + s, (s % 4 + 1) * P
                    a.wait_ge(turned, u + 3)
                    a.wait_ge(out_done, u + 1)
                    a.activation(WT[par][:, 0:n], tp[par][:, 0:n], ACT.Copy).then_inc(wt_ready, 1)

                def take_out(i, s):
                    par, u, t = s % 2, i * 8 + s, s % 4
                    a.wait_ge(out_done, u + 3)
                    a.activation(att[:, t, ds(i * 256 + s // 4 * P, P)], ob[par][:, 0:P], ACT.Copy)
                    a.activation(sq[:], ob[par][:, 0:P], ACT.Square, accum_out=ss[:, t, ds(i * 2 + s // 4, 1)])
                    a.drain().then_inc(out_taken, 1)

                def before():
                    exps(0, 0)
                    exps(0, 1)

                def step(i, s, first, last):
                    take_weights(i, s)
                    if not (last and s >= 6):
                        exps(i, s + 2)
                    if not (first and s < 2):
                        take_out(i, s - 2)

                def after(i):
                    take_out(i, 6)
                    take_out(i, 7)

                pipeline(a, 4, 8, before, step, after)


@stage
def stage_scale_and_turn(k, tag, y, ss, groups, width, eps, w_col_src, out, gain=1.0):
    nc = k.nc
    tiles = groups * width // P
    wc = w_col_src.shape[0] // P
    with ExitStack() as ctx:
        wcol = k.sb(f"{tag}_wcol", [P, wc], F32, ctx)
        whole = [k.sb(f"{tag}_whole{i}", [P, T], F32, ctx) for i in range(2)]
        tp = k.banks(ctx, 4, f"{tag}_tp")
        w_loaded, mean_ready, root_ready, y_ready = (k.sem(f"{tag}_w_loaded"), k.sem(f"{tag}_mean"), k.sem(f"{tag}_root"), k.sem(f"{tag}_y_ready"))
        turned, taken, split_done = (k.sem(f"{tag}_{n}") for n in ("turned", "taken", "split_done"))
        with nc.Block() as block:
            @block.sync
            def _(sp):
                with nc.allow_non_contiguous_dma("one column of weights"):
                    sp.dma_start(wcol[:], w_col_src.rearrange("(a p) -> p a", p=P)).then_inc(w_loaded, 16)

            @block.vector
            def _(v):
                v.tensor_scalar(ss[:], ss[:], 1.0 / (width * gain * gain), eps / (gain * gain), ALU.mult, ALU.add).then_inc(mean_ready, 1)
                v.wait_ge(root_ready, 1)
                v.reciprocal(ss[:], ss[:])
                v.drain()
                for t in range(NT):
                    yt = y[:, t, :].rearrange("p (g w) -> p g w", g=groups)
                    v.tensor_tensor(yt, yt, ss[:, t, :].rearrange("p (g a) -> p g a", a=1).broadcast_to([P, groups, width]), ALU.mult).then_inc(y_ready, 1)
                for n in range(tiles):
                    v.wait_ge(taken, n + 1)
                    split(v, out[0][:, n, :], out[1][:, n, :], whole[n % 2][:]).then_inc(split_done, 1)

            @block.tensor
            def _(pe):
                pe.wait_ge(y_ready, NT)
                for n in range(tiles):
                    if n >= 4:
                        pe.wait_ge(taken, n - 3)
                    for t in range(NT):
                        ins = pe.transpose(tp[n % 4][:, t * P:(t + 1) * P], y[:, t, n * P:(n + 1) * P], k.c("ident"))
                    ins.then_inc(turned, 1)

            @block.scalar
            def _(a):
                a.wait_ge(mean_ready, 1)
                a.activation(ss[:], ss[:], ACT.Sqrt).then_inc(root_ready, 1)
                a.wait_ge(w_loaded, 16)
                for n in range(tiles):
                    a.wait_ge(turned, n + 1)
                    if n >= 2:
                        a.wait_ge(split_done, n - 1)
                    a.activation(whole[n % 2][:], tp[n % 4][:], ACT.Copy, scale=wcol[:, n % wc:n % wc + 1]).then_inc(taken, 1)


XBC0 = 3 * 1024 + 2048
Z0 = 3 * 1024
DT0 = XBC0 + 4096
GA0 = DT0 + 32


@stage
def stage_conv(k, w_in, conv_w, conv_b, xbcT):
    nc = k.nc
    BLOCKS = 32
    with ExitStack() as ctx:
        W = Weights(k, ctx, "cv", KD, P)
        u = [k.sb(f"cv_u{i}", [P, T + 3], F32, ctx) for i in range(2)]
        y = [k.sb(f"cv_y{i}", [P, T], F32, ctx) for i in range(2)]
        taps = k.sb("cv_taps", [P, 4, BLOCKS], F32, ctx)
        bias = k.sb("cv_bias", [P, BLOCKS], F32, ctx)
        acc = k.banks(ctx, 4, "cv_acc")
        taps_loaded, acc_ready, u_ready, y_ready, out_ready, pad_zero = (k.sem("cv_" + n) for n in (
            "taps_loaded", "acc_ready", "u_ready", "y_ready", "out_ready", "pad_zero"))
        h = (k.h_hi, k.h_lo)
        with nc.Block() as block:
            @block.sync
            def _(sp):
                W.load(sp, 0, 0, w_in[:, XBC0:XBC0 + P])
                with nc.allow_non_contiguous_dma("a column of taps per block of channels"):
                    for n in range(4):
                        sp.dma_start(taps[:, n, :], conv_w[n].rearrange("(a p) -> p a", p=P)).then_inc(taps_loaded, 16)
                    sp.dma_start(bias[:], conv_b.rearrange("(a p) -> p a", p=P)).then_inc(taps_loaded, 16)
                W.load(sp, 1, 1, w_in[:, XBC0 + P:XBC0 + 2 * P])
                with sp.Fori(1, BLOCKS // 2) as i:
                    for b in range(2):
                        W.load(sp, i * 2 + b, b, w_in[:, ds(i * (2 * P) + (XBC0 + b * P), P)])

            @block.tensor
            def _(pe):
                W.start_uses(pe)
                with pe.Fori(0, BLOCKS // 4) as i:
                    for m in range(4):
                        W.wait(pe, i * 4 + m)
                        pe.wait_ge(u_ready, i * 4 + m + 1)
                        for n in range(KD):
                            ins = mm3(pe, acc[m][:], W.tile(m % 2, n), both(h, n), n == 0, n == KD - 1)
                        ins.then_inc(acc_ready, 1)
                        W.done(pe)

            @block.scalar
            def _(a):
                a.sem_inc(u_ready, 4)
                a.sem_inc(out_ready, 2)
                a.wait_ge(pad_zero, 1)
                with a.Fori(0, BLOCKS // 8) as i:
                    def silu(m):
                        a.wait_ge(y_ready, i * 8 + m + 3)
                        a.activation(xbcT[:, ds(i * 8 + m, 1), :], y[m % 2][:].rearrange("p (a n) -> p a n", a=1), ACT.Silu).then_inc(out_ready, 1)

                    for m in range(8):
                        a.wait_ge(acc_ready, i * 8 + m + 1)
                        a.wait_ge(y_ready, i * 8 + m + 1)
                        a.activation(u[m % 2][:, 3:], acc[m % 4][:], ACT.Copy).then_inc(u_ready, 1)
                        if m >= 1:
                            silu(m - 1)
                    silu(7)

            @block.vector
            def _(v):
                v.memset(u[0][:, 0:3], 0.0)
                v.memset(u[1][:, 0:3], 0.0)
                v.drain().then_inc(pad_zero, 1)
                v.sem_inc(y_ready, 2)
                W.start_splits(v)

                def convolve(c, b):
                    uu, yy = u[b], y[b]
                    v.wait_ge(u_ready, c + 5)
                    v.wait_ge(out_ready, c + 1)
                    v.tensor_scalar(yy[:], uu[:, 3:], taps[:, 3, ds(c, 1)], bias[:, ds(c, 1)], ALU.mult, ALU.add)
                    for n in range(3):
                        v.drain()
                        ins = v.scalar_tensor_tensor(yy[:], uu[:, n:n + T], taps[:, n, ds(c, 1)], yy[:], ALU.mult, ALU.add)
                    ins.then_inc(y_ready, 1)

                W.split(v, 0, 0, 0)
                v.wait_ge(taps_loaded, 80)
                with v.Fori(0, BLOCKS // 2 - 1) as i:
                    W.split(v, i * 2 + 1, 1, i)
                    convolve(i * 2, 0)
                    W.split(v, i * 2 + 2, 0, i + 1)
                    convolve(i * 2 + 1, 1)
                W.split(v, BLOCKS - 1, 1, BLOCKS // 2 - 1)
                convolve(BLOCKS - 2, 0)
                convolve(BLOCKS - 1, 1)


@stage
def stage_turn(k, tag, src, tiles, dst):
    nc = k.nc
    with ExitStack() as ctx:
        tp = k.banks(ctx, 8, f"{tag}_tp")
        turned, taken_a, taken_v = k.sem(f"{tag}_turned"), k.sem(f"{tag}_taken_a"), k.sem(f"{tag}_taken_v")
        groups = [(t, q) for q in range(tiles // 4) for t in range(NT)]
        with nc.Block() as block:
            @block.tensor
            def _(pe):
                for n, (t, q) in enumerate(groups):
                    if n >= 8:
                        pe.wait_ge(taken_v if n % 2 else taken_a, n // 2 - 3)
                    for j in range(4):
                        ins = pe.transpose(tp[n % 8][:, j * P:(j + 1) * P], src[:, 4 * q + j, t * P:(t + 1) * P], k.c("ident"))
                    ins.then_inc(turned, 1)

            @block.scalar
            def _(a):
                for n, (t, q) in enumerate(groups):
                    if n % 2 == 0:
                        a.wait_ge(turned, n + 1)
                        a.activation(dst[:, t, q * 512:(q + 1) * 512], tp[n % 8][:], ACT.Copy).then_inc(taken_a, 1)

            @block.vector
            def _(v):
                for n, (t, q) in enumerate(groups):
                    if n % 2 == 1:
                        v.wait_ge(turned, n + 1)
                        v.tensor_copy(dst[:, t, q * 512:(q + 1) * 512], tp[n % 8][:]).then_inc(taken_v, 1)


@stage
def stage_ssd_steps(k, w_in, dt_bias, a_log, dt, cum, ecum, wtail, etot, adt):
    nc = k.nc
    H = 32
    with ExitStack() as ctx:
        W = k.sb("sd_W", [P, KD, H], F32, ctx)
        bias = k.sb("sd_bias", [P, H], F32, ctx)
        al = k.sb("sd_alog", [P, H], F32, ctx)
        raw = k.sb("sd_raw", [P, NT, H], F32, ctx)
        mag = k.sb("sd_mag", [P, NT, H], F32, ctx)
        tot = k.sb("sd_tot", [P, NT, H], F32, ctx)
        acc = k.banks(ctx, 3, "sd_acc")
        loaded, raw_mm, mag_ready, ln_ready = k.sem("sd_loaded"), k.sem("sd_raw_mm"), k.sem("sd_mag_ready"), k.sem("sd_ln_ready")
        adt_ready, sums_ready, cum_ready = k.sem("sd_adt_ready"), k.sem("sd_sums_ready"), k.sem("sd_cum_ready")
        with nc.Block() as block:
            @block.sync
            def _(sp):
                sp.dma_start(W[:], w_in[:, DT0:DT0 + H].rearrange("(k p) n -> p k n", p=P)).then_inc(loaded, 16)
                sp.dma_start(bias[:], row_bc(dt_bias)).then_inc(loaded, 16)
                sp.dma_start(al[:], row_bc(a_log)).then_inc(loaded, 16)

            @block.tensor
            def _(pe):
                pe.wait_ge(loaded, 48)
                for t in range(NT):
                    for n in range(KD):
                        pe.matmul(acc[0][:, t * H:(t + 1) * H], k.h_hi[:, n, t * P:(t + 1) * P].bitcast(F32), W[:, n, :], start=(n == 0), stop=False)
                        ins = pe.matmul(acc[0][:, t * H:(t + 1) * H], k.h_lo[:, n, t * P:(t + 1) * P].bitcast(F32), W[:, n, :], start=False, stop=(n == KD - 1))
                ins.then_inc(raw_mm, 1)
                pe.wait_ge(adt_ready, 1)
                flat = adt[:].rearrange("p c h -> p (c h)")
                pe.matmul(acc[1][:, 0:NT * H], k.c("upto"), flat, start=True, stop=True)
                pe.matmul(acc[2][:, 0:NT * H], k.c("ones"), flat, start=True, stop=True).then_inc(sums_ready, 1)

            @block.vector
            def _(v):
                bc = lambda t: t[:].rearrange("p (a h) -> p a h", a=1).broadcast_to([P, NT, H])
                ps = lambda n: acc[n][:, 0:NT * H].rearrange("p (c h) -> p c h", h=H)
                v.wait_ge(raw_mm, 1)
                v.tensor_tensor(raw[:], ps(0), bc(bias), ALU.add)
                v.drain()
                v.scalar_tensor_tensor(mag[:], raw[:], -1.0, raw[:], ALU.mult, ALU.min).then_inc(mag_ready, 1)
                v.wait_ge(ln_ready, 1)
                v.scalar_tensor_tensor(dt[:], raw[:], 0.0, mag[:], ALU.max, ALU.add)
                v.drain()
                v.scalar_tensor_tensor(adt[:], dt[:], -1.0, bc(al), ALU.mult, ALU.mult).then_inc(adt_ready, 1)
                v.wait_ge(sums_ready, 1)
                v.tensor_copy(cum[:], ps(1))
                v.tensor_copy(tot[:], ps(2))
                v.drain()
                v.tensor_tensor(wtail[:], tot[:], cum[:], ALU.subtract).then_inc(cum_ready, 1)

            @block.scalar
            def _(a):
                a.wait_ge(loaded, 48)
                a.activation(al[:], al[:], ACT.Exp)
                a.wait_ge(mag_ready, 1)
                a.activation(mag[:], mag[:], ACT.Exp)
                a.drain()
                a.activation(mag[:], mag[:], ACT.Ln, bias=1.0).then_inc(ln_ready, 1)
                a.wait_ge(cum_ready, 1)
                a.activation(ecum[:], cum[:], ACT.Exp)
                a.activation(etot[:], tot[:], ACT.Exp)
                a.activation(wtail[:], wtail[:], ACT.Exp)


@stage
def stage_ssd(k, xbcT, xs, btok, zs, dt, cum, ecum, wtail, etot, adt, d_skip, ss):
    nc = k.nc
    HG, N = 4, 256
    with ExitStack() as ctx:
        BT = [k.sb(f"ss_bt{i}", [P, T], F32, ctx) for i in range(1)]
        CT = [k.sb(f"ss_ct{i}", [P, T], F32, ctx) for i in range(1)]
        BK = [k.sb(f"ss_bk{i}", [P, NT, P], F32, ctx) for i in range(1)]
        xdt = [k.sb(f"ss_xdt{i}", [P, HG, 64], F32, ctx) for i in range(2)]
        xw = [k.sb(f"ss_xw{i}", [P, HG, 64], F32, ctx) for i in range(2)]
        rows = [k.sb(f"ss_rows{i}", [P, HG, P], F32, ctx) for i in range(2)]
        dec = [k.sb(f"ss_dec{i}", [P, HG, P], F32, ctx) for i in range(2)]
        state = k.sb("ss_state", [P, HG, 64], F32, ctx)
        yo = k.sb("ss_yo", [P, HG, 64], F32, ctx)
        xd = k.sb("ss_xd", [P, HG, 64], F32, ctx)
        dsk = k.sb("ss_dsk", [P, 32], F32, ctx)
        sq = k.sb("ss_sq", [P, N], F32, ctx)
        cb_b = k.banks(ctx, 2, "ss_cb")
        cs_b = k.banks(ctx, 2, "ss_cs")
        yd_b = k.banks(ctx, 2, "ss_yd")
        st_b = k.banks(ctx, 2, "ss_st")
        sem = lambda n: k.sem("ss_" + n)
        dsk_loaded, staged, rows_ready, sums_ready, seg_ready, exp_ready, dec_ready, y_ready, state_ready, chunk_done = map(
            sem, ("dsk_loaded", "staged", "rows_ready", "sums_ready", "seg_ready", "exp_ready", "dec_ready", "y_ready", "state_ready", "chunk_done"))
        group_used = sem("group_used")
        bc = lambda ap: ap.rearrange("p (h a) -> p h a", a=1).broadcast_to([P, HG, 64])
        hv = lambda ap: ap.rearrange("p (h e) -> p h e", h=HG)
        with nc.Block() as block:
            @block.sync
            def _(sp):
                sp.dma_start(dsk[:], row_bc(d_skip)).then_inc(dsk_loaded, 16)

            @block.gpsimd
            def _(g):
                with g.Fori(0, 8) as i:
                    g.wait_ge(group_used, i + 1)
                    one = lambda t: t[:].rearrange("p (a n) -> p a n", a=1)
                    g.tensor_copy(one(BT[0]), xbcT[:, ds(i + 16, 1), :])
                    g.tensor_copy(one(CT[0]), xbcT[:, ds(i + 24, 1), :])
                    g.tensor_copy(BK[0][:], btok[:, :, ds(i * P, P)])
                    g.drain().then_inc(staged, 1)

            @block.tensor
            def _(pe):
                pe.sem_inc(group_used, 1)
                with pe.Fori(0, 8) as i:
                    pe.wait_ge(staged, i + 1)

                    def head_part(c):
                        u = i * 4 + c
                        pe.wait_ge(rows_ready, u + 1)
                        pe.matmul(cs_b[c % 2][:], k.c("ones"), rows[c % 2][:].rearrange("p h n -> p (h n)"), start=True, stop=True)
                        pe.matmul(cb_b[c % 2][:, 0:P], BT[0][:, c * P:(c + 1) * P], CT[0][:, c * P:(c + 1) * P], start=True, stop=True).then_inc(sums_ready, 1)

                    head_part(0)
                    for c in range(NT):
                        u = i * 4 + c
                        if c < NT - 1:
                            head_part(c + 1)
                        pe.wait_ge(dec_ready, u + 1)
                        for h in range(HG):
                            pe.matmul(yd_b[c % 2][:, h * 64:(h + 1) * 64], dec[c % 2][:, h, :], xdt[c % 2][:, h, :], start=True, stop=True)
                        if c < NT - 1:
                            pe.matmul(st_b[c % 2][:, 0:N], BK[0][:, c, :], xw[c % 2][:].rearrange("p h e -> p (h e)"), start=True, stop=True)
                        if c > 0:
                            pe.wait_ge(state_ready, i * 3 + c)
                            pe.matmul(yd_b[c % 2][:, N:2 * N], CT[0][:, c * P:(c + 1) * P], state[:].rearrange("p h e -> p (h e)"), start=True, stop=True)
                        pe.drain().then_inc(y_ready, 1)
                    pe.drain().then_inc(group_used, 1)

            @block.vector
            def _(v):
                v.wait_ge(dsk_loaded, 16)
                with v.Fori(0, 8) as i:
                    xv = lambda c: hv(xs[:, c, ds(i * N, N)])
                    hs = ds(i * HG, HG)

                    def make_rows(c):
                        for h in range(HG):
                            ins = v.tensor_scalar(rows[c % 2][:, h, :], k.c("upto"), adt[:, c, ds(i * HG + h, 1)], None, ALU.mult)
                        ins.then_inc(rows_ready, 1)

                    def decays(c):
                        u = i * 4 + c
                        v.wait_ge(sums_ready, u + 1)
                        for h in range(HG):
                            ins = v.scalar_tensor_tensor(dec[c % 2][:, h, :], cs_b[c % 2][:, h * P:(h + 1) * P], cum[:, c, ds(i * HG + h, 1)],
                                                         k.c("neg_after"), ALU.subtract, ALU.add)
                        ins.then_inc(seg_ready, 1)
                        v.tensor_tensor(xdt[c % 2][:], xv(c), bc(dt[:, c, hs]), ALU.mult)
                        v.drain()
                        v.tensor_tensor(xw[c % 2][:], xdt[c % 2][:], bc(wtail[:, c, hs]), ALU.mult)
                        v.wait_ge(exp_ready, u + 1)
                        v.tensor_tensor(dec[c % 2][:], dec[c % 2][:], cb_b[c % 2][:, 0:P].rearrange("p (a n) -> p a n", a=1).broadcast_to([P, HG, P]),
                                        ALU.mult).then_inc(dec_ready, 1)

                    def outputs(c):
                        u = i * 4 + c
                        v.drain()
                        v.tensor_tensor(xd[:], xv(c), bc(dsk[:, hs]), ALU.mult)
                        v.drain()
                        v.wait_ge(y_ready, u + 1)
                        if c < NT - 1:
                            if c > 0:
                                v.tensor_tensor(state[:], state[:], bc(etot[:, c, hs]), ALU.mult)
                                v.drain()
                                v.tensor_tensor(state[:], state[:], hv(st_b[c % 2][:, 0:N]), ALU.add).then_inc(state_ready, 1)
                            else:
                                v.tensor_copy(state[:], hv(st_b[c % 2][:, 0:N])).then_inc(state_ready, 1)
                        v.tensor_tensor(xd[:], xd[:], hv(yd_b[c % 2][:, 0:N]), ALU.add)
                        if c > 0:
                            v.tensor_tensor(yo[:], hv(yd_b[c % 2][:, N:2 * N]), bc(ecum[:, c, hs]), ALU.mult)
                            v.drain()
                            v.tensor_tensor(xd[:], xd[:], yo[:], ALU.add)
                        v.drain()
                        v.tensor_tensor(xv(c), xd[:], hv(zs[:, c, ds(i * N, N)]), ALU.mult).then_inc(chunk_done, 1)

                    make_rows(0)
                    make_rows(1)
                    decays(0)
                    for c in range(NT):
                        if c + 1 < NT:
                            if c + 2 < NT:
                                make_rows(c + 2)
                            decays(c + 1)
                        outputs(c)

            @block.scalar
            def _(a):
                with a.Fori(0, 8) as i:
                    def square(c):
                        a.wait_ge(chunk_done, i * 4 + c + 1)
                        a.activation(sq[:], xs[:, c, ds(i * N, N)], ACT.Square, accum_out=ss[:, c, ds(i, 1)])
                        a.drain()

                    for c in range(NT):
                        a.wait_ge(seg_ready, i * 4 + c + 1)
                        a.activation(dec[c % 2][:], dec[c % 2][:], ACT.Exp).then_inc(exp_ready, 1)
                        if c >= 1:
                            square(c - 1)
                    square(NT - 1)


E = 64
EH = 512
CAP = 128
XB = 7
NA = 2 * T
SLOTS = (E + XB) * CAP
FAR = 4096


@stage
def stage_gated(k, tag, gate, w_gate, gate_col, w, col, x, blocks, finish, out):
    nc = k.nc
    NV = w.shape[0] // D
    NU = 2 * (1 + NV)
    STEPS = blocks // 2
    with ExitStack() as ctx:
        W = Weights(k, ctx, tag, KD, P)
        sig = [k.sb(f"{tag}_sig{i}", [P, 1, T], F32, ctx) for i in range(2)]
        gate_acc, acc = k.banks(ctx, 2, f"{tag}_gacc"), k.banks(ctx, 2, f"{tag}_acc")
        gate_ready, acc_ready, sig_ready, out_taken = (k.sem(f"{tag}_{n}") for n in ("gate_ready", "acc_ready", "sig_ready", "out_taken"))
        h = (k.h_hi, k.h_lo)
        units = [(m, part) for m in range(2) for part in range(-1, NV)]
        with nc.Block() as block:
            @block.sync
            def _(sp):
                with sp.Fori(0, STEPS) as i:
                    for j, (m, part) in enumerate(units):
                        src = w_gate[:, ds(i * (2 * P) + (gate_col + m * P), P)] if part < 0 else w[part * D:(part + 1) * D, ds(i * (2 * P) + (col + m * P), P)]
                        W.load(sp, i * NU + j, j % 2, src)

            @block.tensor
            def _(pe):
                W.start_uses(pe)
                with pe.Fori(0, STEPS) as i:
                    for j, (m, part) in enumerate(units):
                        u = i * 2 + m
                        W.wait(pe, i * NU + j)
                        if part < 0:
                            pe.wait_ge(sig_ready, u + 1)
                            for q in range(KD):
                                ins = mm3(pe, gate_acc[m][:], W.tile(j % 2, q), both(h, q), q == 0, q == KD - 1)
                            ins.then_inc(gate_ready, 1)
                        else:
                            if part == 0:
                                pe.wait_ge(out_taken, u + 1)
                            for q in range(KD):
                                ins = mm3(pe, acc[m][:], W.tile(j % 2, q), both(x, part * KD + q), part == 0 and q == 0, part == NV - 1 and q == KD - 1)
                            if part == NV - 1:
                                ins.then_inc(acc_ready, 1)
                        W.done(pe)

            @block.scalar
            def _(a):
                a.sem_inc(sig_ready, 2)
                with a.Fori(0, STEPS) as i:
                    for m in range(2):
                        u = i * 2 + m
                        a.wait_ge(gate_ready, u + 1)
                        a.wait_ge(out_taken, u + 1)
                        a.activation(sig[m][:, 0, :], gate_acc[m][:], gate).then_inc(sig_ready, 1)

            @block.vector
            def _(v):
                v.sem_inc(out_taken, 2)
                W.start_splits(v)

                def take(u, m):
                    v.wait_ge(sig_ready, u + 3)
                    v.wait_ge(acc_ready, u + 1)
                    value = acc[m][:].rearrange("p (a n) -> p a n", a=1)
                    if finish == "set":
                        v.tensor_tensor(out[:, ds(u, 1), :], sig[m][:], value, ALU.mult).then_inc(out_taken, 1)
                        return
                    v.tensor_tensor(sig[m][:], sig[m][:], value, ALU.mult)
                    v.drain()
                    if finish == "add":
                        v.tensor_tensor(out[:, ds(u, 1), :], out[:, ds(u, 1), :], sig[m][:], ALU.add).then_inc(out_taken, 1)
                    else:
                        split(v, out[0][:, ds(u, 1), :], out[1][:, ds(u, 1), :], sig[m][:]).then_inc(out_taken, 1)

                def step(i, last=False):
                    for j, (m, part) in enumerate(units):
                        if not (last and j == NU - 1):
                            W.split(v, i * NU + (j + 1), (j + 1) % 2, i * (NU // 2) + (j + 1) // 2)
                        if part == NV - 1:
                            take(i * 2 + m, m)

                W.split(v, 0, 0, 0)
                with v.Fori(0, STEPS - 1) as i:
                    step(i)
                step(STEPS - 1, last=True)


@stage
def stage_residual(k, tag, w, lhs, kt=KD, src=None, reload=None):
    nc = k.nc
    RT = 4
    with ExitStack() as ctx:
        W = Weights(k, ctx, tag, RT, 512)
        acc = k.banks(ctx, 8, f"{tag}_acc")
        acc_ready, src_used, x_loaded = (k.sem(f"{tag}_{n}") for n in ("acc_ready", "src_used", "x_loaded"))
        pieces = [(s, r, min(r + RT, kt)) for s in range(2) for r in range(0, kt, RT)]
        with nc.Block() as block:
            @block.sync
            def _(sp):
                for n, (s, lo, hi) in enumerate(pieces):
                    W.load(sp, n, n % 2, w[lo * P:hi * P, s * 512:(s + 1) * 512], hi - lo)
                if reload is not None:
                    sp.wait_ge(src_used, 1)
                    sp.dma_start(k.x[:], reload.rearrange("(t p) d -> p t d", p=P)).then_inc(x_loaded, 16)

            @block.tensor
            def _(pe):
                W.start_uses(pe)
                for n, (s, lo, hi) in enumerate(pieces):
                    W.wait(pe, n)
                    for t in range(NT):
                        for q in range(lo, hi):
                            ins = mm3(pe, acc[s * 4 + t][:], both(lhs, q, slice(t * P, (t + 1) * P)), W.tile(n % 2, q - lo), q == 0, q == kt - 1)
                        if hi == kt:
                            ins.then_inc(acc_ready, 1)
                    W.done(pe)

            @block.vector
            def _(v):
                W.start_splits(v)
                for n, (s, lo, hi) in enumerate(pieces):
                    if src is not None and s == 0:
                        split(v, lhs[0][:, lo:hi, :], lhs[1][:, lo:hi, :], src[:, lo:hi, :])
                        drained = v.drain()
                        if hi == kt:
                            drained.then_inc(src_used, 1)
                    W.split(v, n, n % 2, n // 2, hi - lo)
                if reload is not None:
                    v.wait_ge(x_loaded, 16)
                for n in range(8):
                    s, t = n // 4, n % 4
                    v.wait_ge(acc_ready, n + 1)
                    v.tensor_tensor(k.x[:, t, s * 512:(s + 1) * 512], k.x[:, t, s * 512:(s + 1) * 512], acc[n][:], ALU.add)


@stage
def stage_route(k, w_gr, b_gr, w_er, b_er, h2, h2_rows, slot_list, gidx, sidx, xexp, weights):
    nc = k.nc
    G, J, A = 8, 8, 8
    with ExitStack() as ctx:
        t_ = lambda n, s, dt=F32: k.sb("rt_" + n, s, dt, ctx)
        W, bias = t_("W", [P, KD, 72]), t_("bias", [P, 72])
        lg = t_("lg", [P, NT, 72])
        m1, m2, cand, sel = t_("m1", [P, NT]), t_("m2", [P, NT]), t_("cand", [P, NT, 8]), t_("sel", [P, NT])
        go, eo = t_("go", [P, NT, G]), t_("eo", [P, 2, NT, J])
        prod, esel = t_("prod", [P, NT, J, G]), t_("esel", [P, NT, J])
        gs, gex, ex = t_("gs", [P, NT]), t_("gex", [P, NT, G]), t_("ex", [P, NT])
        O, before = t_("O", [P, A, E]), t_("before", [P, A, E])
        tmp, rank, da, db = t_("tmp", [P, A, E]), t_("rank", [P, A]), t_("da", [P, A]), t_("db", [P, A])
        cnt, xb, xend, xbase = t_("cnt", [P, E]), t_("xb", [P, E]), t_("xend", [P, E]), t_("xbase", [P, E])
        dest, ids = t_("dest", [P, A], U32), t_("ids", [P, A], I32)
        empty = t_("empty", [E + XB, P], I32)
        lst_i, lst_f = t_("lst_i", [E + XB, P], I32), t_("lst_f", [E + XB, P])
        gf, sf, far = t_("gf", [P, E + XB]), t_("sf", [P, E + XB]), t_("far", [P, E + XB])
        xe = t_("xe", [1, 8])
        xcmp = t_("xcmp", [1, E])
        eight = t_("eight", [P, 8])
        one64 = t_("one64", [P, E])
        acc = k.banks(ctx, 4, "rt_acc")
        (loaded, lg_mm, gmax_ready, gexp_ready, emax_ready, eexp_ready, sums_in, sums_ready, empty_ready, empty_stored, dest_ready,
         scattered, list_loaded, list_f, list_turned, rows_stored) = (k.sem("rt_" + n) for n in (
             "loaded", "lg_mm", "gmax", "gexp", "emax", "eexp", "sums_in", "sums_ready", "empty_ready", "empty_stored", "dest_ready",
             "scattered", "list_loaded", "list_f", "list_turned", "rows_stored"))
        with nc.Block() as block:
            @block.sync
            def _(sp):
                sp.dma_start(W[:, :, 0:8], w_gr.rearrange("(k p) n -> p k n", p=P)).then_inc(loaded, 16)
                sp.dma_start(W[:, :, 8:72], w_er.rearrange("(k p) n -> p k n", p=P)).then_inc(loaded, 16)
                sp.dma_start(bias[:, 0:8], row_bc(b_gr)).then_inc(loaded, 16)
                sp.dma_start(bias[:, 8:72], row_bc(b_er)).then_inc(loaded, 16)
                sp.dma_start(h2_rows.rearrange("(t p) d -> p t d", p=P), h2[:]).then_inc(rows_stored, 16)
                sp.wait_ge(empty_ready, 1)
                sp.dma_start(slot_list.rearrange("(b p) a -> b (p a)", p=P), empty[:]).then_inc(empty_stored, 16)
                sp.wait_ge(scattered, 16 * A)
                sp.dma_start(lst_i[:], slot_list.rearrange("(b p) a -> b (p a)", p=P)).then_inc(list_loaded, 16)
                sp.wait_ge(rows_stored, 16)

            @block.gpsimd
            def _(g):
                g.wait_ge(empty_stored, 16)
                g.wait_ge(dest_ready, 1)
                for a in range(A):
                    g.indirect_dma_start(slot_list, bass.IndirectOffsetOnAxis(dest[:, a:a + 1], 0), ids[:, a:a + 1], None,
                                         bounds_check=SLOTS - 1, oob_is_err=False).then_inc(scattered, 16)

            @block.tensor
            def _(pe):
                pe.wait_ge(loaded, 64)
                for t in range(NT):
                    for n in range(KD):
                        pe.matmul(acc[0][:, t * 72:(t + 1) * 72], k.h_hi[:, n, t * P:(t + 1) * P].bitcast(F32), W[:, n, :], start=(n == 0), stop=False)
                        ins = pe.matmul(acc[0][:, t * 72:(t + 1) * 72], k.h_lo[:, n, t * P:(t + 1) * P].bitcast(F32), W[:, n, :], start=False, stop=(n == KD - 1))
                ins.then_inc(lg_mm, 1)
                pe.wait_ge(sums_in, 1)
                flat = lambda t: t[:].rearrange("p a e -> p (a e)")
                pe.matmul(acc[1][:], k.c("before"), flat(O), start=True, stop=False)
                pe.matmul(acc[1][:], k.c("ones"), flat(before), start=False, stop=True)
                pe.matmul(acc[2][:, 0:E], k.c("ones"), cnt[:], start=True, stop=True).then_inc(sums_ready, 1)
                pe.wait_ge(list_f, 1)
                pe.transpose(acc[3][:, 0:E + XB], lst_f[:], k.c("ident")[0:E + XB, 0:E + XB]).then_inc(list_turned, 1)

            @block.scalar
            def _(a):
                a.wait_ge(gmax_ready, 1)
                a.activation(gex[:], gex[:], ACT.Exp).then_inc(gexp_ready, 1)
                a.wait_ge(emax_ready, 1)
                a.activation(ex[:], ex[:], ACT.Exp).then_inc(eexp_ready, 1)

            @block.vector
            def _(v):
                def do(f, *args, **kw):
                    ins = f(*args, **kw)
                    v.drain()
                    return ins

                bc3 = lambda ap, n: ap.rearrange("p (t a) -> p t a", a=1).broadcast_to([P, ap.shape[1], n])
                iota8 = eight[:].rearrange("p (a j) -> p a j", a=1).broadcast_to([P, NT, 8])

                def first_max(vals, best, onehot):
                    do(v.tensor_reduce, best[:], vals, AX, ALU.max)
                    do(v.tensor_tensor, cand[:], vals, bc3(best[:], 8), ALU.is_equal)
                    do(v.tensor_scalar, cand[:], cand[:], -100.0, 100.0, ALU.mult, ALU.add)
                    do(v.tensor_tensor, cand[:], cand[:], iota8, ALU.add)
                    do(v.tensor_reduce, sel[:], cand[:], AX, ALU.min)
                    do(v.tensor_tensor, onehot, iota8, bc3(sel[:], 8), ALU.is_equal)

                v.memset(empty[:], FAR)
                v.drain().then_inc(empty_ready, 1)
                v.memset(far[:], 0.0)
                v.memset(one64[:], 1.0)
                for j in range(8):
                    v.memset(eight[:, j:j + 1], float(j))
                for a in range(A):
                    v.tensor_scalar(ids[:, a:a + 1], k.c("rank"), float(a * P), None, ALU.add)
                v.wait_ge(loaded, 64)
                v.wait_ge(lg_mm, 1)
                do(v.tensor_tensor, lg[:], acc[0][:, 0:NT * 72].rearrange("p (t n) -> p t n", n=72),
                   bias[:].rearrange("p (a n) -> p a n", a=1).broadcast_to([P, NT, 72]), ALU.add)
                first_max(lg[:, :, 0:8], m1, go[:])
                do(v.tensor_tensor, gex[:], lg[:, :, 0:8], bc3(m1[:], 8), ALU.subtract).then_inc(gmax_ready, 1)
                el = lg[:, :, 8:72].rearrange("p t (g j) -> p t j g", g=G)
                for t in range(NT):
                    v.tensor_tensor(prod[:, t], el[:, t], go[:, t:t + 1, :].broadcast_to([P, J, G]), ALU.mult)
                v.drain()
                do(v.tensor_reduce, esel[:], prod[:], AX, ALU.add)
                first_max(esel[:], m1, eo[:, 0])
                do(v.scalar_tensor_tensor, esel[:], eo[:, 0], -3e38, esel[:], ALU.mult, ALU.add)
                first_max(esel[:], m2, eo[:, 1])
                do(v.tensor_tensor, ex[:], m2[:], m1[:], ALU.subtract).then_inc(emax_ready, 1)
                v.wait_ge(gexp_ready, 1)
                do(v.tensor_reduce, gs[:], gex[:], AX, ALU.add)
                v.wait_ge(eexp_ready, 1)
                do(v.tensor_scalar, sel[:], ex[:], 1.0, None, ALU.add)
                do(v.tensor_tensor, sel[:], sel[:], gs[:], ALU.mult)
                do(v.reciprocal, weights[:, 0, :], sel[:])
                do(v.tensor_tensor, weights[:, 1, :], weights[:, 0, :], ex[:], ALU.mult)
                for c in range(2):
                    for t in range(NT):
                        v.tensor_tensor(O[:, c * NT + t].rearrange("p (g j) -> p g j", g=G),
                                        go[:, t].rearrange("p (g a) -> p g a", a=1).broadcast_to([P, G, J]),
                                        eo[:, c, t:t + 1, :].broadcast_to([P, G, J]), ALU.mult)
                v.memset(before[:, 0], 0.0)
                v.drain()
                for a in range(1, A):
                    do(v.tensor_tensor, before[:, a], before[:, a - 1], O[:, a - 1], ALU.add)
                do(v.tensor_tensor, cnt[:], before[:, A - 1], O[:, A - 1], ALU.add).then_inc(sums_in, 1)
                v.wait_ge(sums_ready, 1)
                ps1 = acc[1][:].rearrange("p (a e) -> p a e", e=E)
                do(v.tensor_tensor, tmp[:], O[:], ps1, ALU.mult)
                do(v.tensor_reduce, rank[:], tmp[:], AX, ALU.add)
                do(v.tensor_copy, cnt[:], acc[2][:, 0:E])
                do(v.tensor_scalar, xb[:], cnt[:], float(CAP), None, ALU.is_gt)
                for m in (2, 3):
                    do(v.scalar_tensor_tensor, xb[:], cnt[:], float(m * CAP), xb[:], ALU.is_gt, ALU.add)
                do(v.tensor_tensor_scan, xend[:], one64[:], xb[:], 0.0, ALU.mult, ALU.add)
                do(v.tensor_tensor, xbase[:], xend[:], xb[:], ALU.subtract)
                do(v.tensor_scalar, xbase[:], xbase[:], float(CAP), float((E - 1) * CAP), ALU.mult, ALU.add)
                bce = lambda ap: ap.rearrange("p (a e) -> p a e", a=1).broadcast_to([P, A, E])
                do(v.tensor_tensor, tmp[:], O[:], bce(k.c("expert_slot")), ALU.mult)
                do(v.tensor_reduce, da[:], tmp[:], AX, ALU.add)
                do(v.tensor_tensor, tmp[:], O[:], bce(xbase[:]), ALU.mult)
                do(v.tensor_reduce, db[:], tmp[:], AX, ALU.add)
                do(v.tensor_tensor, db[:], db[:], da[:], ALU.subtract)
                do(v.tensor_tensor, da[:], da[:], rank[:], ALU.add)
                do(v.scalar_tensor_tensor, db[:], rank[:], float(CAP), db[:], ALU.is_ge, ALU.mult)
                do(v.tensor_tensor, da[:], da[:], db[:], ALU.add)
                v.tensor_copy(dest[:], da[:])
                v.drain().then_inc(dest_ready, 1)
                v.memset(xe[:], 0.0)
                v.drain()
                for b in range(XB):
                    do(v.tensor_scalar, xcmp[:], xend[0:1, :], float(b), None, ALU.is_le)
                    do(v.tensor_reduce, xe[:, b:b + 1], xcmp[:], AX, ALU.add)
                do(v.tensor_scalar, xe[:], xe[:], float(E - 1), None, ALU.min)
                do(v.tensor_copy, xe[:, XB:XB + 1], xend[0:1, E - 1:E])
                v.tensor_copy(xexp[:], xe[:])
                v.wait_ge(list_loaded, 16)
                v.tensor_copy(lst_f[:], lst_i[:])
                v.drain().then_inc(list_f, 1)
                v.wait_ge(list_turned, 1)
                do(v.tensor_copy, sf[:], acc[3][:, 0:E + XB])
                do(v.tensor_scalar, gf[:], sf[:], float(T), -float(T), ALU.is_ge, ALU.mult)
                do(v.tensor_tensor, gf[:], gf[:], sf[:], ALU.add)
                v.tensor_copy(gidx[:, 0:E + XB], gf[:])
                v.tensor_copy(sidx[:, 0:E + XB], sf[:])


@stage
def stage_experts(k, w_gate, w_up, w_down, h2_rows, y_rows, gidx, sidx, xexp):
    nc = k.nc
    HT = EH // P
    with ExitStack() as ctx:
        dbl = lambda n, s, dt=F32: [k.sb(f"ex_{n}{i}", s, dt, ctx) for i in range(2)]
        WG, WU, WD = dbl("WG", [P, KD, EH]), dbl("WU", [P, KD, EH]), dbl("WD", [P, HT, D])
        X, XT, Y = dbl("X", [P, D]), dbl("XT", [P, KD, P]), dbl("Y", [P, D])
        gi, si = dbl("gi", [P, 1], U32), dbl("si", [P, 1], U32)
        sg, hid, hT = k.sb("ex_sg", [P, EH], F32, ctx), k.sb("ex_hid", [P, EH], F32, ctx), k.sb("ex_hT", [P, HT, P], F32, ctx)
        xt_ps, g_ps, u_ps, h_ps, y_ps = k.banks(ctx, 2, "ex_xtp"), k.banks(ctx, 1, "ex_gp")[0], k.banks(ctx, 1, "ex_up")[0], k.banks(ctx, 1, "ex_hp")[0], k.banks(ctx, 2, "ex_yp")
        sem = lambda n: k.sem("ex_" + n)
        g_loaded, u_loaded, d_loaded = ([sem(f"{n}_loaded{i}") for i in range(2)] for n in "gud")
        gathered, scattered = ([sem(f"{n}{i}") for i in range(2)] for n in ("gathered", "scattered"))
        g_used, u_used, d_used, x_turned = (sem(n) for n in ("g_used", "u_used", "d_used", "x_turned"))
        xt_taken, silu_done, hid_ready, h_turned, ht_taken, y_ready, y_taken_v, y_taken_a = (sem(n) for n in (
            "xt_taken", "silu_done", "hid_ready", "h_turned", "ht_taken", "y_ready", "y_taken_v", "y_taken_a"))
        g_ready, u_ready, gi_ready, si_ready = (sem(n) for n in ("g_ready", "u_ready", "gi_ready", "si_ready"))
        gather_due, scatter_due = sem("gather_due"), sem("scatter_due")

        def has_before(n):
            return not isinstance(n, int) or n >= 2

        def units(pair):
            return ((pair * 2 + 1, 1, pair), (pair * 2 + 2, 0, pair + 1))

        def load(sp, n, b, e, used, dst, w, loaded):
            sp.wait_ge(used, n + 1)
            sp.dma_start(dst[b][:].rearrange("p (a k) n -> p a k n", a=1), w[ds(e, 1)].rearrange("a (p k) n -> p a k n", p=P)).then_inc(loaded[b], 16)

        def load_in(sp, unit, e):
            n, b, rnd = unit
            load(sp, n, b, e, g_used, WG, w_gate, g_loaded)
            load(sp, n, b, e, u_used, WU, w_up, u_loaded)

        def load_down(sp, unit, e):
            n, b, rnd = unit
            load(sp, n, b, e, d_used, WD, w_down, d_loaded)

        def gather(g, n, b, rnd):
            g.wait_ge(x_turned, n + 1)
            if has_before(n):
                g.wait_ge(gathered[b], rnd * 16)
            g.tensor_copy(gi[b][:], gidx[:, ds(n, 1)]).then_inc(gi_ready, 1)
            g.wait_ge(gi_ready, n + 1)
            g.sem_inc(gather_due, 1)
            g.indirect_dma_start(X[b][:], None, h2_rows, bass.IndirectOffsetOnAxis(gi[b][:], 0), bounds_check=T - 1, oob_is_err=False).then_inc(gathered[b], 16)

        def scatter(g, n, b, rnd):
            if has_before(n):
                g.wait_ge(scattered[b], rnd * 16)
            g.tensor_copy(si[b][:], sidx[:, ds(n, 1)]).then_inc(si_ready, 1)
            g.wait_ge(si_ready, n + 1)
            g.wait_ge(y_taken_v, n + 2)
            g.wait_ge(y_taken_a, n + 2)
            g.sem_inc(scatter_due, 1)
            g.indirect_dma_start(y_rows, bass.IndirectOffsetOnAxis(si[b][:], 0), Y[b][:], None, bounds_check=NA - 1, oob_is_err=False).then_inc(scattered[b], 16)

        def turn_x(pe, n, b, rnd):
            pe.wait_ge(gathered[b], rnd * 16 + 16)
            pe.wait_ge(xt_taken, n + 1)
            for q in range(KD):
                ins = pe.transpose(xt_ps[q // 4][:, (q % 4) * P:(q % 4 + 1) * P], X[b][:, q::KD], k.c("ident"))
            ins.then_inc(x_turned, 1)

        def gate_up(pe, n, b, rnd):
            pe.wait_ge(xt_taken, n + 2)
            for loaded, free, ps, W, ready, used in ((g_loaded, silu_done, g_ps, WG, g_ready, g_used), (u_loaded, hid_ready, u_ps, WU, u_ready, u_used)):
                pe.wait_ge(loaded[b], rnd * 16 + 16)
                pe.wait_ge(free, n + 1)
                for q in range(KD):
                    ins = pe.matmul(ps[:], XT[b][:, q, :], W[b][:, q, :], start=(q == 0), stop=(q == KD - 1))
                ins.then_inc(ready, 1)
                pe.drain().then_inc(used, 1)

        def down(pe, n, b, rnd):
            pe.wait_ge(hid_ready, n + 2)
            pe.wait_ge(ht_taken, n + 1)
            for q in range(HT):
                ins = pe.transpose(h_ps[:, q * P:(q + 1) * P], hid[:, q::HT], k.c("ident"))
            ins.then_inc(h_turned, 1)
            pe.wait_ge(d_loaded[b], rnd * 16 + 16)
            pe.wait_ge(y_taken_v, n + 1)
            pe.wait_ge(y_taken_a, n + 1)
            pe.wait_ge(ht_taken, n + 2)
            for s in range(2):
                for q in range(HT):
                    ins = pe.matmul(y_ps[s][:], hT[:, q, :], WD[b][:, q, s * 512:(s + 1) * 512], start=(q == 0), stop=(q == HT - 1))
            ins.then_inc(y_ready, 1)
            pe.drain().then_inc(d_used, 1)

        def take_x(v, n, b, rnd):
            v.wait_ge(x_turned, n + 3)
            for s in range(2):
                ins = v.tensor_copy(XT[b][:, s * 4:s * 4 + 4, :], xt_ps[s][:].rearrange("p (q n) -> p q n", q=4))
            ins.then_inc(xt_taken, 1)

        def make_hid(v, n, b, rnd):
            v.wait_ge(u_ready, n + 1)
            v.wait_ge(silu_done, n + 2)
            v.wait_ge(h_turned, n + 1)
            v.tensor_tensor(hid[:], sg[:], u_ps[:], ALU.mult).then_inc(hid_ready, 1)

        def take_y(e, copy, s, taken, n, b, rnd):
            e.wait_ge(y_ready, n + 2)
            if has_before(n):
                e.wait_ge(scattered[b], rnd * 16)
            copy(Y[b][:, s * 512:(s + 1) * 512], y_ps[s][:]).then_inc(taken, 1)

        def silu(a, n, b, rnd):
            a.wait_ge(g_ready, n + 1)
            a.wait_ge(hid_ready, n + 1)
            a.activation(sg[:], g_ps[:], ACT.Silu).then_inc(silu_done, 1)

        def take_h(a, n, b, rnd):
            a.wait_ge(h_turned, n + 2)
            a.wait_ge(y_ready, n + 1)
            a.activation(hT[:].rearrange("p q n -> p (q n)"), h_ps[:], ACT.Copy).then_inc(ht_taken, 1)

        LAST = (E - 1, 1, (E - 1) // 2)

        def run(eng, first, steady, drain):
            def pair(j):
                one, two = units(j)
                steady(one, (j * 2, 0, j), two)
                steady(two, one, (j * 2 + 3, 1, j + 1))

            first((0, 0, 0), (1, 1, 0))
            pair(0)
            with eng.Fori(1, (E - 2) // 2) as j:
                pair(j)
            drain(LAST, (E - 2, 0, (E - 2) // 2))

        def further(eng, body):
            count = eng.value_load(xexp[0:1, XB:XB + 1], min_val=0, max_val=XB)
            with eng.Fori(0, (XB + 1) // 2) as j:
                for b in range(2):
                    with eng.If(j * 2 + b < count):
                        body((j * 2 + (E + b), b, j + E // 2), j * 2 + b)

        with nc.Block() as block:
            @block.sync
            def _(sp):
                def first(u, nxt):
                    load_in(sp, u, u[0])
                def steady(u, prev, nxt):
                    load_in(sp, u, u[0])
                    load_down(sp, prev, prev[0])
                def drain(u, prev):
                    load_in(sp, u, u[0])
                    load_down(sp, prev, prev[0])
                    load_down(sp, u, u[0])
                run(sp, first, steady, drain)

                def body(unit, nth):
                    e = sp.value_load(xexp[0:1, ds(nth, 1)], min_val=0, max_val=E - 1)
                    load_in(sp, unit, e)
                    load_down(sp, unit, e)
                further(sp, body)

            @block.gpsimd
            def _(g):
                g.memset(X[0][:], 0.0)
                g.memset(X[1][:], 0.0)
                g.drain()
                def first(u, nxt):
                    gather(g, *u)
                    gather(g, *nxt)
                def steady(u, prev, nxt):
                    gather(g, *nxt)
                    scatter(g, *prev)
                def drain(u, prev):
                    scatter(g, *prev)
                    scatter(g, *u)
                run(g, first, steady, drain)
                further(g, lambda unit, nth: (gather(g, *unit), scatter(g, *unit)))
                n_more = g.value_load(xexp[0:1, XB:XB + 1], min_val=0, max_val=XB)
                g.wait_ge(scattered[0], E // 2 * 16 + ((n_more + 1) // 2) * 16)
                g.wait_ge(scattered[1], E // 2 * 16 + (n_more // 2) * 16)

            @block.tensor
            def _(pe):
                for s in (g_used, u_used, d_used, x_turned):
                    pe.sem_inc(s, 2)
                for s in (h_turned, y_ready):
                    pe.sem_inc(s, 1)
                def first(u, nxt):
                    turn_x(pe, *u)
                    gate_up(pe, *u)
                    turn_x(pe, *nxt)
                def steady(u, prev, nxt):
                    gate_up(pe, *u)
                    turn_x(pe, *nxt)
                    down(pe, *prev)
                def drain(u, prev):
                    gate_up(pe, *u)
                    down(pe, *prev)
                    down(pe, *u)
                run(pe, first, steady, drain)
                further(pe, lambda unit, nth: (turn_x(pe, *unit), gate_up(pe, *unit), down(pe, *unit)))

            @block.vector
            def _(v):
                for s in (xt_taken, hid_ready, y_taken_v):
                    v.sem_inc(s, 1)
                take = lambda u: take_y(v, lambda o, i: v.tensor_copy(o, i), 0, y_taken_v, *u)
                def first(u, nxt):
                    take_x(v, *u)
                    make_hid(v, *u)
                    take_x(v, *nxt)
                def steady(u, prev, nxt):
                    make_hid(v, *u)
                    take_x(v, *nxt)
                    take(prev)
                def drain(u, prev):
                    make_hid(v, *u)
                    take(prev)
                    take(u)
                run(v, first, steady, drain)
                further(v, lambda unit, nth: (take_x(v, *unit), make_hid(v, *unit), take(unit)))

            @block.scalar
            def _(a):
                for s in (silu_done, ht_taken, y_taken_a):
                    a.sem_inc(s, 1)
                take = lambda u: take_y(a, lambda o, i: a.activation(o, i, ACT.Copy), 1, y_taken_a, *u)
                def first(u, nxt):
                    silu(a, *u)
                def steady(u, prev, nxt):
                    silu(a, *u)
                    take_h(a, *prev)
                    take(prev)
                def drain(u, prev):
                    silu(a, *u)
                    take_h(a, *prev)
                    take(prev)
                    take_h(a, *u)
                    take(u)
                run(a, first, steady, drain)
                further(a, lambda unit, nth: (silu(a, *unit), take_h(a, *unit), take(unit)))


@stage
def stage_combine(k, y_rows, weights):
    nc = k.nc
    with ExitStack() as ctx:
        Y = k.sb("cb_Y", [P, 2 * NT, D], F32, ctx)
        loaded = k.sem("cb_loaded")
        with nc.Block() as block:
            @block.sync
            def _(sp):
                sp.dma_start(Y[:], y_rows.rearrange("(a p) d -> p a d", p=P)).then_inc(loaded, 16)

            @block.vector
            def _(v):
                v.wait_ge(loaded, 16)
                for c in range(2):
                    for t in range(NT):
                        v.scalar_tensor_tensor(k.x[:, t, :], Y[:, c * NT + t, :], weights[:, c, t:t + 1], k.x[:, t, :], ALU.mult, ALU.add)
                    v.drain()


RW = 256
RW_IN = 3 * RW + 128
CH = 64
MH = 8
MQ, MKV = 384, 256
DFF = 2816


def col(v):
    return v.rearrange("(a p) -> p a", p=P)


@stage
def stage_features(k, l, w_in, mu, rkv, rqk, krT, cos32, sin32):
    nc = k.nc
    with ExitStack() as ctx:
        W = Weights(k, ctx, f"ft{l}", KD, P)
        WK = k.sb(f"ft{l}_WK", [P, KD, 32], F32, ctx)
        mus = k.sb(f"ft{l}_mu", [P, 7], F32, ctx)
        u = [k.sb(f"ft{l}_u{i}", [P, T + 1], F32, ctx) for i in range(2)]
        d = k.sb(f"ft{l}_d", [P, T], F32, ctx)
        e = k.sb(f"ft{l}_e", [P, T], F32, ctx)
        acc = k.banks(ctx, 4, f"ft{l}_acc")
        half = k.banks(ctx, 2, f"ft{l}_half")
        small_loaded, acc_ready, u_ready, half_ready, out_ready, pad_zero = (k.sem(f"ft{l}_" + n) for n in (
            "small_loaded", "acc_ready", "u_ready", "half_ready", "out_ready", "pad_zero"))
        h = (k.h_hi, k.h_lo)
        KROPE = 1920 + MQ + MKV
        rows = lambda m: slice(0, P) if m < 11 else slice(64, 96)
        with nc.Block() as block:
            @block.sync
            def _(sp):
                with nc.allow_non_contiguous_dma("columns"):
                    sp.dma_start(mus[:], col(mu)).then_inc(small_loaded, 16)
                sp.dma_start(WK[:], w_in[:, KROPE:KROPE + 32].rearrange("(k p) n -> p k n", p=P)).then_inc(small_loaded, 16)
                for m in range(11):
                    W.load(sp, m, m % 2, w_in[:, m * P:(m + 1) * P])

            @block.tensor
            def _(pe):
                def turn(m):
                    if m < 7:
                        return
                    pe.wait_ge(u_ready, m + 1)
                    if m >= 9:
                        pe.wait_ge(out_ready, m - 1)
                    r = rows(m)
                    turner = k.c("turn64") if m < 11 else k.c("turn32")[r, 64:96]
                    pe.matmul(half[m % 2][r, :], turner, u[m % 2][r, 1:], start=True, stop=True).then_inc(half_ready, 1)

                W.start_uses(pe)
                for m in range(12):
                    if m == 11:
                        pe.wait_ge(small_loaded, 32)
                    if m >= 4:
                        pe.wait_ge(u_ready, m - 3)
                    if m < 11:
                        W.wait(pe, m)
                    for n in range(KD):
                        if m < 11:
                            ins = mm3(pe, acc[m % 4][:], W.tile(m % 2, n), both(h, n), n == 0, n == KD - 1)
                        else:
                            pe.matmul(acc[m % 4][rows(m), :], WK[:, n, :], k.h_hi[:, n, :].bitcast(F32), start=(n == 0), stop=False)
                            ins = pe.matmul(acc[m % 4][rows(m), :], WK[:, n, :], k.h_lo[:, n, :].bitcast(F32), start=False, stop=(n == KD - 1))
                    ins.then_inc(acc_ready, 1)
                    if m < 11:
                        W.done(pe)
                    if m >= 1:
                        turn(m - 1)
                turn(11)

            @block.scalar
            def _(a):
                a.wait_ge(pad_zero, 1)
                for m in range(12):
                    a.wait_ge(acc_ready, m + 1)
                    if m >= 2:
                        a.wait_ge(out_ready, m - 1)
                    a.activation(u[m % 2][rows(m), 1:], acc[m % 4][rows(m), :], ACT.Copy).then_inc(u_ready, 1)

            @block.vector
            def _(v):
                v.memset(u[0][:, 0:1], 0.0)
                v.memset(u[1][:, 0:1], 0.0)
                v.drain().then_inc(pad_zero, 1)
                W.start_splits(v)
                W.split(v, 0, 0, 0)
                v.wait_ge(small_loaded, 32)
                for m in range(12):
                    if m + 1 < 11:
                        W.split(v, m + 1, (m + 1) % 2, (m + 1) // 2)
                    v.wait_ge(u_ready, m + 1)
                    uu, r = u[m % 2], rows(m)
                    v.drain()
                    if m < 7:
                        v.tensor_tensor(d[:], uu[:, 0:T], uu[:, 1:], ALU.subtract)
                        v.drain()
                        v.scalar_tensor_tensor(rkv[:, m, :], d[:], mus[:, m:m + 1], uu[:, 1:], ALU.mult, ALU.add).then_inc(out_ready, 1)
                    else:
                        cos, sin = (k.cos, k.sin) if m < 11 else (cos32, sin32)
                        out = rqk[:, m - 7, :] if m < 11 else krT[r, :]
                        v.tensor_tensor(d[r, :], uu[r, 1:], cos[r, :], ALU.mult)
                        v.wait_ge(half_ready, m - 6)
                        v.tensor_tensor(e[r, :], half[m % 2][r, :], sin[r, :], ALU.mult)
                        v.drain()
                        v.tensor_tensor(out, d[r, :], e[r, :], ALU.add).then_inc(out_ready, 1)


@stage
def stage_tokens(k, l, w_in, vg, lat, ssl):
    nc = k.nc
    base = RW_IN + 2 * RW
    slabs = [(base, 512), (base + 512, MQ), (base + 512 + MQ, MKV)]
    RT = KD // 2
    with ExitStack() as ctx:
        W = Weights(k, ctx, f"tk{l}", RT, 512)
        sq = k.sb(f"tk{l}_sq", [P, MQ], F32, ctx)
        acc = k.banks(ctx, 8, f"tk{l}_acc")
        acc_ready, taken = k.sem(f"tk{l}_acc_ready"), k.sem(f"tk{l}_taken")
        h = (k.h_hi, k.h_lo)
        with nc.Block() as block:
            @block.sync
            def _(sp):
                for n, (lo, w) in enumerate(slabs):
                    for b in range(2):
                        W.load(sp, 2 * n + b, b, w_in[b * RT * P:(b + 1) * RT * P, lo:lo + w], cols=w)

            @block.tensor
            def _(pe):
                W.start_uses(pe)
                for n, (lo, w) in enumerate(slabs):
                    for b in range(2):
                        W.wait(pe, 2 * n + b)
                        for t in range(NT):
                            bank = (n % 2) * 4 + t
                            if n > 1 and b == 0:
                                pe.wait_ge(taken, (n - 2) * 4 + t + 1)
                            for r in range(RT):
                                q = b * RT + r
                                ins = mm3(pe, acc[bank][:, 0:w], both(h, q, slice(t * P, (t + 1) * P)), W.tile(b, r, slice(0, w)), q == 0, q == KD - 1)
                            if b == 1:
                                ins.then_inc(acc_ready, 1)
                        W.done(pe)

            @block.vector
            def _(v):
                W.start_splits(v)
                for n, (lo, w) in enumerate(slabs):
                    for b in range(2):
                        W.split(v, 2 * n + b, b, n, cols=w)

            @block.scalar
            def _(a):
                for n, (lo, w) in enumerate(slabs):
                    for t in range(NT):
                        a.wait_ge(acc_ready, n * 4 + t + 1)
                        if n == 0:
                            a.activation(vg[:, t, 0:RW], acc[(n % 2) * 4 + t][:, 0:RW], ACT.Copy)
                            a.activation(vg[:, t, RW:], acc[(n % 2) * 4 + t][:, RW:], ACT.Silu).then_inc(taken, 1)
                        else:
                            off = 0 if n == 1 else MQ
                            a.activation(lat[:, t, off:off + w], acc[(n % 2) * 4 + t][:, 0:w], ACT.Copy)
                            a.activation(sq[:, 0:w], acc[(n % 2) * 4 + t][:, 0:w], ACT.Square, accum_out=ssl[:, t, n - 1:n])
                            a.drain().then_inc(taken, 1)


@stage
def stage_latents(k, l, lat, ssl, q_norm, kv_norm, latT):
    nc = k.nc
    with ExitStack() as ctx:
        wcol = k.sb(f"la{l}_wcol", [P, 5], F32, ctx)
        tp = k.banks(ctx, 5, f"la{l}_tp")
        w_loaded, mean_ready, root_ready, y_ready, turned = (k.sem(f"la{l}_" + n) for n in ("w_loaded", "mean", "root", "y_ready", "turned"))
        with nc.Block() as block:
            @block.sync
            def _(sp):
                with nc.allow_non_contiguous_dma("columns"):
                    sp.dma_start(wcol[:, 0:3], col(q_norm)).then_inc(w_loaded, 16)
                    sp.dma_start(wcol[:, 3:5], col(kv_norm)).then_inc(w_loaded, 16)

            @block.vector
            def _(v):
                v.tensor_scalar(ssl[:, :, 0:1], ssl[:, :, 0:1], 1.0 / MQ, 1e-6, ALU.mult, ALU.add)
                v.tensor_scalar(ssl[:, :, 1:2], ssl[:, :, 1:2], 1.0 / MKV, 1e-6, ALU.mult, ALU.add)
                v.drain().then_inc(mean_ready, 1)
                v.wait_ge(root_ready, 1)
                v.reciprocal(ssl[:], ssl[:])
                v.drain()
                for t in range(NT):
                    v.tensor_scalar(lat[:, t, 0:MQ], lat[:, t, 0:MQ], ssl[:, t, 0:1], None, ALU.mult)
                    v.tensor_scalar(lat[:, t, MQ:], lat[:, t, MQ:], ssl[:, t, 1:2], None, ALU.mult)
                    v.drain().then_inc(y_ready, 1)

            @block.tensor
            def _(pe):
                pe.wait_ge(y_ready, NT)
                for n in range(5):
                    for t in range(NT):
                        ins = pe.transpose(tp[n][:, t * P:(t + 1) * P], lat[:, t, n * P:(n + 1) * P], k.c("ident"))
                    ins.then_inc(turned, 1)

            @block.scalar
            def _(a):
                a.wait_ge(mean_ready, 1)
                a.activation(ssl[:], ssl[:], ACT.Sqrt).then_inc(root_ready, 1)
                a.wait_ge(w_loaded, 32)
                for n in range(5):
                    a.wait_ge(turned, n + 1)
                    a.activation(latT[:, n, :], tp[n][:], ACT.Copy, scale=wcol[:, n:n + 1])


@stage
def stage_retention(k, l, rqk, vg, mix):
    nc = k.nc
    with ExitStack() as ctx:
        kd = k.sb(f"re{l}_kd", [P, 2, T], F32, ctx)
        qd = k.sb(f"re{l}_qd", [P, 2, T], F32, ctx)
        kt = k.sb(f"re{l}_kt", [P, NT, RW], F32, ctx)
        inn = [k.sb(f"re{l}_in{i}", [P, 4, P], F32, ctx) for i in range(2)]
        R = k.sb(f"re{l}_R", [P, NT, 2, 64], F32, ctx)
        y = k.sb(f"re{l}_y", [P, NT, 4, 64], F32, ctx)
        yc = k.sb(f"re{l}_yc", [P, NT, 4, 64], F32, ctx)
        ss = k.sb(f"re{l}_ss", [P, NT, 4], F32, ctx)
        bk = k.banks(ctx, 8, f"re{l}_bk")
        tp, kv = bk[0:2], bk[2]
        yi, yx, sc = bk[0:2], bk[2:4], (bk[4:6], bk[6:8])
        (dec_ready, turned, kt_ready, kv_ready, R_ready, sc_ready, inn_ready, y_ready, y_taken, mean_ready, root_ready) = (k.sem(f"re{l}_" + n) for n in (
            "dec_ready", "turned", "kt_ready", "kv_ready", "R_ready", "sc_ready", "inn_ready", "y_ready", "y_taken", "mean", "root"))
        lane = lambda h: slice(64 * (h % 2), 64 * (h % 2) + 64)
        with nc.Block() as block:
            @block.vector
            def _(v):
                ch = lambda ap: ap.rearrange("p (c n) -> p c n", n=P)
                over = lambda ap: ap.rearrange("p (a n) -> p a n", a=1).broadcast_to([P, NT, P])
                for b in range(2):
                    v.tensor_tensor(ch(kd[:, b, :]), ch(rqk[:, 2 + b, :]), over(k.c(f"ret_k{b}")), ALU.mult)
                    v.tensor_tensor(ch(qd[:, b, :]), ch(rqk[:, b, :]), over(k.c(f"ret_q{b}")), ALU.mult)
                v.memset(R[:, 0], 0.0)
                v.drain().then_inc(dec_ready, 1)
                for t in range(NT):
                    v.wait_ge(turned, t + 1)
                    v.tensor_copy(kt[:, t, :], tp[t % 2][:, 0:RW]).then_inc(kt_ready, 1)
                v.wait_ge(kv_ready, 1)
                for t in range(NT - 1):
                    v.drain()
                    for b in range(2):
                        v.scalar_tensor_tensor(R[:, t + 1, b, :], R[:, t, b, :], k.c("ret_state", b, b + 1), kv[:, (t * 2 + b) * 64:(t * 2 + b) * 64 + 64],
                                               ALU.mult, ALU.add)
                v.drain().then_inc(R_ready, 1)

                def take_y(t):
                    v.wait_ge(y_ready, t + 1)
                    v.tensor_copy(y[:, t].rearrange("p h e -> p (h e)"), yi[t % 2][:, 0:RW])
                    v.drain()
                    for side in range(2):
                        v.tensor_tensor(y[:, t, side::2, :], y[:, t, side::2, :], yx[side][:, 0:P].rearrange("p (h n) -> p h n", h=2), ALU.add)
                    v.drain().then_inc(y_taken, 1)

                for t in range(NT):
                    v.wait_ge(sc_ready, t + 1)
                    if t >= 2:
                        v.wait_ge(y_ready, t - 1)
                    for side in range(2):
                        ins = v.tensor_tensor(inn[t % 2][:, side::2, :], sc[t % 2][side][:, 0:2 * P].rearrange("p (h n) -> p h n", h=2),
                                              k.c("ret_decay").rearrange("p (h n) -> p h n", h=4)[:, side::2, :], ALU.mult)
                    ins.then_inc(inn_ready, 1)
                    if t >= 1:
                        take_y(t - 1)
                take_y(NT - 1)
                v.drain()
                fl = lambda t: t[:].rearrange("p c h e -> p (c h) e")
                v.tensor_tensor(yc[:], y[:], y[:], ALU.mult)
                v.drain()
                v.tensor_reduce(ss[:].rearrange("p c h -> p (c h)"), fl(yc), AX, ALU.add)
                v.drain()
                v.tensor_scalar(ss[:], ss[:], 1.0 / 64, 1e-6, ALU.mult, ALU.add).then_inc(mean_ready, 1)
                v.wait_ge(root_ready, 1)
                v.reciprocal(ss[:], ss[:])
                v.drain()
                v.tensor_tensor(fl(y), fl(y), ss[:].rearrange("p c h -> p (c h)").rearrange("p (n a) -> p n a", a=1).broadcast_to([P, 16, 64]), ALU.mult)
                v.drain()
                v.tensor_tensor(mix[:, :, RW:2 * RW], y[:].rearrange("p c h e -> p c (h e)"), vg[:, :, RW:], ALU.mult)

            @block.scalar
            def _(a):
                a.wait_ge(mean_ready, 1)
                a.activation(ss[:], ss[:], ACT.Sqrt).then_inc(root_ready, 1)

            @block.tensor
            def _(pe):
                pe.wait_ge(dec_ready, 1)
                for t in range(NT):
                    if t >= 2:
                        pe.wait_ge(kt_ready, t - 1)
                    for b in range(2):
                        ins = pe.transpose(tp[t % 2][:, b * P:(b + 1) * P], kd[:, b, t * P:(t + 1) * P], k.c("ident"))
                    ins.then_inc(turned, 1)
                pe.wait_ge(kt_ready, NT)
                for t in range(NT - 1):
                    for h in range(4):
                        o = (t * 2 + h // 2) * 64
                        ins = pe.matmul(kv[lane(h), o:o + 64], kt[:, t, h * 64:h * 64 + 64], vg[:, t, h * 64:h * 64 + 64], start=True, stop=True)
                ins.then_inc(kv_ready, 1)

                def scores(t):
                    if t >= 2:
                        pe.wait_ge(inn_ready, t - 1)
                    for h in range(4):
                        s = slice(t * P, (t + 1) * P)
                        ins = pe.matmul(sc[t % 2][h % 2][:, (h // 2) * P:(h // 2 + 1) * P], rqk[lane(h), 2 + h // 2, s], rqk[lane(h), h // 2, s], start=True, stop=True)
                    ins.then_inc(sc_ready, 1)

                scores(0)
                pe.wait_ge(R_ready, 1)
                for t in range(NT):
                    if t < NT - 1:
                        scores(t + 1)
                    pe.wait_ge(inn_ready, t + 1)
                    if t >= 1:
                        pe.wait_ge(y_taken, t)
                    for h in range(4):
                        pe.matmul(yi[t % 2][:, h * 64:h * 64 + 64], inn[t % 2][:, h, :], vg[:, t, h * 64:h * 64 + 64], start=True, stop=True)
                    for h in range(4):
                        ins = pe.matmul(yx[h % 2][:, (h // 2) * 64:(h // 2) * 64 + 64], qd[lane(h), h // 2, t * P:(t + 1) * P], R[lane(h), t, h // 2, :],
                                        start=True, stop=True)
                    pe.drain().then_inc(y_ready, 1)


@stage
def stage_mla_up(k, l, latT, krT, w_q_up, w_kv_up, cos32, sin32, QT, KT, v_tok):
    nc = k.nc
    R = slice(64, 96)
    with ExitStack() as ctx:
        WQ, WKV = k.sb(f"mu{l}_WQ", [P, 3, MH * 96], F32, ctx), k.sb(f"mu{l}_WKV", [P, 2, MH * P], F32, ctx)
        d = [k.sb(f"mu{l}_d{i}", [P, T], F32, ctx) for i in range(2)]
        qa, ka, half, va = k.banks(ctx, 2, f"mu{l}_qa"), k.banks(ctx, 2, f"mu{l}_ka"), k.banks(ctx, 2, f"mu{l}_half"), k.banks(ctx, 2, f"mu{l}_va")
        loaded, q_ready, k_ready, q_taken, k_taken, half_ready, rope_done, v_ready, v_taken = (k.sem(f"mu{l}_" + n) for n in (
            "loaded", "q_ready", "k_ready", "q_taken", "k_taken", "half_ready", "rope_done", "v_ready", "v_taken"))
        with nc.Block() as block:
            @block.sync
            def _(sp):
                sp.dma_start(WQ[:], w_q_up.rearrange("(k p) n -> p k n", p=P)).then_inc(loaded, 16)
                sp.dma_start(WKV[:], w_kv_up.rearrange("(k p) n -> p k n", p=P)).then_inc(loaded, 16)

            @block.tensor
            def _(pe):
                pe.wait_ge(loaded, 32)

                def turn(h):
                    pe.wait_ge(q_taken, h + 1)
                    if h >= 2:
                        pe.wait_ge(rope_done, h - 1)
                    pe.matmul(half[h % 2][R, :], k.c("turn32")[R, R], QT[R, h, :], start=True, stop=True).then_inc(half_ready, 1)

                for h in range(MH):
                    if h >= 2:
                        pe.wait_ge(q_taken, h - 1)
                        pe.wait_ge(k_taken, h - 1)
                    for n in range(3):
                        ins = pe.matmul(qa[h % 2][0:96, :], WQ[:, n, h * 96:h * 96 + 96], latT[:, n, :], start=(n == 0), stop=(n == 2))
                    ins.then_inc(q_ready, 1)
                    for n in range(2):
                        ins = pe.matmul(ka[h % 2][0:64, :], WKV[:, n, h * P:h * P + 64], latT[:, 3 + n, :], start=(n == 0), stop=(n == 1))
                    ins.then_inc(k_ready, 1)
                    if h >= 1:
                        turn(h - 1)
                turn(MH - 1)
                for t in range(NT):
                    if t >= 2:
                        pe.wait_ge(v_taken, t - 1)
                    for n in range(2):
                        ins = pe.matmul(va[t % 2][:], latT[:, 3 + n, t * P:(t + 1) * P], WKV[:, n, :].rearrange("p (h c) -> p h c", h=MH)[:, :, 64:],
                                        start=(n == 0), stop=(n == 1))
                    ins.then_inc(v_ready, 1)

            @block.scalar
            def _(a):
                for h in range(MH):
                    a.wait_ge(q_ready, h + 1)
                    a.activation(QT[0:96, h, :], qa[h % 2][0:96, :], ACT.Copy).then_inc(q_taken, 1)
                    a.wait_ge(k_ready, h + 1)
                    a.activation(KT[0:64, h, :], ka[h % 2][0:64, :], ACT.Copy).then_inc(k_taken, 1)
                    a.activation(KT[R, h, :], krT[R, :], ACT.Copy)
                for t in range(NT):
                    a.wait_ge(v_ready, t + 1)
                    a.activation(v_tok[:, t, :], va[t % 2][:], ACT.Copy).then_inc(v_taken, 1)

            @block.vector
            def _(v):
                for h in range(MH):
                    v.wait_ge(half_ready, h + 1)
                    v.drain()
                    v.tensor_tensor(QT[R, h, :], QT[R, h, :], cos32[R, :], ALU.mult)
                    v.tensor_tensor(d[h % 2][R, :], half[h % 2][R, :], sin32[R, :], ALU.mult)
                    v.drain()
                    v.tensor_tensor(QT[R, h, :], QT[R, h, :], d[h % 2][R, :], ALU.add).then_inc(rope_done, 1)


@stage
def stage_mla_attention(k, l, QT, KT, v_tok, mix):
    nc = k.nc
    scale = 96 ** -0.5
    with ExitStack() as ctx:
        two = lambda n, s: [k.sb(f"ml{l}_{n}{i}", s, F32, ctx) for i in range(2)]
        four = lambda n, s: [k.sb(f"ml{l}_{n}{i}", s, F32, ctx) for i in range(4)]
        Q, K, mx, sm, WT = two("q", [96, T]), two("k", [96, T]), two("mx", [P, 1]), two("sm", [P, 1]), two("wt", [P, T])
        S, rs = four("s", [P, T]), four("rs", [P, 1])
        sc, tp, ob = k.banks(ctx, 2, f"ml{l}_sc"), k.banks(ctx, 2, f"ml{l}_tp"), k.banks(ctx, 2, f"ml{l}_ob")
        staged, heads_used, scores_done, masked, bias_ready, exp_done, turned, wt_ready, sum_ready, out_done, out_taken = (k.sem(f"ml{l}_" + n) for n in (
            "staged", "heads_used", "scores", "masked", "bias", "exp", "turned", "wt_ready", "sum_ready", "out_done", "out_taken"))
        with nc.Block() as block:
            @block.gpsimd
            def _(g):
                with g.Fori(0, MH // 2) as i:
                    for b in range(2):
                        g.wait_ge(heads_used, i * 2 + b + 1)
                        for dst, src in ((Q, QT), (K, KT)):
                            g.tensor_copy(dst[b][:].rearrange("p (a n) -> p a n", a=1), src[0:96, ds(i * 2 + b, 1), :])
                        g.drain().then_inc(staged, 1)

            @block.tensor
            def _(pe):
                pe.sem_inc(heads_used, 2)
                pe.sem_inc(out_done, 2)
                pe.sem_inc(turned, 4)

                def scores(i, s):
                    t, u = s % 4, i * 8 + s
                    b = s // 4 % 2
                    if t == 0:
                        pe.wait_ge(staged, i * 2 + s // 4 + 1)
                    pe.wait_ge(masked, u + 1)
                    pe.matmul(sc[t % 2][:, 0:(t + 1) * P], Q[b][:, t * P:(t + 1) * P], K[b][:, 0:(t + 1) * P], start=True, stop=True).then_inc(scores_done, 1)
                    if t == NT - 1:
                        pe.drain().then_inc(heads_used, 1)

                def turn_weights(i, s):
                    t, u = s % 4, i * 8 + s
                    pe.wait_ge(exp_done, u + 1)
                    pe.wait_ge(wt_ready, u + 1)
                    for j in range(t + 1):
                        ins = pe.transpose(tp[t % 2][:, j * P:(j + 1) * P], S[t][:, j * P:(j + 1) * P], k.c("ident"))
                    ins.then_inc(turned, 1)

                def values(i, s):
                    t, u = s % 4, i * 8 + s
                    pe.wait_ge(wt_ready, u + 3)
                    pe.wait_ge(out_taken, u + 3)
                    for j in range(t + 1):
                        ins = pe.matmul(ob[t % 2][:, 0:64], WT[t % 2][:, j * P:(j + 1) * P], v_tok[:, j, ds(i * 128 + s // 4 * 64, 64)], start=(j == 0), stop=(j == t))
                    ins.then_inc(out_done, 1)

                def before():
                    scores(0, 0)
                    scores(0, 1)

                def step(i, s, first, last):
                    if not (last and s >= 6):
                        scores(i, s + 2)
                    turn_weights(i, s)
                    if not (first and s == 0):
                        values(i, s - 1)

                pipeline(pe, MH // 2, 8, before, step, lambda i: values(i, 7))

            @block.vector
            def _(v):
                v.sem_inc(masked, 2)

                def mask_and_max(i, s):
                    t, par, u = s % 4, s % 2, i * 8 + s
                    n = (t + 1) * P
                    v.wait_ge(scores_done, u + 1)
                    v.wait_ge(turned, u + 1)
                    v.tensor_tensor(S[t][:, 0:n], sc[par][:, 0:n], k.c("neg_wide", 512 - n), ALU.add).then_inc(masked, 1)
                    v.drain()
                    v.tensor_reduce(mx[par][:], S[t][:, 0:n], AX, ALU.max)
                    v.drain()
                    v.tensor_scalar(mx[par][:], mx[par][:], -scale, None, ALU.mult).then_inc(bias_ready, 1)

                def invert(i, s):
                    par, u = s % 2, i * 8 + s
                    v.wait_ge(exp_done, u + 1)
                    v.wait_ge(out_taken, u + 1)
                    v.reciprocal(rs[s % 4][:], sm[par][:]).then_inc(sum_ready, 1)

                def before():
                    mask_and_max(0, 0)
                    mask_and_max(0, 1)

                def step(i, s, first, last):
                    invert(i, s)
                    if not (last and s >= 6):
                        mask_and_max(i, s + 2)

                pipeline(v, MH // 2, 8, before, step, lambda i: None)

            @block.scalar
            def _(a):
                a.sem_inc(wt_ready, 2)
                a.sem_inc(out_taken, 4)

                def exps(i, s):
                    t, par, u = s % 4, s % 2, i * 8 + s
                    n = (t + 1) * P
                    a.wait_ge(bias_ready, u + 1)
                    a.activation(S[t][:, 0:n], S[t][:, 0:n], ACT.Exp, bias=mx[par][:], scale=scale, accum_out=sm[par][:])
                    a.drain().then_inc(exp_done, 1)

                def take_weights(i, s):
                    par, u, n = s % 2, i * 8 + s, (s % 4 + 1) * P
                    a.wait_ge(turned, u + 5)
                    a.wait_ge(out_done, u + 1)
                    a.activation(WT[par][:, 0:n], tp[par][:, 0:n], ACT.Copy).then_inc(wt_ready, 1)

                def take_out(i, s):
                    par, u, t = s % 2, i * 8 + s, s % 4
                    a.wait_ge(out_done, u + 3)
                    a.wait_ge(sum_ready, u + 1)
                    a.activation(mix[:, t, ds(i * 128 + (2 * RW + s // 4 * 64), 64)], ob[par][:, 0:64], ACT.Copy, scale=rs[t][:]).then_inc(out_taken, 1)

                def before():
                    exps(0, 0)
                    exps(0, 1)

                def step(i, s, first, last):
                    take_weights(i, s)
                    if not (last and s >= 6):
                        exps(i, s + 2)
                    if not (first and s < 2):
                        take_out(i, s - 2)

                def after(i):
                    take_out(i, 6)
                    take_out(i, 7)

                pipeline(a, MH // 2, 8, before, step, after)


@stage
def stage_rwkv_prep(k, rkv, w, v_first, out, eb, vt, gt, bonus, layer):
    nc = k.nc
    A_, R_, B_, K_ = out
    Be, Ke, pc = eb
    with ExitStack() as ctx:
        names = ["w0", "a0", "k_k", "k_a", "r_k"] + (["v0"] if layer else [])
        cols = k.sb(f"rp{layer}_cols", [P, 7, 2], F32, ctx)
        wl = k.sb(f"rp{layer}_wl", [P, RW], F32, ctx)
        big = lambda n: k.sb(f"rp{layer}_" + n, [P, 2, T], F32, ctx)
        sgw, av, kk, t1, cum, e1 = (big(n) for n in ("sgw", "av", "kk", "t1", "cum", "e1"))
        if layer:
            v1, v2, low = k.sb(f"rp{layer}_v1", [P, 2, 32], F32, ctx), k.sb(f"rp{layer}_v2", [32, RW], F32, ctx), k.sb(f"rp{layer}_low", [32, T], F32, ctx)
        bk = k.banks(ctx, 8, f"rp{layer}_bk")
        (loaded, low_ready, wa_ready, sig_ready, v1_ready, low_v_ready, v2_ready, vsig_ready, v_done, sq_ready, norm_ready, root_in, root_ready,
         cum_ready, exp_ready, exp_used, tok_in, tok_ready, rk_in) = (k.sem(f"rp{layer}_" + n) for n in (
             "loaded", "low_ready", "wa_ready", "sig_ready", "v1_ready", "low_v_ready", "v2_ready", "vsig_ready", "v_done", "sq_ready", "norm_ready",
             "root_in", "root_ready", "cum_ready", "exp_ready", "exp_used", "tok_in", "tok_ready", "rk_in"))
        n_loads = len(names) + 3 + (2 if layer else 0)
        r, kx, vx, lowrank = rkv[:, 0:2, :], rkv[:, 2:4, :], rkv[:, 4:6, :], rkv[:, 6, :]
        chunks = lambda ap: ap.rearrange("p b (c n) -> p (b c) n", n=CH)
        with nc.Block() as block:
            @block.sync
            def _(sp):
                with nc.allow_non_contiguous_dma("columns"):
                    for n, name in enumerate(names):
                        sp.dma_start(cols[:, n, :], col(w[name])).then_inc(loaded, 16)
                sp.dma_start(wl[0:32, :], w["w2"]).then_inc(loaded, 16)
                sp.dma_start(wl[32:64, :], w["a2"]).then_inc(loaded, 16)
                sp.dma_start(wl[64:128, :], w["g2"]).then_inc(loaded, 16)
                if layer:
                    sp.dma_start(v1[:], w["v1"].rearrange("(k p) n -> p k n", p=P)).then_inc(loaded, 16)
                    sp.dma_start(v2[:], w["v2"]).then_inc(loaded, 16)

            @block.tensor
            def _(pe):
                pe.wait_ge(loaded, 16 * n_loads)
                pe.wait_ge(low_ready, 1)
                for b in range(2):
                    pe.matmul(bk[b][:], wl[0:32, b * P:(b + 1) * P], rkv[0:32, 6, :], start=True, stop=True)
                    ins = pe.matmul(bk[2 + b][:], wl[32:64, b * P:(b + 1) * P], rkv[32:64, 6, :], start=True, stop=True)
                ins.then_inc(wa_ready, 1)
                for t in range(NT):
                    ins = pe.matmul(bk[4 + t // 2][:, (t % 2) * RW:(t % 2) * RW + RW], rkv[64:128, 6, t * P:(t + 1) * P], wl[64:128, :], start=True, stop=True)
                ins.then_inc(wa_ready, 1)
                if layer:
                    for b in range(2):
                        ins = pe.matmul(bk[6][0:32, :], v1[:, b, :], rkv[:, 4 + b, :], start=(b == 0), stop=(b == 1))
                    ins.then_inc(v1_ready, 1)
                    pe.wait_ge(low_v_ready, 1)
                    pe.wait_ge(sig_ready, 1)
                    for b in range(2):
                        ins = pe.matmul(bk[b][:], v2[:, b * P:(b + 1) * P], low[:], start=True, stop=True)
                    ins.then_inc(v2_ready, 1)
                pe.wait_ge(sq_ready, 1)
                pe.wait_ge(sig_ready, 1)
                for b in range(2):
                    ins = pe.matmul(bk[2 + b][:], k.c("same_head"), t1[:, b, :], start=True, stop=True)
                ins.then_inc(norm_ready, 1)
                pe.wait_ge(v_done, 1)
                pe.wait_ge(tok_in, 1)
                for t in range(NT):
                    for b in range(2):
                        ins = pe.transpose(bk[4 + t // 2][:, (t % 2) * RW + b * P:(t % 2) * RW + (b + 1) * P], rkv[:, 4 + b, t * P:(t + 1) * P], k.c("ident"))
                ins.then_inc(tok_ready, 1)
                pe.wait_ge(rk_in, 1)
                for t in range(NT):
                    for b in range(2):
                        ins = pe.matmul(bk[7][:, t * 4 + 2 * b:t * 4 + 2 * b + 2], t1[:, b, t * P:(t + 1) * P], k.c("same_head")[:, 0:P:64], start=True, stop=True)
                ins.then_inc(tok_ready, 1)

            @block.scalar
            def _(a):
                a.activation(rkv[0:32, 6, :], rkv[0:32, 6, :], ACT.Tanh)
                a.activation(rkv[64:128, 6, :], rkv[64:128, 6, :], ACT.Sigmoid)
                a.drain().then_inc(low_ready, 1)
                a.wait_ge(loaded, 16 * n_loads)
                a.wait_ge(wa_ready, 1)
                for b in range(2):
                    a.activation(sgw[:, b, :], bk[b][:], ACT.Sigmoid, bias=cols[:, 0, b:b + 1])
                    a.activation(av[:, b, :], bk[2 + b][:], ACT.Sigmoid, bias=cols[:, 1, b:b + 1])
                a.drain().then_inc(sig_ready, 1)
                if layer:
                    a.wait_ge(v1_ready, 1)
                    a.activation(low[:], bk[6][0:32, :], ACT.Copy).then_inc(low_v_ready, 1)
                    a.wait_ge(v2_ready, 1)
                    for b in range(2):
                        ins = a.activation(e1[:, b, :], bk[b][:], ACT.Sigmoid, bias=cols[:, 5, b:b + 1])
                    a.drain().then_inc(vsig_ready, 1)
                a.wait_ge(root_in, 1)
                a.activation(kk[:], kk[:], ACT.Sqrt).then_inc(root_ready, 1)
                for n in range(4):
                    a.wait_ge(cum_ready, n + 1)
                    if n:
                        a.wait_ge(exp_used, n)
                    a.activation(e1[:], t1[:] if n >= 2 else cum[:], ACT.Exp, scale=-1.0 if n == 1 else 1.0).then_inc(exp_ready, 1)

            @block.vector
            def _(v):
                def do(f, *args, **kw):
                    ins = f(*args, **kw)
                    v.drain()
                    return ins

                c = lambda n, b: cols[:, n, b:b + 1]
                v.wait_ge(loaded, 16 * n_loads)
                for b in range(2):
                    v.tensor_scalar(kk[:, b, :], rkv[:, 2 + b, :], c(2, b), None, ALU.mult)
                v.drain()
                do(v.tensor_tensor, t1[:], kk[:], kk[:], ALU.mult).then_inc(sq_ready, 1)
                v.wait_ge(wa_ready, 2)
                for h in range(2):
                    v.tensor_copy(gt[:, 2 * h:2 * h + 2, :].rearrange("p t n -> p (t n)"), bk[4 + h][:])
                v.drain().then_inc(tok_in, 1)
                v.wait_ge(sig_ready, 1)
                do(v.tensor_scalar, sgw[:], sgw[:], -float(np.exp(-0.5)), None, ALU.mult)
                for b in range(2):
                    v.tensor_tensor_scan(cum[:, b, :], k.c("rw_keep"), sgw[:, b, :], 0.0, ALU.mult, ALU.add)
                v.drain()
                if layer:
                    v.wait_ge(vsig_ready, 1)
                    v.wait_ge(norm_ready, 1)
                    do(v.tensor_tensor, t1[:], v_first[:], vx, ALU.subtract)
                    do(v.tensor_tensor, t1[:], t1[:], e1[:], ALU.mult)
                    do(v.tensor_tensor, vx, vx, t1[:], ALU.add)
                else:
                    do(v.tensor_copy, v_first[:], vx)
                v.drain().then_inc(v_done, 1)
                v.drain().then_inc(cum_ready, 1)
                v.wait_ge(norm_ready, 1)
                for b in range(2):
                    v.tensor_copy(t1[:, b, :], kk[:, b, :])
                    v.drain()
                    v.tensor_scalar(kk[:, b, :], bk[2 + b][:], 1e-24, None, ALU.max)
                v.drain().then_inc(root_in, 1)
                v.wait_ge(root_ready, 1)
                do(v.reciprocal, kk[:], kk[:])
                do(v.tensor_tensor, kk[:], kk[:], t1[:], ALU.mult)
                for b in range(2):
                    v.tensor_scalar(t1[:, b, :], av[:, b, :], -1.0, c(3, b), ALU.add, ALU.mult)
                v.drain()
                do(v.scalar_tensor_tensor, kx, t1[:], 1.0, kx, ALU.add, ALU.mult)
                do(v.tensor_tensor, av[:], kk[:], av[:], ALU.mult)
                v.wait_ge(exp_ready, 1)
                v.tensor_tensor(R_[:], r, e1[:], ALU.mult)
                v.tensor_copy(pc[:], chunks(e1[:])[:, :, CH - 1])
                v.drain().then_inc(exp_used, 1)
                v.drain().then_inc(cum_ready, 1)
                v.wait_ge(exp_ready, 2)
                v.tensor_tensor(B_[:], av[:], e1[:], ALU.mult)
                v.tensor_tensor(K_[:], kx, e1[:], ALU.mult)
                do(v.tensor_tensor, t1[:], cum[:], sgw[:], ALU.subtract)
                v.drain().then_inc(exp_used, 1)
                v.drain().then_inc(cum_ready, 1)
                v.wait_ge(exp_ready, 3)
                v.tensor_tensor(A_[:], kk[:], e1[:], ALU.mult)
                v.drain().then_inc(exp_used, 1)
                do(v.tensor_tensor, chunks(t1[:]), chunks(cum[:])[:, :, CH - 1:CH].broadcast_to([P, 16, CH]), chunks(cum[:]), ALU.subtract)
                v.drain().then_inc(cum_ready, 1)
                v.wait_ge(exp_ready, 4)
                v.tensor_tensor(Be[:], av[:], e1[:], ALU.mult)
                v.tensor_tensor(Ke[:], kx, e1[:], ALU.mult)
                v.wait_ge(tok_ready, 1)
                for h in range(2):
                    v.tensor_copy(vt[:, 2 * h:2 * h + 2, :].rearrange("p t n -> p (t n)"), bk[4 + h][:])
                do(v.tensor_tensor, t1[:], r, kx, ALU.mult)
                for b in range(2):
                    v.tensor_scalar(t1[:, b, :], t1[:, b, :], c(4, b), None, ALU.mult)
                v.drain().then_inc(rk_in, 1)
                v.wait_ge(tok_ready, 2)
                v.tensor_copy(bonus[:], bk[7][:, 0:16])


@stage
def stage_rwkv_chunks(k, l, out, eb, vt, y, spent):
    nc = k.nc
    A_, R_, B_, K_ = out
    Be, Ke, pc = eb
    HH = 4
    W4 = HH * P
    with ExitStack() as ctx:
        grid = lambda n, w=P: k.sb(f"rc{l}_" + n, [P, NT, HH, w], F32, ctx)
        LT, MT = grid("LT"), grid("MT")
        Ti, TT, RB, RK = (grid(n) for n in ("Ti", "TT", "RB", "RK"))
        tok = k.sb(f"rc{l}_tok", [P, NT, 3, RW], F32, ctx)
        AM, TW = grid("AM"), grid("TW")
        Lm = [k.sb(f"rc{l}_Lm{i}", [P, W4], F32, ctx) for i in range(2)]
        X = [k.sb(f"rc{l}_X{i}", [P, W4], F32, ctx) for i in range(2)]
        G = spent[:, 0:2, :]
        H, Z = (spent[:, 2 * n:2 * n + 2, :].rearrange("p b (c n) -> p b c n", c=8) for n in (1, 2))
        S = k.sb(f"rc{l}_S", [P, 8, 2, CH], F32, ctx)
        bk = k.banks(ctx, 8, f"rc{l}_bk")
        lane = lambda h: slice(64 * (h % 2), 64 * (h % 2) + 64)
        pair = lambda p: (2 * (p % 3), 2 * (p % 3) + 1)
        s_ = {n: k.sem(f"rc{l}_" + n) for n in ("prod", "masked", "turned", "tok_taken", "lm", "x_mm", "x_sb", "y_mm", "t_new", "mv", "am", "tw_mm", "tw",
                                               "gh_mm", "gh", "s_mm", "s_new", "yo_mm", "yo_taken", "zero")}
        with nc.Block() as block:
            @block.tensor
            def _(pe):
                pe.sem_inc(s_["y_mm"], 2)
                for t in range(NT):
                    sl = slice(t * P, (t + 1) * P)
                    for n, (lhs, rhs) in enumerate(((B_, A_), (A_, B_), (K_, A_), (B_, R_), (K_, R_))):
                        if 5 * t + n >= 3:
                            pe.wait_ge(s_["masked"], 5 * t + n - 2)
                        for h in range(HH):
                            o = bk[pair(5 * t + n)[h % 2]][:, (h // 2) * P:(h // 2 + 1) * P]
                            ins = pe.matmul(o, lhs[lane(h), h // 2, sl], rhs[lane(h), h // 2, sl], start=True, stop=True)
                        pe.drain().then_inc(s_["prod"], 1)
                    if t:
                        pe.wait_ge(s_["tok_taken"], 2 * t)
                    for n, src in enumerate((A_, Be, Ke)):
                        for b in range(2):
                            o = n * RW + b * P
                            ins = pe.transpose(bk[6 + o // 512][:, o % 512:o % 512 + P], src[:, b, sl], k.c("ident"))
                    ins.then_inc(s_["turned"], 1)
                pe.wait_ge(s_["masked"], 5 * NT)
                with pe.Fori(0, 5) as lv:
                    def second(t):
                        u = lv * 4 + t
                        pe.wait_ge(s_["x_sb"], u + 1)
                        pe.wait_ge(s_["t_new"], u + 1)
                        for h in range(HH):
                            hs = slice(h * P, (h + 1) * P)
                            pe.matmul(bk[2 + t % 2][:, hs], TT[:, t, h, :], X[t % 2][:, hs], start=True, stop=True)
                            ins = pe.matmul(bk[4 + t % 2][:, hs], X[t % 2][:, hs], TT[:, t, h, :], start=True, stop=True)
                        ins.then_inc(s_["y_mm"], 1)

                    for t in range(NT):
                        u = lv * 4 + t
                        pe.wait_ge(s_["lm"], u + 1)
                        pe.wait_ge(s_["t_new"], lv * 4 + 2)
                        for h in range(HH):
                            hs = slice(h * P, (h + 1) * P)
                            ins = pe.matmul(bk[t % 2][:, hs], Lm[t % 2][:, hs], Ti[:, t, h, :], start=True, stop=True)
                        ins.then_inc(s_["x_mm"], 1)
                        if t:
                            second(t - 1)
                    second(NT - 1)
                pe.wait_ge(s_["t_new"], 2 + 5 * NT)
                for t in range(NT):
                    if t >= 2:
                        pe.wait_ge(s_["am"], t - 1)
                    for h in range(HH):
                        ins = pe.matmul(bk[t % 2][:, h * 64:h * 64 + 64], MT[:, t, h, :], vt[:, t, h * 64:h * 64 + 64], start=True, stop=True)
                    ins.then_inc(s_["mv"], 1)
                for t in range(NT):
                    pe.wait_ge(s_["am"], t + 1)
                    if t >= 2:
                        pe.wait_ge(s_["tw"], t - 1)
                    for h in range(HH):
                        ins = pe.matmul(bk[2 + t % 2][:, h * P:(h + 1) * P], TT[:, t, h, :], AM[:, t, h, :], start=True, stop=True)
                    ins.then_inc(s_["tw_mm"], 1)
                for t in range(NT):
                    pe.wait_ge(s_["tw"], t + 1)
                    if t:
                        pe.wait_ge(s_["gh"], t)
                    for h in range(HH):
                        v_h = vt[:, t, h * 64:h * 64 + 64]
                        pe.matmul(bk[4][lane(h), (h // 2) * P:(h // 2 + 1) * P], TW[:, t, h, 0:64], RB[:, t, h, :], start=True, stop=True)
                        pe.matmul(bk[7][:, h * 64:h * 64 + 64], RK[:, t, h, :], v_h, start=True, stop=False)
                        pe.matmul(bk[7][:, h * 64:h * 64 + 64], RB[:, t, h, :], TW[:, t, h, 64:128], start=False, stop=True)
                    for h in range(HH):
                        for c in range(2):
                            rows = slice(64 * c, 64 * c + 64)
                            o = (h // 2) * 64
                            f = slice(h * 64, h * 64 + 64)
                            pe.matmul(bk[c][lane(h), o:o + 64], TW[rows, t, h, 0:64], tok[rows, t, 1, f], start=True, stop=True)
                            pe.matmul(bk[5 + c][lane(h), o:o + 64], tok[rows, t, 2, f], vt[rows, t, f], start=True, stop=False)
                            ins = pe.matmul(bk[5 + c][lane(h), o:o + 64], tok[rows, t, 1, f], TW[rows, t, h, 64:128], start=False, stop=True)
                    pe.drain().then_inc(s_["gh_mm"], 1)
                for c in range(7):
                    pe.wait_ge(s_["s_new"], c + 1)
                    for h in range(HH):
                        ins = pe.matmul(bk[c % 2][lane(h), (h // 2) * 64:(h // 2) * 64 + 64], H[lane(h), h // 2, c, :], S[lane(h), c, h // 2, :], start=True, stop=True)
                    pe.drain().then_inc(s_["s_mm"], 1)
                pe.wait_ge(s_["s_new"], 8)
                for t in range(NT):
                    if t >= 2:
                        pe.wait_ge(s_["yo_taken"], t - 1)
                    for h in range(HH):
                        for c in range(2):
                            ins = pe.matmul(bk[2 + 2 * (t % 2) + h % 2][64 * c:64 * c + 64, (h // 2) * 64:(h // 2) * 64 + 64], G[lane(h), h // 2, t * P + 64 * c:t * P + 64 * c + 64],
                                            S[lane(h), 2 * t + c, h // 2, :], start=True, stop=True)
                    pe.drain().then_inc(s_["yo_mm"], 1)

            @block.scalar
            def _(a):
                for t in range(NT):
                    a.wait_ge(s_["turned"], t + 1)
                    flat = tok[:, t].rearrange("p n f -> p (n f)")
                    a.activation(flat[:, 0:512], bk[6][:], ACT.Copy).then_inc(s_["tok_taken"], 1)
                    a.activation(flat[:, 512:768], bk[7][:, 0:RW], ACT.Copy).then_inc(s_["tok_taken"], 1)
                with a.Fori(0, 5) as lv:
                    for t in range(NT):
                        a.wait_ge(s_["x_mm"], lv * 4 + t + 1)
                        a.wait_ge(s_["y_mm"], lv * 4 + t + 1)
                        a.activation(X[t % 2][:], bk[t % 2][:], ACT.Copy).then_inc(s_["x_sb"], 1)
                for t in range(NT):
                    a.activation(AM[:, t, :, 0:64], tok[:, t, 0, :].rearrange("p (h n) -> p h n", h=HH), ACT.Copy)
                    a.wait_ge(s_["mv"], t + 1)
                    a.activation(AM[:, t, :, 64:128], bk[t % 2][:, 0:RW].rearrange("p (h n) -> p h n", h=HH), ACT.Copy)
                    a.drain().then_inc(s_["am"], 1)

            @block.vector
            def _(v):
                over = lambda name: k.c(name).rearrange("p (a n) -> p a n", a=1).broadcast_to([P, HH, P])
                v3 = lambda b: bk[b][:].rearrange("p (h n) -> p h n", h=HH)
                v.memset(S[:, 0], 0.0)
                v.drain()
                for t in range(NT):
                    for n, (dst, mask) in enumerate(((LT[:, t], "rw_before"), (Ti[:, t], "rw_level0_t"), (MT[:, t], "rw_before"), (RB[:, t], "rw_upto"), (RK[:, t], "rw_upto"))):
                        v.wait_ge(s_["prod"], 5 * t + n + 1)
                        for side in range(2):
                            ins = v.tensor_tensor(dst[:, side::2, :], bk[pair(5 * t + n)[side]][:, 0:2 * P].rearrange("p (h n) -> p h n", h=2),
                                                  over(mask)[:, 0:2, :], ALU.mult)
                        ins.then_inc(s_["masked"], 1)
                    v.drain()
                    v.tensor_tensor(Ti[:, t], over("ident"), Ti[:, t], ALU.subtract)
                    v.tensor_tensor(TT[:, t], LT[:, t], over("rw_level0"), ALU.mult)
                    v.drain()
                    v.tensor_tensor(TT[:, t], over("ident"), TT[:, t], ALU.subtract)
                v.drain()
                v.sem_inc(s_["t_new"], 2)
                at1 = WHERE["rw_level1"][0]
                with v.Fori(0, 5) as lv:
                    def mask(t):
                        v.wait_ge(s_["x_mm"], lv * 4 + max(t - 1, 0))
                        v.tensor_tensor(Lm[t % 2][:].rearrange("p (h n) -> p h n", h=HH), LT[:, t],
                                        k.consts[:, ds(lv * P + at1, P)].rearrange("p (a n) -> p a n", a=1).broadcast_to([P, HH, P]), ALU.mult).then_inc(s_["lm"], 1)

                    mask(0)
                    mask(1)
                    for t in range(NT):
                        if t + 2 < NT:
                            mask(t + 2)
                        v.wait_ge(s_["y_mm"], lv * 4 + t + 3)
                        v.tensor_tensor(Ti[:, t], Ti[:, t], v3(2 + t % 2), ALU.subtract)
                        v.tensor_tensor(TT[:, t], TT[:, t], v3(4 + t % 2), ALU.subtract)
                        v.drain().then_inc(s_["t_new"], 1)
                for t in range(NT):
                    v.wait_ge(s_["tw_mm"], t + 1)
                    v.tensor_copy(TW[:, t, :, 0:64], v3(2 + t % 2)[:, :, 0:64])
                    v.tensor_scalar(TW[:, t, :, 64:128], v3(2 + t % 2)[:, :, 64:128], -1.0, None, ALU.mult)
                    v.drain().then_inc(s_["tw"], 1)
                for t in range(NT):
                    v.wait_ge(s_["gh_mm"], t + 1)
                    sl = slice(t * P, (t + 1) * P)
                    v.tensor_tensor(G[:, :, sl], R_[:, :, sl], bk[4][:, 0:RW].rearrange("p (b n) -> p b n", b=2), ALU.subtract)
                    v.tensor_copy(y[:, t, :], bk[7][:, 0:RW])
                    half = lambda n: bk[n][:, 0:P].rearrange("p (b n) -> p b n", b=2)
                    for b in range(2):
                        for c in range(2):
                            for side in range(2):
                                r = slice(64 * side, 64 * side + 64)
                                v.scalar_tensor_tensor(H[r, b, 2 * t + c, :], k.c("ident")[r, r], pc[r, b * 8 + 2 * t + c:b * 8 + 2 * t + c + 1], half(c)[r, b, :], ALU.mult, ALU.subtract)
                    for c in range(2):
                        v.tensor_copy(Z[:, :, 2 * t + c, :], half(5 + c))
                    v.drain().then_inc(s_["gh"], 1)
                v.drain().then_inc(s_["s_new"], 1)
                for c in range(7):
                    v.wait_ge(s_["s_mm"], c + 1)
                    v.tensor_tensor(S[:, c + 1], bk[c % 2][:, 0:P].rearrange("p (b n) -> p b n", b=2), Z[:, :, c, :], ALU.add).then_inc(s_["s_new"], 1)
                for t in range(NT):
                    v.wait_ge(s_["yo_mm"], t + 1)
                    yh = y[:, t, :].rearrange("p (h n) -> p h n", h=HH)
                    for side in range(2):
                        ins = v.tensor_tensor(yh[:, side::2, :], yh[:, side::2, :], bk[2 + 2 * (t % 2) + side][:, 0:P].rearrange("p (h n) -> p h n", h=2), ALU.add)
                    ins.then_inc(s_["yo_taken"], 1)


@stage
def stage_rwkv_out(k, l, y, vt, gt, bonus, gn_w, gn_b, mix):
    nc = k.nc
    with ExitStack() as ctx:
        wb = k.sb(f"ro_{l}wb", [P, 2, RW], F32, ctx)
        sq = k.sb(f"ro_{l}sq", [P, NT, RW], F32, ctx)
        mean, var = k.sb(f"ro_{l}mean", [P, 16], F32, ctx), k.sb(f"ro_{l}var", [P, 16], F32, ctx)
        loaded, var_ready, root_ready = k.sem(f"ro_{l}loaded"), k.sem(f"ro_{l}var_ready"), k.sem(f"ro_{l}root")
        with nc.Block() as block:
            @block.sync
            def _(sp):
                sp.dma_start(wb[:, 0, :], row_bc(gn_w)).then_inc(loaded, 16)
                sp.dma_start(wb[:, 1, :], row_bc(gn_b)).then_inc(loaded, 16)

            @block.scalar
            def _(a):
                a.wait_ge(var_ready, 1)
                a.activation(var[:], var[:], ACT.Sqrt).then_inc(root_ready, 1)

            @block.vector
            def _(v):
                def do(f, *args, **kw):
                    ins = f(*args, **kw)
                    v.drain()
                    return ins

                hv = lambda t: t[:].rearrange("p t (h n) -> p (t h) n", n=64)
                bc = lambda t: t[:].rearrange("p (g a) -> p g a", a=1).broadcast_to([P, 16, 64])
                do(v.tensor_reduce, mean[:], hv(y), AX, ALU.add)
                do(v.tensor_scalar, mean[:], mean[:], 1.0 / 64, None, ALU.mult)
                do(v.tensor_tensor, hv(y), hv(y), bc(mean), ALU.subtract)
                do(v.tensor_tensor, sq[:], y[:], y[:], ALU.mult)
                do(v.tensor_reduce, var[:], hv(sq), AX, ALU.add)
                do(v.tensor_scalar, var[:], var[:], 1.0 / 64, 64e-5, ALU.mult, ALU.add).then_inc(var_ready, 1)
                do(v.tensor_tensor, hv(sq), hv(vt), bc(bonus), ALU.mult)
                v.wait_ge(root_ready, 1)
                do(v.reciprocal, var[:], var[:])
                do(v.tensor_tensor, hv(y), hv(y), bc(var), ALU.mult)
                v.wait_ge(loaded, 32)
                for n, op in ((0, ALU.mult), (1, ALU.add)):
                    do(v.tensor_tensor, y[:], y[:], wb[:, n:n + 1, :].broadcast_to([P, NT, RW]), op)
                do(v.tensor_tensor, y[:], y[:], sq[:], ALU.add)
                v.tensor_tensor(mix[:, :, 0:RW], y[:], gt[:], ALU.mult)


def second_layer(k, l, ap, cos32, sin32, v_first):
    g = lambda n: ap[n + "_2"][l]
    with ExitStack() as c0:
        mix = k.sb(f"mix{l}", [P, NT, D], F32, c0)
        rkv = k.sb(f"rkv{l}", [P, 7, T], F32, c0)
        with ExitStack() as c1:
            sb = lambda n, s: k.sb(f"{n}{l}", s, F32, c1)
            rqk, krT, vg, lat, ssl, latT = (sb("rqk", [P, 4, T]), sb("krT", [P, T]), sb("vg", [P, NT, 2 * RW]), sb("lat", [P, NT, MQ + MKV]),
                                            sb("ssl", [P, NT, 2]), sb("latT", [P, 5, T]))
            with ExitStack() as c2:
                k.make_room_for_h(f"a{l}", c2)
                stage_norm(k, f"na{l}", g("attn_norm"))
                stage_features(k, l, g("w_in"), g("rw_mu"), rkv, rqk, krT, cos32, sin32)
                stage_tokens(k, l, g("w_in"), vg, lat, ssl)
            stage_latents(k, l, lat, ssl, g("mla_q_norm"), g("mla_kv_norm"), latT)
            stage_retention(k, l, rqk, vg, mix)
            QT, KT, v_tok = sb("QT", [P, MH, T]), sb("KT", [P, MH, T]), sb("mv_tok", [P, NT, 512])
            stage_mla_up(k, l, latT, krT, g("mla_w_q_up"), g("mla_w_kv_up"), cos32, sin32, QT, KT, v_tok)
            stage_mla_attention(k, l, QT, KT, v_tok, mix)
        with ExitStack() as c1:
            sb = lambda n, s: k.sb(f"rw_{n}{l}", s, F32, c1)
            out = tuple(sb(n, [P, 2, T]) for n in "ARBK")
            eb = (sb("Be", [P, 2, T]), sb("Ke", [P, 2, T]), sb("pc", [P, 16]))
            vt, gt, bonus, y = sb("vt", [P, NT, RW]), sb("gt", [P, NT, RW]), sb("bonus", [P, 16]), sb("y", [P, NT, RW])
            w = {n: g("rw_" + n) for n in ("w0", "w2", "a0", "a2", "g2", "k_k", "k_a")}
            w["r_k"] = g("rw_r_k").rearrange("h n -> (h n)")
            if l:
                w.update({n: ap[f"rw_{n}_2"][l - 1] for n in ("v0", "v1", "v2")})
            stage_rwkv_prep(k, rkv, w, v_first, out, eb, vt, gt, bonus, l)
            stage_rwkv_chunks(k, l, out, eb, vt, y, rkv)
            stage_rwkv_out(k, l, y, vt, gt, bonus, g("rw_gn_w"), g("rw_gn_b"), mix)
        mixT = k.pair(f"mixT{l}", KD, c0)
        stage_turn_back(k, l, mix, mixT)
        stage_residual(k, f"ro{l}", g("w_out"), mixT)
    with ExitStack() as c0:
        fT = k.pair(f"fT{l}", DFF // P, c0)
        with ExitStack() as c1:
            k.make_room_for_h(f"f{l}", c1)
            stage_norm(k, f"nf{l}", g("ffn_norm"))
            gu = g("w_gate_up")
            stage_gated(k, f"ff{l}", ACT.Silu, gu, 0, gu, DFF, (k.h_hi, k.h_lo), DFF // P, "split", fT)
        stage_residual(k, f"fd{l}", g("w_down"), fT, DFF // P)


@stage
def stage_turn_back(k, l, src, dst):
    nc = k.nc
    with ExitStack() as ctx:
        tp = k.banks(ctx, KD, f"tb{l}_tp")
        turned = k.sem(f"tb{l}_turned")
        with nc.Block() as block:
            @block.tensor
            def _(pe):
                for n in range(KD):
                    for t in range(NT):
                        ins = pe.transpose(tp[n][:, t * P:(t + 1) * P], src[:, t, n * P:(n + 1) * P], k.c("ident"))
                    ins.then_inc(turned, 1)

            @block.vector
            def _(v):
                for n in range(KD):
                    v.wait_ge(turned, n + 1)
                    split(v, dst[0][:, n, :], dst[1][:, n, :], tp[n][:])


def first_block(k, ap):
    nc = k.nc
    w_in = ap["w_in"][0]
    stage_rope_tables(k, "r1", ap["positions"], "freq64", k.cos, k.sin)
    with ExitStack() as mix_ctx:
        k.make_room_for_h("x", mix_ctx)
        stage_norm(k, "n1", ap["norm_mix_w"][0])
        merged = k.x[:].rearrange("p t (a n) -> p (t a) n", n=T)
        with ExitStack() as ctx:
            attT = k.pair("attT", KD, ctx)
            with ExitStack() as att_ctx:
                qkT, lam = k.sb("qkT", [P, 16, T], F32, att_ctx), k.sb("lam", [P, 1], F32, att_ctx)
                stage_qk(k, "qk", w_in, qkT)
                v_tok, att_ss = k.sb("v_tok", [P, NT, D], F32, att_ctx), k.sb("att_ss", [P, NT, 8], F32, att_ctx)
                stage_token_major(k, "v", w_in, 2048, 2, lambda a, ps, s, t: a.activation(v_tok[:, t, ds(s * 512, 512)], ps[:], ACT.Copy))
                stage_lambda(k, [ap[n] for n in ("lambda_q1", "lambda_k1", "lambda_q2", "lambda_k2")], lam, LAM_INIT)
                stage_diff_attention(k, qkT, v_tok, k.x, att_ss, lam)
                stage_scale_and_turn(k, "an", k.x, att_ss, 8, 128, 1e-5, ap["subln_w"][0], attT, gain=1.0 - LAM_INIT)
            stage_gated(k, "ma", ACT.Sigmoid, w_in, GA0, ap["w_branch_attn"][0], 0, attT, KD, "set", merged)
        with ExitStack() as ctx:
            xs, ssd_ss = k.sb("xs", [P, NT, 2048], F32, ctx), k.sb("ssd_ss", [P, NT, 8], F32, ctx)
            with ExitStack() as scan_ctx:
                xbcT = k.sb("xbcT", [P, 32, T], F32, scan_ctx)
                zs = xbcT[:, 0:16, :].rearrange("p (t a) n -> p t (a n)", t=NT)
                stage_conv(k, w_in, ap["conv_w"][0], ap["conv_b"][0], xbcT)
                stage_turn(k, "tx", xbcT, 16, xs)
                stage_token_major(k, "z", w_in, Z0, 4, lambda a, ps, s, t: a.activation(zs[:, t, ds(s * 512, 512)], ps[:], ACT.Silu), n_raw=1)
                steps = [k.sb("sd_" + n, [P, NT, 32], F32, scan_ctx) for n in ("dt", "cum", "ecum", "wtail", "etot", "adt")]
                stage_ssd_steps(k, w_in, ap["dt_bias"][0], ap["a_log"][0], *steps)
                btok = k.sb("btok", [P, NT, 1024], F32, scan_ctx)
                stage_turn(k, "tb", xbcT[:, 16:24, :], 8, btok)
                stage_ssd(k, xbcT, xs, btok, zs, *steps, ap["d_skip"][0], ssd_ss)
            yT = k.pair("yT", 16, ctx)
            stage_scale_and_turn(k, "sn", xs, ssd_ss, 8, 256, 1e-5, ap["ssd_norm_w"][0], yT)
            stage_gated(k, "ms", ACT.Sigmoid, w_in, GA0 + D, ap["w_branch_ssd"][0], 0, yT, KD, "add", merged)
        mergedT = k.pair("mergedT", KD, mix_ctx)
        stage_residual(k, "wo", ap["w_out"][0], mergedT, src=merged, reload=ap["x"][0])
    h2_rows = nc.dram_tensor("h2_rows", (T, D), F32, kind="Internal").ap()
    y_rows = nc.dram_tensor("y_rows", (NA, D), F32, kind="Internal").ap()
    slot_list = nc.dram_tensor("slot_list", (SLOTS, 1), I32, kind="Internal").ap()
    with ExitStack() as moe_ctx:
        gidx, sidx = (k.sb(n, [P, E + XB + 1], U32, moe_ctx) for n in ("gidx", "sidx"))
        xexp, weights = k.sb("xexp", [1, 8], I32, moe_ctx), k.sb("moe_w", [P, 2, NT], F32, moe_ctx)
        with ExitStack() as ctx:
            h2 = k.sb("h2", [P, NT, D], F32, ctx)
            k.make_room_for_h("moe", ctx)
            stage_norm(k, "n2", ap["norm_ffn_w"][0], keep=h2)
            stage_route(k, ap["w_group_router"][0], ap["b_group_router"][0], ap["w_expert_router"][0], ap["b_expert_router"][0],
                        h2, h2_rows, slot_list, gidx, sidx, xexp, weights)
        stage_experts(k, ap["w_expert_gate"][0], ap["w_expert_up"][0], ap["w_expert_down"][0], h2_rows, y_rows, gidx, sidx, xexp)
        stage_combine(k, y_rows, weights)
    stage_norm(k, "nb", ap["final_norm_w"], keep=k.x, transposed=False)


def second_block(k, ap):
    with ExitStack() as ctx:
        cos32, sin32 = k.sb("cos32", [P, T], F32, ctx), k.sb("sin32", [P, T], F32, ctx)
        v_first = k.sb("v_first", [P, 2, T], F32, ctx)
        stage_rope_tables(k, "r2", ap["positions_2"], "freq64", k.cos, k.sin)
        stage_rope_tables(k, "r3", ap["positions_2"], "freq32", cos32, sin32)
        for l in range(2):
            second_layer(k, l, ap, cos32, sin32, v_first)
    stage_norm(k, "ne", ap["final_norm_2"], keep=k.x, transposed=False)


@stage
def stage_store(k, out):
    nc = k.nc
    stored = k.sem("result_stored")
    with nc.Block() as block:
        @block.sync
        def _(sp):
            sp.dma_start(out[0].rearrange("(t p) d -> p t d", p=P), k.x[:]).then_inc(stored, 16)
            sp.wait_ge(stored, 16)


def build(nc, ap, consts, out):
    with ExitStack() as ctx:
        k = Core(nc, ctx, consts)
        stage_load(k, ap["x"])
        first_block(k, ap)
        second_block(k, ap)
        stage_store(k, out)


def kernel(**inputs):
    import numpy as _np
    import concourse.bacc as _bacc
    from concourse import mybir as _mybir
    from concourse.bass_utils import run_bass_kernel_spmd as _run

    nc = _bacc.Bacc("TRN2", target_bir_lowering=False, num_devices=1)
    arrays, ap = {}, {}
    for name, value in inputs.items():
        a = _np.ascontiguousarray(value)
        arrays[f"in_{name}_dram"] = a
        ap[name] = nc.dram_tensor(f"in_{name}_dram", a.shape, _mybir.dt.from_np(a.dtype), kind="ExternalInput").ap()
    arrays["in_shape_constants_dram"] = shape_constants()[0]
    consts = nc.dram_tensor("in_shape_constants_dram", (P, CONST_COLS), F32, kind="ExternalInput").ap()
    out = nc.dram_tensor("out_0_dram", (1, T, D), F32, kind="ExternalOutput").ap()
    build(nc, ap, consts, out)
    r = _run(nc, [arrays], core_ids=[0])
    return r.results[0]["out_0_dram"]
```
